# Optimizing a Trainium2 kernel written in Bass

```python
import math
import jax, jax.numpy as jnp
from jax import lax
import numpy as np

D_MODEL = 1024
BATCH = 1
SEQ = 256
DEPTH = 2

N_MIXERS = 4
PLE_DIM = 256
ALPHA = (2 * DEPTH) ** 0.25
BETA_INIT = (8 * DEPTH) ** -0.25
LN_EPS = 1e-5

GM_CHUNK = 128
GM_WIDTH = 2 * D_MODEL
GM_GROUPS = 8
FOX_HEADS = 16
FOX_HEAD_DIM = D_MODEL // FOX_HEADS
FOX_BLOCK = 128
GDN_HEADS = 8
GDN_DK = 128
GDN_DV = 128
GDN_CONV = 4
GDN_CHUNK = 64
SSD_INNER = 2 * D_MODEL
SSD_HEAD_DIM = 64
SSD_HEADS = SSD_INNER // SSD_HEAD_DIM
SSD_GROUPS = 4
SSD_STATE = 128
SSD_CONV = 4
SSD_CHUNK = 64
D_FF = 3584
N_EXPERTS = 8
TOP_K = 2

N_LAYERS_PER_MIXER = tuple((DEPTH - m + N_MIXERS - 1) // N_MIXERS for m in range(N_MIXERS))
N_DENSE = (DEPTH + 1) // 2
N_MOE = DEPTH // 2

kernel_name = "hybrid_interleaved_gmlp_fox_gdn_ssd_moe"

def layer_norm(x, g, b):
    xf = x.astype(jnp.float32)
    mu = jnp.mean(xf, axis=-1, keepdims=True)
    var = jnp.mean(jnp.square(xf - mu), axis=-1, keepdims=True)
    return ((xf - mu) * lax.rsqrt(var + LN_EPS) * g.astype(jnp.float32) + b.astype(jnp.float32)).astype(x.dtype)

def rms_norm(x, g, eps=1e-6):
    xf = x.astype(jnp.float32)
    return (xf * lax.rsqrt(jnp.mean(xf * xf, axis=-1, keepdims=True) + eps) * g.astype(jnp.float32)).astype(x.dtype)

def l2_norm(x, eps=1e-6):
    return x * lax.rsqrt(jnp.sum(x * x, axis=-1, keepdims=True) + eps)

def causal_dwconv(x, w):
    k, c = w.shape
    return lax.conv_general_dilated(x, w[:, None, :].astype(x.dtype), window_strides=(1,), padding=[(k - 1, 0)],
                                    dimension_numbers=("NWC", "WIO", "NWC"), feature_group_count=c)

def gmlp_mixer(x, w_in, b_in, ln_g, ln_b, w_s, b_s, w_out):
    bsz, s, _ = x.shape
    z = jax.nn.gelu(x @ w_in + b_in)
    u, v = jnp.split(z, 2, axis=-1)
    v = layer_norm(v, ln_g, ln_b)
    v = v.reshape(bsz, s // GM_CHUNK, GM_CHUNK, GM_GROUPS, GM_WIDTH // GM_GROUPS)
    mask = jnp.tril(jnp.ones((GM_CHUNK, GM_CHUNK), dtype=bool))
    ws = jnp.where(mask, w_s, jnp.zeros_like(w_s))
    sv = jnp.einsum("gts,bnsgc->bntgc", ws, v) + b_s.T[None, None, :, :, None]
    return (u * sv.reshape(bsz, s, GM_WIDTH)) @ w_out

def fox_mixer(x, w_in, b_f, w_out):
    bsz, s, _ = x.shape
    h, dh = FOX_HEADS, FOX_HEAD_DIM
    width = h * dh
    q, k, v, f = jnp.split(x @ w_in, [width, 2 * width, 3 * width], axis=-1)
    q = q.reshape(bsz, s, h, dh).transpose(0, 2, 1, 3) * (dh ** -0.5)
    k = k.reshape(bsz, s, h, dh).transpose(0, 2, 1, 3)
    v = v.reshape(bsz, s, h, dh).transpose(0, 2, 1, 3)
    log_f = jax.nn.log_sigmoid((f + b_f).astype(jnp.float32))
    c = jnp.cumsum(log_f, axis=1).transpose(0, 2, 1)
    outs = []
    for blk in range(s // FOX_BLOCK):
        q0, q1 = blk * FOX_BLOCK, (blk + 1) * FOX_BLOCK
        logits = jnp.einsum("bhtd,bhsd->bhts", q[:, :, q0:q1], k[:, :, :q1]).astype(jnp.float32)
        logits = logits + c[:, :, q0:q1, None] - c[:, :, None, :q1]
        mask = (q0 + jnp.arange(FOX_BLOCK))[:, None] >= jnp.arange(q1)[None, :]
        logits = jnp.where(mask, logits, -jnp.inf)
        probs = jax.nn.softmax(logits, axis=-1).astype(v.dtype)
        outs.append(jnp.einsum("bhts,bhsd->bhtd", probs, v[:, :, :q1]))
    o = jnp.concatenate(outs, axis=2).transpose(0, 2, 1, 3).reshape(bsz, s, width)
    return o @ w_out

def gated_delta_chunked(q, k, v, beta, g):
    bsz, s, h, dk = q.shape
    dv = v.shape[-1]
    c = GDN_CHUNK
    n = s // c
    to_chunks = lambda t: t.reshape(bsz, n, c, h, -1).transpose(0, 3, 1, 2, 4)
    q, k, v = to_chunks(q), to_chunks(k), to_chunks(v)
    beta = beta.reshape(bsz, n, c, h).transpose(0, 3, 1, 2)
    gc = jnp.cumsum(g.reshape(bsz, n, c, h).transpose(0, 3, 1, 2), axis=-1)
    causal = jnp.tril(jnp.ones((c, c), dtype=bool))
    strict = jnp.tril(jnp.ones((c, c), dtype=bool), -1)
    decay = jnp.exp(jnp.where(causal, gc[..., :, None] - gc[..., None, :], -jnp.inf))
    kb = k * beta[..., None]
    m = jnp.where(strict, jnp.einsum("bhnid,bhnjd->bhnij", kb, k) * decay, 0.0)
    a = m + jnp.eye(c, dtype=m.dtype)
    u = lax.linalg.triangular_solve(a, v * beta[..., None], left_side=True, lower=True, unit_diagonal=True)
    w = lax.linalg.triangular_solve(a, kb * jnp.exp(gc)[..., None], left_side=True, lower=True, unit_diagonal=True)
    aqk = jnp.einsum("bhnid,bhnjd->bhnij", q, k) * decay

    def step(state, inp):
        qc, kc, uc, wc, ac, gcc = inp
        v_new = uc - jnp.einsum("bhcd,bhde->bhce", wc, state)
        o = jnp.einsum("bhcd,bhde->bhce", qc * jnp.exp(gcc)[..., None], state) + jnp.einsum("bhij,bhje->bhie", ac, v_new)
        g_last = gcc[..., -1]
        state = state * jnp.exp(g_last)[..., None, None] + jnp.einsum(
            "bhcd,bhce->bhde", kc * jnp.exp(g_last[..., None] - gcc)[..., None], v_new)
        return state, o

    xs = tuple(jnp.moveaxis(t, 2, 0) for t in (q, k, u, w, aqk, gc))
    state0 = jnp.zeros((bsz, h, dk, dv), jnp.float32)
    _, o = lax.scan(step, state0, xs)
    return o.transpose(1, 0, 3, 2, 4).reshape(bsz, s, h, dv)

def gdn_mixer(x, w_in, conv_w, a_log, dt_bias, norm_g, w_out):
    bsz, s, _ = x.shape
    h, dk, dv = GDN_HEADS, GDN_DK, GDN_DV
    qk_w, v_w = h * dk, h * dv
    qkv, gate, b_logit, a_logit = jnp.split(x @ w_in, [2 * qk_w + v_w, 2 * qk_w + 2 * v_w, 2 * qk_w + 2 * v_w + h], axis=-1)
    qkv = jax.nn.silu(causal_dwconv(qkv, conv_w)).astype(jnp.float32)
    q, k, v = jnp.split(qkv, [qk_w, 2 * qk_w], axis=-1)
    q = l2_norm(q.reshape(bsz, s, h, dk)) * (dk ** -0.5)
    k = l2_norm(k.reshape(bsz, s, h, dk))
    v = v.reshape(bsz, s, h, dv)
    beta = jax.nn.sigmoid(b_logit.astype(jnp.float32))
    g = -jnp.exp(a_log.astype(jnp.float32)) * jax.nn.softplus((a_logit + dt_bias).astype(jnp.float32))
    o = gated_delta_chunked(q, k, v, beta, g).astype(x.dtype)
    o = rms_norm(o, norm_g) * jax.nn.silu(gate.reshape(bsz, s, h, dv))
    return o.reshape(bsz, s, v_w) @ w_out

def ssd_chunked(xdt, a, bm, cm):
    bsz, s, h, p = xdt.shape
    g, n_state = bm.shape[2], bm.shape[3]
    j = h // g
    c = SSD_CHUNK
    n = s // c
    xs = (jnp.moveaxis(xdt.reshape(bsz, n, c, g, j, p), 1, 0),
          jnp.moveaxis(a.reshape(bsz, n, c, g, j), 1, 0),
          jnp.moveaxis(bm.reshape(bsz, n, c, g, n_state), 1, 0),
          jnp.moveaxis(cm.reshape(bsz, n, c, g, n_state), 1, 0))
    causal = jnp.tril(jnp.ones((c, c), dtype=bool))

    def step(state, inp):
        xc, ac, bc, cc = inp
        acum = jnp.cumsum(ac, axis=1)
        acum_t = acum.transpose(0, 2, 3, 1)
        lmat = jnp.exp(jnp.where(causal, acum_t[..., :, None] - acum_t[..., None, :], -jnp.inf))
        cb = jnp.einsum("btgn,bsgn->bgts", cc, bc)
        y = jnp.einsum("bgts,bgjts,bsgjp->btgjp", cb, lmat, xc)
        y = y + jnp.einsum("btgn,bgjpn->btgjp", cc, state) * jnp.exp(acum)[..., None]
        last = acum_t[..., -1]
        state = state * jnp.exp(last)[..., None, None] + jnp.einsum(
            "bsgn,bgjs,bsgjp->bgjpn", bc, jnp.exp(last[..., None] - acum_t), xc)
        return state, y

    state0 = jnp.zeros((bsz, g, j, p, n_state), jnp.float32)
    _, ys = lax.scan(step, state0, xs)
    return jnp.moveaxis(ys, 0, 1).reshape(bsz, s, h, p)

def ssd_mixer(x, w_in, conv_w, conv_b, dt_bias, a_log, d_skip, norm_g, w_out):
    bsz, s, _ = x.shape
    h, p, g, n_state = SSD_HEADS, SSD_HEAD_DIM, SSD_GROUPS, SSD_STATE
    z, xbc, dt = jnp.split(x @ w_in, [SSD_INNER, 2 * SSD_INNER + 2 * g * n_state], axis=-1)
    xbc = jax.nn.silu(causal_dwconv(xbc, conv_w) + conv_b)
    xs, bm, cm = jnp.split(xbc.astype(jnp.float32), [SSD_INNER, SSD_INNER + g * n_state], axis=-1)
    xs = xs.reshape(bsz, s, h, p)
    bm = bm.reshape(bsz, s, g, n_state)
    cm = cm.reshape(bsz, s, g, n_state)
    dt = jax.nn.softplus((dt + dt_bias).astype(jnp.float32))
    a = dt * (-jnp.exp(a_log.astype(jnp.float32)))
    y = ssd_chunked(xs * dt[..., None], a, bm, cm) + xs * d_skip.astype(jnp.float32)[:, None]
    y = y.reshape(bsz, s, SSD_INNER).astype(x.dtype) * jax.nn.silu(z)
    y = rms_norm(y.reshape(bsz, s, g, SSD_INNER // g), norm_g.reshape(g, SSD_INNER // g)).reshape(bsz, s, SSD_INNER)
    return y @ w_out

def swiglu(x, w_gate, w_up, w_down):
    return (jax.nn.silu(x @ w_gate) * (x @ w_up)) @ w_down

def moe_swiglu(x, w_router, w_gate, w_up, w_down):
    logits = (x @ w_router).astype(jnp.float32)
    top_vals, top_idx = lax.top_k(logits, TOP_K)
    weights = jax.nn.softmax(top_vals, axis=-1)
    combine = jnp.sum(jax.nn.one_hot(top_idx, N_EXPERTS, dtype=jnp.float32) * weights[..., None], axis=-2).astype(x.dtype)
    out = jnp.zeros_like(x)
    for e in range(N_EXPERTS):
        out = out + combine[..., e:e + 1] * swiglu(x, w_gate[e], w_up[e], w_down[e])
    return out

def _normal(k, shape, fan_in, scale=1.0):
    return jax.random.normal(k, shape, jnp.float32) * (scale * fan_in ** -0.5)

def _dt_bias(k, shape):
    dt = jnp.exp(jax.random.uniform(k, shape, jnp.float32, math.log(1e-3), math.log(1e-1)))
    return dt + jnp.log(-jnp.expm1(-dt))

def _a_log(k, shape):
    return jnp.log(jax.random.uniform(k, shape, jnp.float32, 1.0, 16.0))

def setup_inputs(seed: int = 0) -> dict:
    key = jax.random.key(seed)
    ks = iter(jax.random.split(key, 48))
    nA, nB, nC, nD = N_LAYERS_PER_MIXER
    d = D_MODEL
    gdn_in = 2 * GDN_HEADS * GDN_DK + 2 * GDN_HEADS * GDN_DV + 2 * GDN_HEADS
    gdn_conv_ch = 2 * GDN_HEADS * GDN_DK + GDN_HEADS * GDN_DV
    ssd_conv_ch = SSD_INNER + 2 * SSD_GROUPS * SSD_STATE
    ssd_in = SSD_INNER + ssd_conv_ch + SSD_HEADS
    inp = {}
    inp["x"] = jax.random.normal(next(ks), (BATCH, SEQ, d), jnp.float32)
    inp["p"] = jax.random.normal(next(ks), (DEPTH, BATCH, SEQ, PLE_DIM), jnp.float32)
    inp["ln_g"] = 1.0 + 0.02 * jax.random.normal(next(ks), (DEPTH, 2, d), jnp.float32)
    inp["ln_b"] = 0.02 * jax.random.normal(next(ks), (DEPTH, 2, d), jnp.float32)
    inp["gm_w_in"] = _normal(next(ks), (nA, d, 2 * GM_WIDTH), d)
    inp["gm_b_in"] = 0.02 * jax.random.normal(next(ks), (nA, 2 * GM_WIDTH), jnp.float32)
    inp["gm_ln_g"] = 1.0 + 0.02 * jax.random.normal(next(ks), (nA, GM_WIDTH), jnp.float32)
    inp["gm_ln_b"] = 0.02 * jax.random.normal(next(ks), (nA, GM_WIDTH), jnp.float32)
    inp["gm_w_s"] = _normal(next(ks), (nA, GM_GROUPS, GM_CHUNK, GM_CHUNK), GM_CHUNK)
    inp["gm_b_s"] = 1.0 + 0.1 * jax.random.normal(next(ks), (nA, GM_GROUPS, GM_CHUNK), jnp.float32)
    inp["gm_w_out"] = _normal(next(ks), (nA, GM_WIDTH, d), GM_WIDTH, BETA_INIT)
    inp["fox_w_in"] = _normal(next(ks), (nB, d, 3 * d + FOX_HEADS), d)
    inp["fox_b_f"] = jax.random.uniform(next(ks), (nB, FOX_HEADS), jnp.float32, 1.0, 4.0)
    inp["fox_w_out"] = _normal(next(ks), (nB, d, d), d, BETA_INIT)
    inp["gdn_w_in"] = _normal(next(ks), (nC, d, gdn_in), d)
    inp["gdn_conv_w"] = _normal(next(ks), (nC, GDN_CONV, gdn_conv_ch), GDN_CONV)
    inp["gdn_a_log"] = _a_log(next(ks), (nC, GDN_HEADS))
    inp["gdn_dt_bias"] = _dt_bias(next(ks), (nC, GDN_HEADS))
    inp["gdn_norm_g"] = 1.0 + 0.02 * jax.random.normal(next(ks), (nC, GDN_DV), jnp.float32)
    inp["gdn_w_out"] = _normal(next(ks), (nC, GDN_HEADS * GDN_DV, d), GDN_HEADS * GDN_DV, BETA_INIT)
    inp["ssd_w_in"] = _normal(next(ks), (nD, d, ssd_in), d)
    inp["ssd_conv_w"] = _normal(next(ks), (nD, SSD_CONV, ssd_conv_ch), SSD_CONV)
    inp["ssd_conv_b"] = 0.02 * jax.random.normal(next(ks), (nD, ssd_conv_ch), jnp.float32)
    inp["ssd_dt_bias"] = _dt_bias(next(ks), (nD, SSD_HEADS))
    inp["ssd_a_log"] = _a_log(next(ks), (nD, SSD_HEADS))
    inp["ssd_d"] = 1.0 + 0.1 * jax.random.normal(next(ks), (nD, SSD_HEADS), jnp.float32)
    inp["ssd_norm_g"] = 1.0 + 0.02 * jax.random.normal(next(ks), (nD, SSD_INNER), jnp.float32)
    inp["ssd_w_out"] = _normal(next(ks), (nD, SSD_INNER, d), SSD_INNER, BETA_INIT)
    inp["ffn_w_gate"] = _normal(next(ks), (N_DENSE, d, D_FF), d)
    inp["ffn_w_up"] = _normal(next(ks), (N_DENSE, d, D_FF), d)
    inp["ffn_w_down"] = _normal(next(ks), (N_DENSE, D_FF, d), D_FF, BETA_INIT)
    inp["moe_w_router"] = _normal(next(ks), (N_MOE, d, N_EXPERTS), d)
    inp["moe_w_gate"] = _normal(next(ks), (N_MOE, N_EXPERTS, d, D_FF), d)
    inp["moe_w_up"] = _normal(next(ks), (N_MOE, N_EXPERTS, d, D_FF), d)
    inp["moe_w_down"] = _normal(next(ks), (N_MOE, N_EXPERTS, D_FF, d), D_FF, BETA_INIT)
    inp["ple_w_gate"] = _normal(next(ks), (DEPTH, d, d), d)
    inp["ple_b_gate"] = 0.02 * jax.random.normal(next(ks), (DEPTH, d), jnp.float32)
    inp["ple_w_proj"] = _normal(next(ks), (DEPTH, PLE_DIM, d), PLE_DIM)
    return inp

def reference(x, p, ln_g, ln_b, gm_w_in, gm_b_in, gm_ln_g, gm_ln_b, gm_w_s, gm_b_s, gm_w_out,
              fox_w_in, fox_b_f, fox_w_out, gdn_w_in, gdn_conv_w, gdn_a_log, gdn_dt_bias, gdn_norm_g, gdn_w_out,
              ssd_w_in, ssd_conv_w, ssd_conv_b, ssd_dt_bias, ssd_a_log, ssd_d, ssd_norm_g, ssd_w_out,
              ffn_w_gate, ffn_w_up, ffn_w_down, moe_w_router, moe_w_gate, moe_w_up, moe_w_down,
              ple_w_gate, ple_b_gate, ple_w_proj):
    h = x
    for i in range(DEPTH):
        m, j = i % N_MIXERS, i // N_MIXERS
        if m == 0:
            y = gmlp_mixer(h, gm_w_in[j], gm_b_in[j], gm_ln_g[j], gm_ln_b[j], gm_w_s[j], gm_b_s[j], gm_w_out[j])
        elif m == 1:
            y = fox_mixer(h, fox_w_in[j], fox_b_f[j], fox_w_out[j])
        elif m == 2:
            y = gdn_mixer(h, gdn_w_in[j], gdn_conv_w[j], gdn_a_log[j], gdn_dt_bias[j], gdn_norm_g[j], gdn_w_out[j])
        else:
            y = ssd_mixer(h, ssd_w_in[j], ssd_conv_w[j], ssd_conv_b[j], ssd_dt_bias[j], ssd_a_log[j], ssd_d[j],
                          ssd_norm_g[j], ssd_w_out[j])
        h = layer_norm(ALPHA * h + y, ln_g[i, 0], ln_b[i, 0])
        if i % 2 == 0:
            f = swiglu(h, ffn_w_gate[i // 2], ffn_w_up[i // 2], ffn_w_down[i // 2])
        else:
            f = moe_swiglu(h, moe_w_router[i // 2], moe_w_gate[i // 2], moe_w_up[i // 2], moe_w_down[i // 2])
        h = layer_norm(ALPHA * h + f, ln_g[i, 1], ln_b[i, 1])
        h = h + jax.nn.sigmoid(h @ ple_w_gate[i] + ple_b_gate[i]) * (p[i] @ ple_w_proj[i])
    return h


_drawn_inputs = setup_inputs


def setup_inputs(seed=0):
    import zlib

    import numpy as np

    out = dict(_drawn_inputs(seed))
    spreads = {}
    factors = {'gm_b_in': 5.694,
     'gm_ln_g': 77.877,
     'gm_ln_b': 76.397,
     'ple_b_gate': 7.899,
     'gm_b_s': 3.623}
    for name, (base, spread) in spreads.items():
        noise = np.random.default_rng([zlib.crc32(name.encode()), seed]).standard_normal(out[name].shape)
        drawn = base * np.exp(spread * noise) if base else spread * noise
        out[name] = __import__('jax').numpy.asarray(drawn.astype(out[name].dtype))
    for name, factor in factors.items():
        out[name] = (out[name] * factor).astype(out[name].dtype)
    return out
```

```python
from contextlib import ExitStack

import concourse.bass as bass
from concourse import mybir

F32 = mybir.dt.float32
F32R = mybir.dt.float32r
I32 = mybir.dt.int32
ALU = mybir.AluOpType
ACT = mybir.ActivationFunctionType
AX = mybir.AxisListType.X

P = 128
W = 512
RAW = 6
SPL = 3
LN_EPS = 1e-5


def build_trunk(nc, x, p, ln_g, ln_b, gm_w_in, gm_b_in, gm_ln_g, gm_ln_b, gm_w_s, gm_b_s, gm_w_out,
                fox_w_in, fox_b_f, fox_w_out, ffn_w_gate, ffn_w_up, ffn_w_down,
                moe_w_router, moe_w_gate, moe_w_up, moe_w_down, ple_w_gate, ple_b_gate, ple_w_proj, out):
    _, S, D = x.shape
    DEPTH = p.shape[0]
    PD = p.shape[3]
    T = S // P
    KD = D // P
    GW = gm_w_out.shape[1]
    GG = gm_w_s.shape[1]
    GC = GW // GG
    H = fox_b_f.shape[1]
    DH = D // H
    FA = DH + 2
    F = ffn_w_down.shape[1]
    NE = moe_w_router.shape[2]
    NJ = F // W
    ALPHA = float((2 * DEPTH) ** 0.25)
    assert T == 2 and D == 2 * W and F % W == 0 and GW == 4 * W and GC * 2 == W and PD == 2 * P
    assert gm_w_s.shape[2] == P and S == 2 * P

    G_GIN = 0
    N_GIN = 2 * GW // W
    G_GOUT = G_GIN + 2 * N_GIN
    G_FFN = G_GOUT + GW // (2 * P)
    G_BLK = 6
    G_PLE = G_FFN + G_BLK * NJ
    G_FIN = G_PLE + 5
    N_FIN = 3 * D // W
    G_FOUT = G_FIN + 2 * N_FIN
    G_MOE = G_FOUT + D // (2 * P)
    G_EXP = G_BLK * NJ
    assert G_EXP % RAW == 0 and G_BLK % SPL == 0 and G_BLK == RAW

    GIN_ORDER = [*range(N_GIN // 2, N_GIN), *range(N_GIN // 2)]

    base = (nc.sbuf_base + 31) // 32 * 32
    cursor = [base]

    def at(name, shape, dt, offset=None):
        size = 4
        for n in shape[1:]:
            size *= n
        if offset is None:
            offset = cursor[0]
            cursor[0] += (size + 31) // 32 * 32
        return nc.alloc_sbuf_tensor_at(name, shape, dt, offset=offset), offset + (size + 31) // 32 * 32

    def keep(name, shape, dt=F32):
        return at(name, shape, dt)[0]

    raw = keep("raw", [P, RAW, 4, W])
    wh = keep("wh", [P, SPL, 4, W], F32R)
    wl = keep("wl", [P, SPL, 4, W], F32R)
    h = keep("h", [P, T, D])
    hth_at = cursor[0]
    hth = keep("hth", [P, KD, S], F32R)
    htl = keep("htl", [P, KD, S], F32R)
    xh, nxt = at("xh", [P, T, D], F32R, hth_at)
    xl, _ = at("xl", [P, T, D], F32R, nxt)
    par_b = keep("par_b", [P, 4, D])
    par_a = cursor[0]
    b_in, end_a = at("b_in", [P, 2 * GW], F32)
    ln0, _ = at("ln0", [P, 4, D], F32, par_a)
    o_nat, nxt = at("o_nat", [P, T, D], F32, par_a)
    pn1, nxt = at("pn1", [P, T, PD], F32, par_a)
    pp1, nxt = at("pp1", [P, T, D], F32, nxt)
    ysh, nxt = at("ysh", [P, D], F32R, nxt)
    assert nxt <= end_a
    ple_b = keep("ple_b", [P, DEPTH, D])

    ident = keep("ident", [P, P])
    upper = keep("upper", [P, P])
    ones = keep("ones", [P, P])
    zeros = keep("zeros", [P, P], F32R)
    iota_i = keep("iota_i", [P, P], I32)
    iota = keep("iota", [P, P])
    mask = keep("mask", [P, 3 * P])
    bs_t = keep("bs_t", [P, GG])
    bf_bc = keep("bf_bc", [P, H])
    wf = keep("wf", [P, KD, H])
    wfh = keep("wfh", [P, KD, H], F32R)
    wfl = keep("wfl", [P, KD, H], F32R)
    wr = keep("wr", [P, KD, NE])
    wrh = keep("wrh", [P, KD, NE], F32R)
    wrl = keep("wrl", [P, KD, NE], F32R)
    stats = keep("stats", [P, T, 4, 6])
    mv = keep("mv", [P, T, 2])
    var = keep("var", [P, T])
    std = keep("std", [P, T])
    rstd = keep("rstd", [P, T])
    nwt = keep("nwt", [P, T])
    z_f = keep("z_f", [P, T, H])
    a_f = keep("a_f", [P, T, H])
    lg = keep("lg", [P, T, NE])
    top8 = keep("top8", [P, T, 8])
    eqk = keep("eqk", [P, T, NE])
    key = keep("key", [P, T])
    sel1 = keep("sel1", [P, T, NE])
    sel2 = keep("sel2", [P, T, NE])
    prio = keep("prio", [P, NE])
    prio_i = keep("prio_i", [P, NE], I32)
    gap = keep("gap", [P, T])
    den = keep("den", [P, T])
    w_top = keep("w_top", [P, 2, T])
    member = keep("member", [P, T, NE])
    slots = keep("slots", [P, 2, T, NE])
    comb = keep("comb", [P, T, NE])
    cnt = keep("cnt", [P, 1])
    cnt_i = keep("cnt_i", [P, 1], I32)
    wcur = keep("wcur", [P, T])
    wslot = keep("wslot", [P, 1])

    ph = cursor[0]
    u, nxt = at("u", [P, T, GW], F32, ph)
    v, nxt = at("v", [P, T, GW], F32, nxt)
    ws_raw, _ = at("ws_raw", [P, GG, P], F32, ph)
    ws_t, end = at("ws_t", [P, GG, P], F32, nxt)
    acc, nxt = at("acc", [P, T, D], F32, ph)
    bth, nxt = at("bth", [P, 4, S], F32R, nxt)
    btl, nxt = at("btl", [P, 4, S], F32R, nxt)
    sg, nxt = at("sg", [P, T, W], F32, nxt)
    hb, nxt = at("hb", [P, T, W], F32, nxt)
    per_layer = nxt
    xeh, nxt = at("xeh", [P, KD, P], F32R, nxt)
    xel, nxt = at("xel", [P, KD, P], F32R, nxt)
    sel, nxt = at("sel", [P, T, P], F32R, nxt)
    sel_t, nxt = at("sel_t", [P, S], F32R, nxt)
    end = max(end, nxt)
    ysl, nxt = at("ysl", [P, D], F32R, nxt)
    end = max(end, nxt)
    pn0, nxt = at("pn0", [P, T, PD], F32, per_layer)
    pth, nxt = at("pth", [P, PD // P, S], F32R, nxt)
    ptl, nxt = at("ptl", [P, PD // P, S], F32R, nxt)
    pp0, nxt = at("pp0", [P, T, D], F32, nxt)
    end = max(end, nxt)
    sig = acc
    q_nat, nxt = at("q_nat", [P, T, H, FA], F32, ph)
    k_nat, nxt = at("k_nat", [P, T, H, FA], F32, nxt)
    v_nat, nxt = at("v_nat", [P, T, D], F32, nxt)
    qk_t, nxt = at("qk_t", [P, 2, 2 * S], F32, nxt)
    prob, nxt = at("prob", [P, 2, 3 * P], F32, nxt)
    prob_t, nxt = at("prob_t", [P, 2, 3 * P], F32, nxt)
    nmax = at("nmax", [P, 2, T], F32, nxt)[0]
    rsum = at("rsum", [P, 2, T], F32, nxt + 32)[0]
    rinv = at("rinv", [P, 2, T], F32, nxt + 64)[0]
    end = max(end, nxt + 96)
    assert end <= nc.sbuf_usable_end, (end, nc.sbuf_usable_end)

    ps = [nc.alloc_psum_tensor(f"ps{i}", [P, W], F32) for i in range(8)]

    def sem(name):
        return nc.alloc_semaphore(name)

    raw_landed = [sem(f"raw_landed{i}") for i in range(RAW)]
    raw_landed2 = [sem(f"raw_landed2_{i}") for i in range(5)]
    streams = [dict(hi=sem(f"hi_split{i}"), lo=sem(f"lo_split{i}"), used=sem(f"used{i}"),
                    tp=sem(f"tp_filled{i}"), tp_hi=sem(f"tp_hi{i}"), tp_lo=sem(f"tp_lo{i}"),
                    var=sem(f"ln_var{i}"), std=sem(f"ln_std{i}"), h=sem(f"h_ready{i}"),
                    projc=sem(f"proj_copied{i}"), 
                    gb=sem(f"gate_biased{i}"), gs=sem(f"gate_sigmoid{i}"))
               for i in range(2)]
    x_landed = [sem(f"x_landed{m}") for m in range(T)]
    ws_landed = sem("ws_landed")
    b_in_landed = sem("b_in_landed")
    gln_landed = sem("gln_landed")
    bs_landed = sem("bs_landed")
    ln0_landed = sem("ln0_landed")
    ln1_landed = sem("ln1_landed")
    pleb_landed = sem("pleb_landed")
    pn_landed = [sem("pn0_landed"), sem("pn1_landed")]
    wf_landed = sem("wf_landed")
    bf_landed = sem("bf_landed")
    wr_landed = sem("wr_landed")
    out_landed = sem("out_landed")
    const_step = sem("const_step")
    const_ready = sem("const_ready")
    ws_tp = sem("ws_tp")
    ws_copied = sem("ws_copied")
    ws_masked = sem("ws_masked")
    gm_biased = sem("gm_biased")
    gm_gelu = sem("gm_gelu")
    v_normed = sem("v_normed")
    sv_full = sem("sv_full")
    mixed = sem("mixed")
    acc_init = sem("acc_init")
    silu_done = sem("silu_done")
    hid_ready = sem("hid_ready")
    part_full = sem("part_full")
    part_added = sem("part_added")
    small_split = sem("small_split")
    f_full = sem("f_full")
    f_exp = sem("f_exp")
    f_abs = sem("f_abs")
    f_log = sem("f_log")
    f_logf = sem("f_logf")
    c_full = sem("c_full")
    qk_ready = sem("qk_ready")
    fin_copied = sem("fin_copied")
    at_qk = sem("at_qk")
    at_qkc = sem("at_qkc")
    at_log = sem("at_log")
    at_masked = sem("at_masked")
    at_max = sem("at_max")
    at_exp = sem("at_exp")
    at_pt = sem("at_pt")
    at_ptc = sem("at_ptc")
    at_o = sem("at_o")
    at_on = sem("at_on")
    lg_full = sem("lg_full")
    gap_ready = sem("gap_ready")
    gap_exp = sem("gap_exp")
    mem_ready = sem("mem_ready")
    rank_full = sem("rank_full")
    route_ready = sem("route_ready")
    xh_ready = sem("xh_ready")
    xl_ready = sem("xl_ready")
    sel_ready = sem("sel_ready")
    st_full = sem("st_full")
    st_copied = sem("st_copied")
    gx_full = sem("gx_full")
    gx_hi = sem("gx_hi")
    gx_lo = sem("gx_lo")
    e_silu = sem("e_silu")
    e_hid = sem("e_hid")
    e_tp = sem("e_tp")
    e_hi = sem("e_hi")
    e_lo = sem("e_lo")
    ys_hi = sem("ys_hi")
    ys_lo = sem("ys_lo")
    sc_full = sem("sc_full")
    sc_added = sem("sc_added")
    moe_done = sem("moe_done")
    dve_step = sem("dve_step")
    dve_step2 = sem("dve_step2")

    def cols(w, n0, half):
        return w[half * 4 * P:(half + 1) * 4 * P, bass.ds(n0, W)].rearrange("(c p) n -> p c n", p=P)

    def rows(w, k0):
        return w[bass.ds(k0, 2 * P), :].rearrange("(c p) n -> p c n", p=P)

    def flat(t):
        return t.rearrange("p (c t) n -> p c (t n)", c=2)

    def split_phase(g):
        return g % RAW, g % SPL, g // RAW + 1

    whole = ExitStack()
    block = whole.enter_context(nc.Block())

    @block.sync
    def _(sp):
        g = [0]

        def load(src, by_rows=False):
            n = g[0]
            g[0] += 1
            slot = n % RAW
            if n >= RAW:
                sp.wait_ge(streams[0]["lo"], n - RAW + 1)
            dst = flat(raw[:, slot]) if by_rows else raw[:, slot]
            sp.dma_start(dst, src).then_inc(raw_landed[slot], 16)

        for m in range(T):
            sp.dma_start(h[:, m, :], x[0, m * P:(m + 1) * P, :]).then_inc(x_landed[m], 16)
        for nb in GIN_ORDER:
            for half in range(2):
                load(cols(gm_w_in[0], nb * W, half))
        for k in range(GW // (2 * P)):
            load(rows(gm_w_out[0], k * 2 * P), True)

        def block_loads(first, g0, gate, up, down, j):
            n = 0
            for w in (gate, up):
                for half in range(2):
                    wait_load(g0 + n, first + n, cols(w, j * W, half))
                    n += 1
            return n

        def wait_load(gv, gs, src, by_rows=False):
            slot = gs % RAW
            sp.wait_ge(streams[0]["lo"], gv - RAW + 1)
            dst = flat(raw[:, slot]) if by_rows else raw[:, slot]
            sp.dma_start(dst, src).then_inc(raw_landed[slot], 16)

        def swiglu_loads(first, g0, gate, up, down):
            block_loads(first, g0, gate, up, down, 0)
            with sp.Fori(1, NJ) as j:
                gj = sp.snap(g0 + 4 + (j - 1) * G_BLK)
                block_loads(first + 4, gj, gate, up, down, j)
                for k in range(2):
                    wait_load(gj + 4 + k, first + 8 + k, rows(down, (j - 1) * W + k * 2 * P), True)
            for k in range(2):
                wait_load(g0 + G_EXP - 2 + k, first + G_EXP - 2 + k, rows(down, (NJ - 1) * W + k * 2 * P), True)

        swiglu_loads(G_FFN, G_FFN, ffn_w_gate[0], ffn_w_up[0], ffn_w_down[0])
        g[0] = G_PLE
        load(rows(ple_w_proj[0], 0), True)
        for nb in range(2):
            for half in range(2):
                load(cols(ple_w_gate[0], nb * W, half))
        for nb in range(N_FIN):
            for half in range(2):
                load(cols(fox_w_in[0], nb * W, half))
        for k in range(D // (2 * P)):
            load(rows(fox_w_out[0], k * 2 * P), True)

        def experts(rnd):
            with sp.Fori(rnd * NE, (rnd + 1) * NE) as e:
                g0 = sp.snap(G_MOE + e * G_EXP)
                ex = sp.snap(e - rnd * NE)

                def of(w):
                    return w[0, bass.ds(ex, 1)].rearrange("a k n -> (a k) n")

                swiglu_loads(G_MOE, g0, of(moe_w_gate), of(moe_w_up), of(moe_w_down))

        experts(0)
        sp.wait_ge(route_ready, 1)
        with sp.If(sp.value_load(cnt_i[0:1, 0:1], min_val=0, max_val=S) > P):
            experts(1)
        sp.wait_ge(moe_done, 1)
        sp.dma_start(flat(raw[:, 0]), rows(ple_w_proj[1], 0)).then_inc(raw_landed2[0], 16)
        for n in range(4):
            sp.dma_start(raw[:, 1 + n], cols(ple_w_gate[1], n // 2 * W, n % 2)).then_inc(raw_landed2[1 + n], 16)
        for nb in range(2):
            for m in range(T):
                sp.wait_ge(streams[1]["h"], T + 1 + nb * T + m)
                sp.dma_start(out[0, m * P:(m + 1) * P, nb * W:(nb + 1) * W],
                             h[:, m, nb * W:(nb + 1) * W]).then_inc(out_landed, 16)
        sp.wait_ge(out_landed, 16 * 2 * T)

    @block.gpsimd
    def _(pool):
        step = [0]

        def seq(ins):
            step[0] += 1
            ins.then_inc(const_step, 1)
            pool.wait_ge(const_step, step[0])

        def bcast(dst, src, s):
            pool.dma_start(dst, src.partition_broadcast(P)).then_inc(s, 16)

        seq(pool.memset(ident[:, :], 0.0))
        seq(pool.affine_select(out=ident[:, :], in_=ident[:, :], compare_op=ALU.not_equal, fill=1.0, base=0,
                               pattern=[[-1, P]], channel_multiplier=1))
        pool.dma_start(ws_raw[:, :, :], gm_w_s[0].rearrange("g t s -> t g s")).then_inc(ws_landed, 16)
        bcast(b_in[:, :], gm_b_in[0], b_in_landed)
        seq(pool.memset(ones[:, :], 1.0))
        seq(pool.affine_select(out=upper[:, :], in_=ones[:, :], compare_op=ALU.is_ge, fill=0.0, base=0,
                               pattern=[[1, P]], channel_multiplier=-1))
        seq(pool.memset(zeros[:, :].bitcast(F32), 0.0))
        seq(pool.memset(mask[:, :], 0.0))
        for c in (0, 2):
            seq(pool.affine_select(out=mask[:, c * P:(c + 1) * P], in_=mask[:, c * P:(c + 1) * P],
                                   compare_op=ALU.is_ge, fill=-1e30, base=0, pattern=[[-1, P]],
                                   channel_multiplier=1))
        seq(pool.iota(iota_i[:, :], pattern=[[1, P]], base=0, channel_multiplier=0))
        seq(pool.tensor_copy(iota[:, :], iota_i[:, :]))
        seq(pool.iota(prio_i[:, :], pattern=[[-1, NE]], base=NE, channel_multiplier=0))
        pool.tensor_copy(prio[:, :], prio_i[:, :]).then_inc(const_ready, 1)
        for i, src in enumerate((gm_ln_g, gm_ln_b)):
            bcast(par_b[:, 2 * i:2 * i + 2, :].rearrange("p a d -> p (a d)"), src[0], gln_landed)
        pool.dma_start(bs_t[:, :], gm_b_s[0].rearrange("g t -> t g"),
                       allow_slow_non_contiguous=True).then_inc(bs_landed, 16)
        bcast(ple_b[:, :, :].rearrange("p a d -> p (a d)"), ple_b_gate.rearrange("a d -> (a d)"), pleb_landed)
        pool.dma_start(wf[:, :, :], fox_w_in[0, :, 3 * D:3 * D + H].rearrange("(c p) n -> p c n", p=P))\
            .then_inc(wf_landed, 16)
        bcast(bf_bc[:, :], fox_b_f[0], bf_landed)
        pool.dma_start(wr[:, :, :], moe_w_router[0].rearrange("(c p) n -> p c n", p=P)).then_inc(wr_landed, 16)
        pool.wait_ge(ws_copied, 2)
        pool.affine_select(out=ws_t[:, :, :], in_=ws_t[:, :, :], compare_op=ALU.is_ge, fill=0.0, base=0,
                           pattern=[[0, GG], [1, P]], channel_multiplier=-1).then_inc(ws_masked, 1)

        def norms(dst, layer, s):
            for n in range(2):
                bcast(dst[:, 2 * n, :], ln_g[layer, n], s)
                bcast(dst[:, 2 * n + 1, :], ln_b[layer, n], s)

        pool.wait_ge(gm_biased, 2 * N_GIN)
        norms(ln0, 0, ln0_landed)
        pool.wait_ge(mixed, 2 * T * 2)
        norms(par_b, 1, ln1_landed)
        pool.wait_ge(streams[0]["used"], G_FFN)
        pool.dma_start(pn0[:, :, :], p[0, 0].rearrange("(m p) n -> p m n", p=P)).then_inc(pn_landed[0], 16)
        pool.wait_ge(streams[0]["used"], G_MOE)
        pool.dma_start(pn1[:, :, :], p[1, 0].rearrange("(m p) n -> p m n", p=P)).then_inc(pn_landed[1], 16)

    @block.scalar
    def _(act):
        s0, s1 = streams

        def round_hi(g, st=s0, landed=None):
            slot, ss, n = split_phase(g)
            if landed is None:
                act.wait_ge(raw_landed[slot], 16 * n)
            else:
                act.wait_ge(landed[g], 16)
            if g >= SPL:
                act.wait_ge(st["used"], g - SPL + 1)
            nc.scalar.copy(wh[:, ss], raw[:, slot]).then_inc(st["hi"], 1)

        def round_at(gv, gs, rv):
            act.wait_ge(raw_landed[gs % RAW], rv * 16)
            act.wait_ge(s0["used"], gv - SPL + 1)
            nc.scalar.copy(wh[:, gs % SPL], raw[:, gs % RAW]).then_inc(s0["hi"], 1)

        nt = [0, 0]

        def tp_hi(dst, n=W, which=0):
            st = streams[which]
            act.wait_ge(st["tp"], nt[which] + 1)
            bank = ps[6 + nt[which] % 2]
            nc.scalar.copy(dst, bank[:, 0:n].rearrange("p (c t) -> p c t", t=P)).then_inc(st["tp_hi"], 1)
            nt[which] += 1

        def stream_t(dst, q, m):
            return dst[:, 4 * q:4 * q + 4, m * P:(m + 1) * P]

        def ln_sqrt(k, which=0):
            act.wait_ge(streams[which]["var"], k)
            nc.scalar.activation(std[:, :], var[:, :], ACT.Sqrt).then_inc(streams[which]["std"], 1)

        for m in range(T):
            for q in range(2):
                tp_hi(stream_t(hth, q, m))
        round_hi(0)
        round_hi(1)
        for i in range(N_GIN):
            round_hi(2 * i + 2)
            round_hi(2 * i + 3)
            act.wait_ge(gm_biased, T * (i + 1))
            nb = GIN_ORDER[i] * W
            dst = u[:, :, nb:nb + W] if nb < GW else v[:, :, nb - GW:nb - GW + W]
            nc.scalar.activation(dst, dst, ACT.Gelu_apprx_tanh).then_inc(gm_gelu, 1)
            if i == 4:
                ln_sqrt(1)
        for q in range(4):
            for m in range(T):
                tp_hi(stream_t(hth, q % 2, m))
            round_hi(G_GOUT + 2 * q + 2)
            round_hi(G_GOUT + 2 * q + 3)

        ln_sqrt(2)
        for m in range(T):
            for q in range(2):
                tp_hi(stream_t(hth, q, m))
        act.wait_ge(s0["h"], T)
        for m in range(T):
            nc.scalar.mul(acc[:, m, :], h[:, m, :], ALPHA).then_inc(acc_init, 1)
        g = G_FFN

        def silu(j):
            for m in range(T):
                nc.scalar.activation(sg[:, m, :], ps[m][:, :], ACT.Silu).then_inc(silu_done, 1)

        round_hi(g + 2)
        round_hi(g + 3)
        act.wait_ge(s0["used"], g + 2)
        silu(0)
        round_hi(g + 4)
        round_hi(g + 5)
        n_tp = nt[0]
        with act.Fori(1, NJ) as j:
            gj = act.snap(g + 4 + (j - 1) * G_BLK)
            rj = act.snap((g + 4) // RAW + j)

            def rnd(k):
                round_at(gj + k, g + 4 + k, rj + ((g + 4 + k) // RAW - (g + 4) // RAW))

            rnd(2)
            rnd(3)
            act.wait_ge(hid_ready, T * j)
            act.wait_ge(s0["used"], gj + 2)
            silu(j)
            for m in range(T):
                act.wait_ge(s0["tp"], j * T + (n_tp - T + m + 1))
                nc.scalar.copy(bth[:, :, m * P:(m + 1) * P],
                               ps[6 + m][:, :].rearrange("p (c t) -> p c t", t=P)).then_inc(s0["tp_hi"], 1)
            for k in range(4, 8):
                rnd(k)
        nt[0] += (NJ - 1) * T
        for m in range(T):
            tp_hi(bth[:, :, m * P:(m + 1) * P])

        def ple(which, g0, pp, landed=None):
            st = streams[which]
            for m in range(T):
                tp_hi(pth[:, :, m * P:(m + 1) * P], 2 * P, which)
            round_hi(g0, st, landed)
            round_hi(g0 + 1, st, landed)
            round_hi(g0 + 2, st, landed)
            for i in range(2 * T):
                act.wait_ge(st["used"], g0 + 1)
                nc.scalar.copy(pp[:, i // 2, i % 2 * W:(i % 2 + 1) * W], ps[i][:, :]).then_inc(st["projc"], 1)

        def ple_gate(which, g0, last, landed=None):
            st = streams[which]
            ln_sqrt(3 if which == 0 else 1, which)
            for m in range(T):
                for q in range(2):
                    tp_hi(stream_t(hth, q, m), W, which)
            for nb in range(2):
                for k in range(2):
                    n = g0 + 3 + 2 * nb + k
                    if n < last:
                        round_hi(n, st, landed)
                for m in range(T):
                    act.wait_ge(st["gb"], nb * T + m + 1)
                    part = sig[:, m, nb * W:(nb + 1) * W]
                    nc.scalar.activation(part, part, ACT.Sigmoid).then_inc(st["gs"], 1)

        ple(0, G_PLE, pp0)
        ple_gate(0, G_PLE, G_PLE + 7)
        act.wait_ge(wf_landed, 16)
        nc.scalar.copy(wfh[:, :, :], wf[:, :, :]).then_inc(small_split, 1)
        act.wait_ge(wr_landed, 16)
        nc.scalar.copy(wrh[:, :, :], wr[:, :, :]).then_inc(small_split, 1)
        for nb in range(2):
            for m in range(T):
                tp_hi(stream_t(hth, nb, m))
        act.wait_ge(f_abs, 1)
        nc.scalar.activation(a_f[:, :, :], a_f[:, :, :], ACT.Exp, scale=-1.0).then_inc(f_exp, 1)
        act.wait_ge(f_abs, 2)
        nc.scalar.activation(a_f[:, :, :], a_f[:, :, :], ACT.Ln).then_inc(f_log, 1)
        for i in range(N_FIN):
            round_hi(G_FIN + 2 * i + 2)
            round_hi(G_FIN + 2 * i + 3)
            act.wait_ge(s0["used"], G_FIN + 2 * i + 2)
            what, half = i // 2, i % 2
            for m in range(T):
                bank = ps[i % 2 * 2 + m]
                if what < 2:
                    dst = (q_nat, k_nat)[what][:, m, half * (H // 2):(half + 1) * (H // 2), 0:DH]
                    src = bank[:, :].rearrange("p (h d) -> p h d", d=DH)
                    ins = nc.scalar.mul(dst, src, DH ** -0.5) if what == 0 else nc.scalar.copy(dst, src)
                else:
                    ins = nc.scalar.copy(v_nat[:, m, half * W:(half + 1) * W], bank[:, :])
                ins.then_inc(fin_copied, 1)
        for s in range(H + 1):
            if s < H:
                act.wait_ge(at_qk, s + 1)
                nc.scalar.copy(qk_t[0:FA, s % 2, :], ps[6 + s % 2][0:FA, :]).then_inc(at_qkc, 1)
            if s >= 1:
                hd = s - 1
                act.wait_ge(at_max, T * (hd + 1))
                for m, (a, b) in enumerate(((0, P), (P, 3 * P))):
                    part = prob[:, hd % 2, a:b]
                    nc.scalar.activation(part, part, ACT.Exp, bias=nmax[:, hd % 2, m:m + 1],
                                         accum_out=rsum[:, hd % 2, m:m + 1]).then_inc(at_exp, 1)
        for m in range(T):
            for q in range(2):
                tp_hi(stream_t(hth, q, m))
        round_hi(G_FOUT + 2)
        round_hi(G_FOUT + 3)
        ln_sqrt(4)
        for m in range(T):
            for q in range(2):
                tp_hi(stream_t(hth, q, m))
        act.wait_ge(s0["h"], T + T + 2 * T + T)
        for m in range(T):
            nc.scalar.mul(acc[:, m, :], h[:, m, :], ALPHA).then_inc(acc_init, 1)
        act.wait_ge(lg_full, 1)
        for m in range(T):
            nc.scalar.copy(xh[:, m, :], h[:, m, :]).then_inc(xh_ready, 1)
        act.wait_ge(gap_ready, 1)
        nc.scalar.activation(gap[:, :], gap[:, :], ACT.Exp).then_inc(gap_exp, 1)

        def experts(rnd_no):
            with act.Fori(rnd_no * NE, (rnd_no + 1) * NE) as e:
                g0 = act.snap(G_MOE + e * G_EXP)
                r0 = act.snap(G_MOE // RAW + e * NJ)
                e1 = act.snap(e + 1)

                def rnd(k):
                    round_at(g0 + k, G_MOE + k, r0 + ((G_MOE + k) // RAW - G_MOE // RAW + 1))

                rnd(0)
                rnd(1)
                act.wait_ge(st_full, e1)
                nc.scalar.copy(sel_t[:, :], ps[7][:, 0:S]).then_inc(st_copied, 1)
                nc.scalar.copy(wslot[:, :], ps[7][:, S:S + 1]).then_inc(st_copied, 1)
                for q in range(2):
                    act.wait_ge(gx_full, e1 * 2 - (1 - q))
                    nc.scalar.copy(xeh[:, 4 * q:4 * q + 4, :],
                                   ps[4 + q][:, :].rearrange("p (c t) -> p c t", t=P)).then_inc(gx_hi, 1)
                rnd(2)
                rnd(3)
                act.wait_ge(s0["used"], g0 + 2)
                nc.scalar.activation(sg[:, 0, :], ps[0][:, :], ACT.Silu).then_inc(e_silu, 1)
                rnd(4)
                rnd(5)
                with act.Fori(1, NJ) as j:
                    gj = act.snap(g0 + j * G_BLK)
                    rj = act.snap(r0 + j)
                    ej = act.snap(e * NJ + j)

                    def rnd_j(k):
                        k -= 2
                        round_at(gj + k, G_MOE + k, rj + ((G_MOE + k) // RAW - G_MOE // RAW + 1))

                    rnd_j(2)
                    rnd_j(3)
                    act.wait_ge(e_hid, ej)
                    act.wait_ge(s0["used"], gj)
                    nc.scalar.activation(sg[:, 0, :], ps[0][:, :], ACT.Silu).then_inc(e_silu, 1)
                    act.wait_ge(e_tp, ej)
                    nc.scalar.copy(bth[:, :, 0:P],
                                   ps[6][:, :].rearrange("p (c t) -> p c t", t=P)).then_inc(e_hi, 1)
                    for k in range(4, 8):
                        rnd_j(k)
                act.wait_ge(e_tp, e1 * NJ)
                nc.scalar.copy(bth[:, :, 0:P],
                               ps[6][:, :].rearrange("p (c t) -> p c t", t=P)).then_inc(e_hi, 1)
                act.wait_ge(s0["used"], g0 + G_EXP)
                for half in range(2):
                    nc.scalar.activation(ysh[:, half * W:(half + 1) * W], ps[2 + half][:, :], ACT.Copy,
                                         scale=wslot[:, 0:1]).then_inc(ys_hi, 1)

        experts(0)
        act.wait_ge(route_ready, 1)
        with act.If(act.value_load(cnt_i[0:1, 0:1], min_val=0, max_val=S) > P):
            experts(1)
        ple(1, 0, pp1, raw_landed2)
        ple_gate(1, 0, 5, raw_landed2)

    @block.vector
    def _(dve):
        s0, s1 = streams
        step = [0, 0]

        def seq(ins, which=0):
            s = (dve_step, dve_step2)[which]
            step[which] += 1
            ins.then_inc(s, 1)
            dve.wait_ge(s, step[which])

        def rest_lo(g, st=s0):
            slot, ss, _ = split_phase(g)
            dve.wait_ge(st["hi"], g + 1)
            nc.vector.tensor_tensor(wl[:, ss], raw[:, slot], wh[:, ss].bitcast(F32), ALU.subtract)\
                .then_inc(st["lo"], 1)

        def rest_at(gv, gs):
            dve.wait_ge(s0["hi"], gv + 1)
            nc.vector.tensor_tensor(wl[:, gs % SPL], raw[:, gs % RAW], wh[:, gs % SPL].bitcast(F32),
                                    ALU.subtract).then_inc(s0["lo"], 1)

        nt = [0, 0]

        def tp_lo(dst, hi, n=W, which=0):
            st = streams[which]
            dve.wait_ge(st["tp_hi"], nt[which] + 1)
            bank = ps[6 + nt[which] % 2]
            nc.vector.tensor_tensor(dst, bank[:, 0:n].rearrange("p (c t) -> p c t", t=P), hi.bitcast(F32),
                                    ALU.subtract).then_inc(st["tp_lo"], 1)
            nt[which] += 1

        def stream_t(dst, q, m):
            return dst[:, 4 * q:4 * q + 4, m * P:(m + 1) * P]

        def stream_lo(q, m, which=0):
            tp_lo(stream_t(htl, q, m), stream_t(hth, q, m), W, which)

        def ln_var(n_stats, which=0):
            for m in range(T):
                seq(nc.vector.bn_aggr(mv[:, m, :], stats[:, m, 0:n_stats, :].rearrange("p a b -> p (a b)")), which)
            nc.vector.tensor_scalar(var[:, :], mv[:, :, 1], LN_EPS, None, ALU.add)\
                .then_inc(streams[which]["var"], 1)

        def ln_rstd(k, which=0):
            dve.wait_ge(streams[which]["std"], k)
            seq(nc.vector.reciprocal(rstd[:, :], std[:, :]), which)
            seq(nc.vector.tensor_tensor(nwt[:, :], rstd[:, :], rstd[:, :], ALU.mult), which)
            seq(nc.vector.tensor_tensor(nwt[:, :], nwt[:, :], var[:, :], ALU.mult), which)
            seq(nc.vector.tensor_scalar(nwt[:, :], nwt[:, :], -0.5, 1.5, ALU.mult, ALU.add), which)
            seq(nc.vector.tensor_tensor(rstd[:, :], rstd[:, :], nwt[:, :], ALU.mult), which)

        def ln_apply(dst, src, m, gain, bias, done, which=0):
            seq(nc.vector.tensor_scalar(dst, src, mv[:, m, 0:1], rstd[:, m:m + 1], ALU.subtract, ALU.mult), which)
            seq(nc.vector.tensor_tensor(dst, dst, gain, ALU.mult), which)
            nc.vector.tensor_tensor(dst, dst, bias, ALU.add).then_inc(done, 1)

        def norm(k, par, n, which=0):
            for m in range(T):
                for half in range(2):
                    seq(nc.vector.bn_stats(stats[:, m, half, :], acc[:, m, half * W:(half + 1) * W]), which)
            ln_var(2, which)
            ln_rstd(k, which)
            for m in range(T):
                ln_apply(h[:, m, :], acc[:, m, :], m, par[:, 2 * n, :], par[:, 2 * n + 1, :],
                         streams[which]["h"], which)

        def residual():
            for i in range(2 * T):
                m, half = i // 2, i % 2
                part = slice(half * W, (half + 1) * W)
                seq(nc.vector.scalar_tensor_tensor(out=acc[:, m, part], in0=h[:, m, part], scalar=ALPHA,
                                                   in1=ps[i][:, :], op0=ALU.mult, op1=ALU.add))

        dve.wait_ge(x_landed[0], 16)
        for m in range(T):
            for q in range(2):
                stream_lo(q, m)
        for i in range(2):
            dve.wait_ge(ws_tp, i + 1)
            nc.vector.tensor_copy(ws_t[:, 4 * i:4 * i + 4, :],
                                  ps[4 + i][:, :].rearrange("p (g t) -> p g t", t=P)).then_inc(ws_copied, 1)
        rest_lo(0)
        rest_lo(1)
        dve.wait_ge(b_in_landed, 16)

        def v_stats(i):
            dve.wait_ge(gm_gelu, i + 1)
            for m in range(T):
                seq(nc.vector.bn_stats(stats[:, m, i, :], v[:, m, i * W:(i + 1) * W]))

        for i in range(N_GIN):
            rest_lo(2 * i + 2)
            rest_lo(2 * i + 3)
            dve.wait_ge(s0["used"], 2 * i + 2)
            nb = GIN_ORDER[i] * W
            for m in range(T):
                dst = u[:, m, nb:nb + W] if nb < GW else v[:, m, nb - GW:nb - GW + W]
                nc.vector.tensor_tensor(dst, ps[i % 2 * 2 + m][:, :], b_in[:, nb:nb + W], ALU.add)\
                    .then_inc(gm_biased, 1)
            if 1 <= i <= 4:
                v_stats(i - 1)
            if i == 4:
                ln_var(4)
            if i == 5:
                ln_rstd(1)
                dve.wait_ge(gln_landed, 32)
            if i in (5, 6):
                m = i - 5
                ln_apply(v[:, m, :], v[:, m, :], m, par_b[:, 0:2, :].rearrange("p a d -> p (a d)"),
                         par_b[:, 2:4, :].rearrange("p a d -> p (a d)"), v_normed)
        dve.wait_ge(gm_gelu, N_GIN)
        dve.wait_ge(bs_landed, 16)
        n_mix = 0
        for q in range(4):
            for m in range(T):
                n_mix += 1
                dve.wait_ge(sv_full, n_mix)
                for k in range(2):
                    grp = 2 * q + k
                    part = u[:, m, grp * GC:(grp + 1) * GC]
                    nc.vector.scalar_tensor_tensor(out=part, in0=ps[4 + m][:, k * GC:(k + 1) * GC],
                                                   scalar=bs_t[:, grp:grp + 1], in1=part, op0=ALU.add,
                                                   op1=ALU.mult).then_inc(mixed, 1)
            if q >= 1:
                for m in range(T):
                    stream_lo((q - 1) % 2, m)
                rest_lo(G_GOUT + 2 * q)
                rest_lo(G_GOUT + 2 * q + 1)
        for m in range(T):
            stream_lo(1, m)
        rest_lo(G_FFN)
        rest_lo(G_FFN + 1)
        dve.wait_ge(s0["used"], G_FFN)
        residual()
        dve.wait_ge(ln0_landed, 64)
        norm(2, ln0, 0)
        for m in range(T):
            for q in range(2):
                stream_lo(q, m)
        g = G_FFN

        def hid(j):
            for m in range(T):
                nc.vector.tensor_tensor(hb[:, m, :], ps[2 + m][:, :], sg[:, m, :], ALU.mult)\
                    .then_inc(hid_ready, 1)

        def parts(n0, gv):
            for i in range(2 * T):
                m, half = i // 2, i % 2
                part = acc[:, m, half * W:(half + 1) * W]
                if i < 2 * T - 1:
                    dve.wait_ge(part_full, n0 + (i + 1))
                else:
                    dve.wait_ge(s0["used"], gv + 2)
                nc.vector.tensor_tensor(part, part, ps[4 + i % 2][:, :], ALU.add).then_inc(part_added, 1)

        rest_lo(g + 2)
        rest_lo(g + 3)
        rest_lo(g + 4)
        rest_lo(g + 5)
        dve.wait_ge(acc_init, T)
        dve.wait_ge(silu_done, T)
        dve.wait_ge(s0["used"], g + 4)
        hid(0)
        n_tp = nt[0]
        with dve.Fori(1, NJ) as j:
            gj = dve.snap(g + 4 + (j - 1) * G_BLK)
            rest_at(gj + 2, g + 6)
            rest_at(gj + 3, g + 7)
            for m in range(T):
                dve.wait_ge(s0["tp_hi"], j * T + (n_tp - T + m + 1))
                nc.vector.tensor_tensor(btl[:, :, m * P:(m + 1) * P],
                                        ps[6 + m][:, :].rearrange("p (c t) -> p c t", t=P),
                                        bth[:, :, m * P:(m + 1) * P].bitcast(F32), ALU.subtract)\
                    .then_inc(s0["tp_lo"], 1)
            rest_at(gj + 4, g + 8)
            rest_at(gj + 5, g + 9)
            dve.wait_ge(silu_done, j * T + T)
            dve.wait_ge(s0["used"], gj + 4)
            hid(j)
            rest_at(gj + 6, g + 10)
            parts((j - 1) * (2 * T - 1), gj + 4)
            rest_at(gj + 7, g + 11)
        nt[0] += (NJ - 1) * T
        for m in range(T):
            tp_lo(btl[:, :, m * P:(m + 1) * P], bth[:, :, m * P:(m + 1) * P])
        parts((NJ - 1) * (2 * T - 1), g + G_EXP - 2)
        dve.wait_ge(part_added, NJ * 2 * T)

        def ple(which, g0, k, par, pp, last):
            st = streams[which]
            for m in range(T):
                tp_lo(ptl[:, :, m * P:(m + 1) * P], pth[:, :, m * P:(m + 1) * P], 2 * P, which)
            for i in range(3):
                rest_lo(g0 + i, st)
            norm(k, par, 1, which)
            for m in range(T):
                for q in range(2):
                    stream_lo(q, m, which)
            for nb in range(2):
                for i in range(2):
                    n = g0 + 3 + 2 * nb + i
                    if n < last:
                        rest_lo(n, st)
                part = slice(nb * W, (nb + 1) * W)
                dve.wait_ge(st["used"], g0 + 3 + 2 * nb)
                for m in range(T):
                    nc.vector.tensor_tensor(sig[:, m, part], ps[2 * nb + m][:, :], ple_b[:, which, part],
                                            ALU.add).then_inc(st["gb"], 1)
                for m in range(T):
                    dve.wait_ge(st["gs"], nb * T + m + 1)
                    seq(nc.vector.tensor_tensor(sig[:, m, part], sig[:, m, part], pp[:, m, part], ALU.mult), which)
                    nc.vector.tensor_tensor(h[:, m, part], h[:, m, part], sig[:, m, part], ALU.add)\
                        .then_inc(st["h"], 1)

        dve.wait_ge(pleb_landed, 16)
        ple(0, G_PLE, 3, ln0, pp0, G_PLE + 7)
        dve.wait_ge(small_split, 1)
        nc.vector.tensor_tensor(wfl[:, :, :], wf[:, :, :], wfh[:, :, :].bitcast(F32), ALU.subtract)\
            .then_inc(small_split, 1)
        dve.wait_ge(small_split, 3)
        nc.vector.tensor_tensor(wrl[:, :, :], wr[:, :, :], wrh[:, :, :].bitcast(F32), ALU.subtract)\
            .then_inc(small_split, 1)
        for nb in range(2):
            for m in range(T):
                stream_lo(nb, m)
        dve.wait_ge(f_full, 1)
        dve.wait_ge(bf_landed, 16)
        for m in range(T):
            seq(nc.vector.tensor_tensor(z_f[:, m, :], ps[4][:, m * H:(m + 1) * H], bf_bc[:, :], ALU.add))
        nc.vector.scalar_tensor_tensor(out=a_f[:, :, :], in0=z_f[:, :, :], scalar=-1.0, in1=z_f[:, :, :],
                                       op0=ALU.mult, op1=ALU.max).then_inc(f_abs, 1)
        dve.wait_ge(f_exp, 1)
        nc.vector.tensor_scalar(a_f[:, :, :], a_f[:, :, :], 1.0, None, ALU.add).then_inc(f_abs, 1)
        seq(nc.vector.tensor_scalar(z_f[:, :, :], z_f[:, :, :], 0.0, None, ALU.min))
        dve.wait_ge(f_log, 1)
        nc.vector.tensor_tensor(z_f[:, :, :], z_f[:, :, :], a_f[:, :, :], ALU.subtract).then_inc(f_logf, 1)
        dve.wait_ge(c_full, 1)
        for m in range(T):
            c = ps[5][:, m * H:(m + 1) * H]
            nc.vector.memset(q_nat[:, m, :, DH], 1.0).then_inc(qk_ready, 1)
            nc.vector.tensor_copy(q_nat[:, m, :, DH + 1], c).then_inc(qk_ready, 1)
            nc.vector.tensor_scalar(k_nat[:, m, :, DH], c, -1.0, None, ALU.mult).then_inc(qk_ready, 1)
            nc.vector.memset(k_nat[:, m, :, DH + 1], 1.0).then_inc(qk_ready, 1)
        for i in range(N_FIN):
            rest_lo(G_FIN + 2 * i + 2)
            rest_lo(G_FIN + 2 * i + 3)
        for s in range(1, H + 3):
            if s <= H:
                hd = s - 1
                dve.wait_ge(at_log, hd + 1)
                if hd >= 2:
                    dve.wait_ge(at_pt, hd - 1)
                nc.vector.tensor_tensor(prob[:, hd % 2, :], ps[hd % 2][:, 0:3 * P], mask[:, :], ALU.add)\
                    .then_inc(at_masked, 1)
            if 0 <= s - 2 < H:
                hd = s - 2
                dve.wait_ge(at_pt, hd + 1)
                if hd >= 2:
                    dve.wait_ge(at_o, hd - 1)
                nc.vector.tensor_copy(prob_t[:, hd % 2, :], ps[2 + hd % 2][:, 0:3 * P]).then_inc(at_ptc, 1)
                if hd >= 2:
                    dve.wait_ge(at_on, T * (hd - 1))
                seq(nc.vector.reciprocal(rinv[:, hd % 2, :], rsum[:, hd % 2, :]))
            if s - 1 < H:
                hd = s - 1
                dve.wait_ge(at_masked, hd + 1)
                for m, (a, b) in enumerate(((0, P), (P, 3 * P))):
                    nc.vector.tensor_reduce(nmax[:, hd % 2, m:m + 1], prob[:, hd % 2, a:b], AX, ALU.max,
                                            negate=True).then_inc(at_max, 1)
            if s >= 3:
                hd = s - 3
                dve.wait_ge(at_o, hd + 1)
                for m in range(T):
                    nc.vector.tensor_scalar(o_nat[:, m, hd * DH:(hd + 1) * DH],
                                            ps[4 + hd % 2][:, m * DH:(m + 1) * DH],
                                            rinv[:, hd % 2, m:m + 1], None, ALU.mult).then_inc(at_on, 1)
        for m in range(T):
            for q in range(2):
                stream_lo(q, m)
        rest_lo(G_FOUT + 2)
        rest_lo(G_FOUT + 3)
        dve.wait_ge(s0["used"], G_MOE)
        residual()
        dve.wait_ge(ln1_landed, 64)
        norm(4, par_b, 0)
        for m in range(T):
            for q in range(2):
                stream_lo(q, m)
        dve.wait_ge(lg_full, 1)
        dve.wait_ge(const_ready, 1)
        seq(nc.vector.tensor_copy(lg[:, :, :], ps[4][:, 0:T * NE].rearrange("p (m e) -> p m e", e=NE)))
        for m in range(T):
            seq(nc.vector.max(top8[:, m, :], lg[:, m, :]))
        nc.vector.tensor_tensor(gap[:, :], top8[:, :, 1], top8[:, :, 0], ALU.subtract).then_inc(gap_ready, 1)

        def first(dst, m, rank, but=None):
            seq(nc.vector.tensor_scalar(eqk[:, m, :], lg[:, m, :], top8[:, m, rank:rank + 1], None, ALU.is_equal))
            if but is not None:
                seq(nc.vector.tensor_tensor(eqk[:, m, :], eqk[:, m, :], but, ALU.is_gt))
            seq(nc.vector.tensor_tensor(eqk[:, m, :], eqk[:, m, :], prio[:, :], ALU.mult))
            seq(nc.vector.tensor_reduce(key[:, m:m + 1], eqk[:, m, :], AX, ALU.max))
            seq(nc.vector.tensor_scalar(dst, prio[:, :], key[:, m:m + 1], None, ALU.is_equal))

        for m in range(T):
            first(sel1[:, m, :], m, 0)
            first(sel2[:, m, :], m, 1, sel1[:, m, :])
        nc.vector.tensor_tensor(member[:, :, :], sel1[:, :, :], sel2[:, :, :], ALU.add).then_inc(mem_ready, 1)
        dve.wait_ge(gap_exp, 1)
        seq(nc.vector.tensor_scalar(den[:, :], gap[:, :], 1.0, None, ALU.add))
        seq(nc.vector.reciprocal(w_top[:, 0, :], den[:, :]))
        seq(nc.vector.tensor_tensor(w_top[:, 1, :], w_top[:, 0, :], gap[:, :], ALU.mult))
        for m in range(T):
            seq(nc.vector.tensor_scalar(comb[:, m, :], sel1[:, m, :], w_top[:, 0, m:m + 1], None, ALU.mult))
            seq(nc.vector.scalar_tensor_tensor(out=comb[:, m, :], in0=sel2[:, m, :], scalar=w_top[:, 1, m:m + 1],
                                               in1=comb[:, m, :], op0=ALU.mult, op1=ALU.add))
        dve.wait_ge(rank_full, 1)
        ranks = ps[5][:, 0:T * NE].rearrange("p (m e) -> p m e", e=NE)
        seq(nc.vector.tensor_tensor(slots[:, 0, :, :], member[:, :, :], ranks, ALU.mult))
        seq(nc.vector.tensor_scalar(slots[:, 0, :, :], slots[:, 0, :, :], -1.0, None, ALU.add))
        seq(nc.vector.tensor_scalar(slots[:, 1, :, :], slots[:, 0, :, :], float(-P), None, ALU.add))
        seq(nc.vector.tensor_reduce(cnt[:, :], ps[5][:, T * NE:(T + 1) * NE], AX, ALU.max))
        nc.vector.tensor_copy(cnt_i[:, :], cnt[:, :]).then_inc(route_ready, 1)
        for m in range(T):
            dve.wait_ge(xh_ready, m + 1)
            nc.vector.tensor_tensor(xl[:, m, :], h[:, m, :], xh[:, m, :].bitcast(F32), ALU.subtract)\
                .then_inc(xl_ready, 1)
        dve.wait_ge(acc_init, 2 * T)

        def experts(rnd_no):
            with dve.Fori(rnd_no * NE, (rnd_no + 1) * NE) as e:
                g0 = dve.snap(G_MOE + e * G_EXP)
                e1 = dve.snap(e + 1)
                ex = dve.snap(e - rnd_no * NE)
                for m in range(T):
                    nc.vector.tensor_scalar(sel[:, m, :], iota[:, :], slots[:, rnd_no, m, bass.ds(ex, 1)], None,
                                            ALU.is_equal).then_inc(sel_ready, 1)
                nc.vector.tensor_copy(wcur[:, :], comb[:, :, bass.ds(ex, 1)].rearrange("p m a -> p (m a)"))\
                    .then_inc(sel_ready, 1)
                rest_at(g0, G_MOE)
                rest_at(g0 + 1, G_MOE + 1)
                for q in range(2):
                    dve.wait_ge(gx_hi, e1 * 2 - (1 - q))
                    part = slice(4 * q, 4 * q + 4)
                    nc.vector.tensor_tensor(xel[:, part, :], ps[4 + q][:, :].rearrange("p (c t) -> p c t", t=P),
                                            xeh[:, part, :].bitcast(F32), ALU.subtract).then_inc(gx_lo, 1)
                for k in range(2, 6):
                    rest_at(g0 + k, G_MOE + k)

                def hidden(n, gv):
                    dve.wait_ge(e_silu, n)
                    dve.wait_ge(s0["used"], gv)
                    nc.vector.tensor_tensor(hb[:, 0, :], ps[1][:, :], sg[:, 0, :], ALU.mult).then_inc(e_hid, 1)

                def hidden_lo(n):
                    dve.wait_ge(e_hi, n)
                    nc.vector.tensor_tensor(btl[:, :, 0:P], ps[6][:, :].rearrange("p (c t) -> p c t", t=P),
                                            bth[:, :, 0:P].bitcast(F32), ALU.subtract).then_inc(e_lo, 1)

                hidden(e * NJ + 1, g0 + 4)
                with dve.Fori(1, NJ) as j:
                    gj = dve.snap(g0 + j * G_BLK)
                    ej = dve.snap(e * NJ + j)
                    rest_at(gj, G_MOE)
                    rest_at(gj + 1, G_MOE + 1)
                    hidden_lo(ej)
                    rest_at(gj + 2, G_MOE + 2)
                    rest_at(gj + 3, G_MOE + 3)
                    hidden(ej + 1, gj + 2)
                    rest_at(gj + 4, G_MOE + 4)
                    rest_at(gj + 5, G_MOE + 5)
                hidden_lo(e1 * NJ)
                for half in range(2):
                    dve.wait_ge(ys_hi, e1 * 2 - (1 - half))
                    part = slice(half * W, (half + 1) * W)
                    nc.vector.scalar_tensor_tensor(out=ysl[:, part], in0=ps[2 + half][:, :], scalar=wslot[:, 0:1],
                                                   in1=ysh[:, part].bitcast(F32), op0=ALU.mult,
                                                   op1=ALU.subtract).then_inc(ys_lo, 1)
                for i in range(2 * T):
                    half, m = i // 2, i % 2
                    dve.wait_ge(sc_full, e1 * (2 * T) - (2 * T - 1 - i))
                    part = acc[:, m, half * W:(half + 1) * W]
                    nc.vector.tensor_tensor(part, part, ps[4 + i % 2][:, :], ALU.add).then_inc(sc_added, 1)
                dve.wait_ge(sc_added, e1 * (2 * T))

        experts(0)
        dve.wait_ge(route_ready, 1)
        with dve.If(dve.value_load(cnt_i[0:1, 0:1], min_val=0, max_val=S) > P):
            experts(1)
        nc.vector.memset(nwt[:, :], 0.0).then_inc(moe_done, 1)
        ple(1, 0, 1, par_b, pp1, 5)

    @block.tensor
    def _(pe):
        s0, s1 = streams

        def mm(o, a, b, start, stop):
            return nc.tensor.matmul(o, a, b, start=start, stop=stop)

        def mm3(o, ah, al, slot, c, start, stop):
            mm(o, ah, wh[:, slot, c], start, False)
            mm(o, ah, wl[:, slot, c], False, False)
            return mm(o, al, wh[:, slot, c], False, stop)

        nt = [0, 0]

        def turn(srcs, which=0):
            st = streams[which]
            n = nt[which]
            if n >= 2:
                pe.wait_ge(st["tp_lo"], n - 1)
            for c, src in enumerate(srcs):
                last = nc.tensor.transpose(ps[6 + n % 2][:, c * P:(c + 1) * P], src, ident[:, :])
            last.then_inc(st["tp"], 1)
            nt[which] += 1

        def turned(which=0):
            pe.wait_ge(streams[which]["tp_lo"], nt[which])

        def quarter(t, m, q):
            return [t[:, m, (4 * q + c) * P:(4 * q + c + 1) * P] for c in range(4)]

        def cols_granules(g, banks, st=s0, g_of=None, last_inc=None):
            for half in range(2):
                pe.wait_ge(st["lo"], g + half + 1)
                for c in range(4):
                    k = 4 * half + c
                    for m in range(T):
                        tok = slice(m * P, (m + 1) * P)
                        last = mm3(ps[banks[m]][:, :], hth[:, k, tok], htl[:, k, tok],
                                   (g_of if g_of is not None else g) % SPL if half == 0 else
                                   ((g_of if g_of is not None else g) + 1) % SPL, c, k == 0, k == KD - 1)
                last.then_inc(st["used"], 1)

        def rows_granule(g, ah, al, k0, k, first, final, st=s0):
            pe.wait_ge(st["lo"], g + 1)
            for kk in range(2):
                for m in range(T):
                    tok = slice(m * P, (m + 1) * P)
                    for half in range(2):
                        last = mm3(ps[2 * m + half][:, :], ah[:, k0 + kk, tok], al[:, k0 + kk, tok], g % SPL,
                                   2 * kk + half, first and kk == 0, final and kk == 1)
            last.then_inc(st["used"], 1)

        pe.wait_ge(const_step, 2)
        for m in range(T):
            pe.wait_ge(x_landed[m], 16)
            for q in range(2):
                turn(quarter(h, m, q))
        pe.wait_ge(ws_landed, 16)
        for i in range(2):
            for c in range(4):
                last = nc.tensor.transpose(ps[4 + i][:, c * P:(c + 1) * P], ws_raw[:, 4 * i + c, :], ident[:, :])
            last.then_inc(ws_tp, 1)
        turned()
        for i in range(N_GIN):
            if i >= 2:
                pe.wait_ge(gm_biased, T * (i - 1))
            cols_granules(2 * i, [i % 2 * 2, i % 2 * 2 + 1])
        pe.wait_ge(v_normed, T)
        pe.wait_ge(ws_masked, 1)

        def u_turn(q):
            for m in range(T):
                pe.wait_ge(mixed, (q * T + m + 1) * 2)
                turn(quarter(u, m, q))

        def u_product(q):
            turned()
            for k in range(2):
                rows_granule(G_GOUT + 2 * q + k, hth, htl, 4 * (q % 2) + 2 * k, k, q == 0 and k == 0,
                             q == 3 and k == 1)

        for q in range(4):
            for m in range(T):
                if q >= 1:
                    pe.wait_ge(mixed, ((q - 1) * T + m + 1) * 2)
                else:
                    pe.wait_ge(ws_copied, 2)
                for k in range(2):
                    grp = 2 * q + k
                    last = mm(ps[4 + m][:, k * GC:(k + 1) * GC], ws_t[:, grp, :], v[:, m, grp * GC:(grp + 1) * GC],
                              True, True)
                last.then_inc(sv_full, 1)
            if q >= 1:
                u_turn(q - 1)
                if q == 1:
                    pe.wait_ge(gm_biased, T * N_GIN)
                u_product(q - 1)
        u_turn(3)
        u_product(3)

        n_h = [0]

        def stream_turn(which=0):
            for m in range(T):
                n_h[0] += 1
                pe.wait_ge(streams[which]["h"], n_h[0])
                for q in range(2):
                    turn(quarter(h, m, q), which)
            turned(which)

        stream_turn()

        g = G_FFN

        def down(gv, gs, n0):
            pe.wait_ge(s0["lo"], gv + 2)
            for i in range(2 * T):
                m, half = i // 2, i % 2
                if i >= 2:
                    pe.wait_ge(part_added, n0 + (i - 1))
                for kk in range(4):
                    tok = slice(m * P, (m + 1) * P)
                    last = mm3(ps[4 + i % 2][:, :], bth[:, kk, tok], btl[:, kk, tok], (gs + kk // 2) % SPL,
                               2 * (kk % 2) + half, kk == 0, kk == 3)
                if i < 2 * T - 1:
                    last.then_inc(part_full, 1)
                else:
                    last.then_inc(s0["used"], 2)

        cols_granules(g, [0, 1])
        cols_granules(g + 2, [2, 3])
        n_tp = nt[0]
        with pe.Fori(1, NJ) as j:
            gj = pe.snap(g + 4 + (j - 1) * G_BLK)
            pe.wait_ge(silu_done, j * T)
            cols_granules(gj, [0, 1], g_of=g + 4)
            for m in range(T):
                pe.wait_ge(hid_ready, (j - 1) * T + (m + 1))
                for c in range(4):
                    last = nc.tensor.transpose(ps[6 + m][:, c * P:(c + 1) * P], hb[:, m, c * P:(c + 1) * P],
                                               ident[:, :])
                last.then_inc(s0["tp"], 1)
            cols_granules(gj + 2, [2, 3], g_of=g + 6)
            pe.wait_ge(s0["tp_lo"], j * T + n_tp)
            down(gj + 4, g + 8, (j - 1) * (2 * T))
        nt[0] += (NJ - 1) * T
        assert nt[0] % 2 == 0
        pe.wait_ge(hid_ready, NJ * T)
        for m in range(T):
            turn([hb[:, m, c * P:(c + 1) * P] for c in range(4)])
        turned()
        down(g + G_EXP - 2, g + G_EXP - 2, (NJ - 1) * 2 * T)

        def ple(which, g0, pn):
            st = streams[which]
            pe.wait_ge(pn_landed[which], 16)
            for m in range(T):
                turn([pn[:, m, c * P:(c + 1) * P] for c in range(2)], which)
            turned(which)
            rows_granule(g0, pth, ptl, 0, 0, True, True, st)
            stream_turn(which)
            pe.wait_ge(st["projc"], 2 * T)
            for nb in range(2):
                cols_granules(g0 + 1 + 2 * nb, [2 * nb, 2 * nb + 1], st)

        ple(0, G_PLE, pn0)
        for nb in range(2):
            for m in range(T):
                n_h[0] += 1
                pe.wait_ge(s0["h"], n_h[0])
                turn(quarter(h, m, nb))
        turned()

        def small(bank, n, wsh, wsl):
            for m in range(T):
                tok = slice(m * P, (m + 1) * P)
                o = ps[bank][:, m * n:(m + 1) * n]
                for k in range(KD):
                    mm(o, hth[:, k, tok], wsh[:, k, :], k == 0, False)
                    mm(o, hth[:, k, tok], wsl[:, k, :], False, False)
                    last = mm(o, htl[:, k, tok], wsh[:, k, :], False, k == KD - 1)
            return last

        pe.wait_ge(small_split, 4)
        small(4, H, wfh, wfl).then_inc(f_full, 1)

        def prefix(bank, n, src):
            mm(ps[bank][:, 0:n], upper[:, :], src[:, 0, :], True, True)
            mm(ps[bank][:, n:2 * n], upper[:, :], src[:, 1, :], True, False)
            return mm(ps[bank][:, n:2 * n], ones[:, :], src[:, 0, :], False, True)

        pe.wait_ge(f_logf, 1)
        pe.wait_ge(const_ready, 1)
        prefix(5, H, z_f).then_inc(c_full, 1)
        for i in range(N_FIN):
            if i >= 2:
                pe.wait_ge(fin_copied, T * (i - 1))
            cols_granules(G_FIN + 2 * i, [i % 2 * 2, i % 2 * 2 + 1])
        pe.wait_ge(fin_copied, T * N_FIN)
        pe.wait_ge(qk_ready, 4 * T)
        for s in range(H + 3):
            if s < H:
                b = s % 2
                if s >= 2:
                    pe.wait_ge(at_qkc, s - 1)
                for i, t in enumerate((q_nat, k_nat)):
                    for m in range(T):
                        last = nc.tensor.transpose(ps[6 + b][0:FA, i * S + m * P:i * S + (m + 1) * P],
                                                   t[:, m, s, :], ident[:, :])
                last.then_inc(at_qk, 1)
            if 0 <= s - 1 < H:
                hd = s - 1
                b = hd % 2
                pe.wait_ge(at_qkc, hd + 1)
                if hd >= 2:
                    pe.wait_ge(at_masked, hd - 1)
                mm(ps[b][:, 0:P], qk_t[0:FA, b, 0:P], qk_t[0:FA, b, S:S + P], True, True)
                mm(ps[b][:, P:3 * P], qk_t[0:FA, b, P:2 * P], qk_t[0:FA, b, S:2 * S], True, True)\
                    .then_inc(at_log, 1)
            if 0 <= s - 2 < H:
                hd = s - 2
                b = hd % 2
                pe.wait_ge(at_exp, T * (hd + 1))
                if hd >= 2:
                    pe.wait_ge(at_ptc, hd - 1)
                for c in range(3):
                    last = nc.tensor.transpose(ps[2 + b][:, c * P:(c + 1) * P], prob[:, b, c * P:(c + 1) * P],
                                               ident[:, :])
                last.then_inc(at_pt, 1)
            if s >= 3:
                hd = s - 3
                b = hd % 2
                pe.wait_ge(at_ptc, hd + 1)
                if hd >= 2:
                    pe.wait_ge(at_on, T * (hd - 1))
                val = slice(hd * DH, (hd + 1) * DH)
                mm(ps[4 + b][:, 0:DH], prob_t[:, b, 0:P], v_nat[:, 0, val], True, True)
                mm(ps[4 + b][:, DH:2 * DH], prob_t[:, b, P:2 * P], v_nat[:, 0, val], True, False)
                mm(ps[4 + b][:, DH:2 * DH], prob_t[:, b, 2 * P:3 * P], v_nat[:, 1, val], False, True)\
                    .then_inc(at_o, 1)
        pe.wait_ge(at_on, T * H)
        for m in range(T):
            for q in range(2):
                turn(quarter(o_nat, m, q))
        turned()
        for k in range(4):
            rows_granule(G_FOUT + k, hth, htl, 2 * k, k, k == 0, k == 3)
        stream_turn()
        small(4, NE, wrh, wrl).then_inc(lg_full, 1)
        pe.wait_ge(mem_ready, 1)
        prefix(5, NE, member)
        mm(ps[5][:, T * NE:(T + 1) * NE], ones[:, :], member[:, 0, :], True, False)
        mm(ps[5][:, T * NE:(T + 1) * NE], ones[:, :], member[:, 1, :], False, True).then_inc(rank_full, 1)
        pe.wait_ge(route_ready, 1)
        pe.wait_ge(xl_ready, T)

        def experts(rnd_no):
            with pe.Fori(rnd_no * NE, (rnd_no + 1) * NE) as e:
                g0 = pe.snap(G_MOE + e * G_EXP)
                e1 = pe.snap(e + 1)
                pe.wait_ge(sel_ready, e1 * (T + 1))
                for m in range(T):
                    nc.tensor.transpose(ps[7][:, m * P:(m + 1) * P], sel[:, m, :].bitcast(F32), ident[:, :])
                for m in range(T):
                    last = mm(ps[7][:, S:S + 1], sel[:, m, :].bitcast(F32), wcur[:, m:m + 1], m == 0, m == T - 1)
                last.then_inc(st_full, 1)
                for q in range(2):
                    for c in range(4):
                        k = slice((4 * q + c) * P, (4 * q + c + 1) * P)
                        o = ps[4 + q][:, c * P:(c + 1) * P]
                        for m in range(T):
                            mm(o, xh[:, m, k], sel[:, m, :], m == 0, False)
                            last = mm(o, xl[:, m, k], sel[:, m, :], False, m == T - 1)
                    last.then_inc(gx_full, 1)
                for half in range(2):
                    for c in range(4):
                        mm(ps[2 + half][:, c * P:(c + 1) * P], zeros[:, :], zeros[:, :], c == 0, False)
                pe.wait_ge(gx_lo, e1 * 2)

                def gate_or_up(gv, gs, bank):
                    for half in range(2):
                        pe.wait_ge(s0["lo"], gv + (half + 1))
                        for c in range(4):
                            k = 4 * half + c
                            last = mm3(ps[bank][:, :], xeh[:, k, :], xel[:, k, :], (gs + half) % SPL, c, k == 0,
                                       k == KD - 1)
                        last.then_inc(s0["used"], 1)

                def hidden_turn(n):
                    pe.wait_ge(e_hid, n)
                    for c in range(4):
                        last = nc.tensor.transpose(ps[6][:, c * P:(c + 1) * P], hb[:, 0, c * P:(c + 1) * P],
                                                   ident[:, :])
                    last.then_inc(e_tp, 1)

                def expert_down(n, gv, gs, final):
                    pe.wait_ge(e_lo, n)
                    for i in range(2):
                        pe.wait_ge(s0["lo"], gv + (i + 1))
                        for kk in range(2):
                            for half in range(2):
                                last = mm3(ps[2 + half][:, :], bth[:, 2 * i + kk, 0:P], btl[:, 2 * i + kk, 0:P],
                                           (gs + i) % SPL, 2 * kk + half, False, final and i == 1 and kk == 1)
                        last.then_inc(s0["used"], 1)

                gate_or_up(g0, G_MOE, 0)
                gate_or_up(g0 + 2, G_MOE + 2, 1)
                with pe.Fori(1, NJ) as j:
                    gj = pe.snap(g0 + j * G_BLK)
                    ej = pe.snap(e * NJ + j)
                    pe.wait_ge(e_silu, ej)
                    gate_or_up(gj - 2, G_MOE - 2, 0)
                    hidden_turn(ej)
                    gate_or_up(gj, G_MOE, 1)
                    expert_down(ej, gj + 2, G_MOE + 2, False)
                hidden_turn(e1 * NJ)
                expert_down(e1 * NJ, g0 + (G_EXP - 2), G_MOE - 2, True)
                for i in range(2 * T):
                    half, m = i // 2, i % 2
                    if m == 0:
                        pe.wait_ge(ys_lo, e1 * 2 - (1 - half))
                        pe.wait_ge(st_copied, e1 * 2)
                    if i >= 2:
                        pe.wait_ge(sc_added, e * (2 * T) + (i - 1))
                    part = slice(half * W, (half + 1) * W)
                    tok = slice(m * P, (m + 1) * P)
                    mm(ps[4 + i % 2][:, :], sel_t[:, tok], ysh[:, part], True, False)
                    mm(ps[4 + i % 2][:, :], sel_t[:, tok], ysl[:, part], False, True).then_inc(sc_full, 1)

        experts(0)
        with pe.If(pe.value_load(cnt_i[0:1, 0:1], min_val=0, max_val=S) > P):
            experts(1)
        pe.wait_ge(moe_done, 1)
        n_h[0] = 0
        ple(1, 0, pn1)

    whole.close()


_INS = ["x", "p", "ln_g", "ln_b", "gm_w_in", "gm_b_in", "gm_ln_g", "gm_ln_b", "gm_w_s", "gm_b_s", "gm_w_out",
        "fox_w_in", "fox_b_f", "fox_w_out", "ffn_w_gate", "ffn_w_up", "ffn_w_down",
        "moe_w_router", "moe_w_gate", "moe_w_up", "moe_w_down", "ple_w_gate", "ple_b_gate", "ple_w_proj"]


def kernel(**inputs):
    import numpy as _np
    import concourse.bacc as _bacc
    from concourse import mybir as _mybir
    from concourse.bass_utils import run_bass_kernel_spmd as _run

    nc = _bacc.Bacc("TRN2", target_bir_lowering=False, num_devices=1)
    arrays, args = {}, []
    for name in _INS:
        a = _np.ascontiguousarray(inputs[name])
        arrays[f"in_{name}_dram"] = a
        args.append(nc.dram_tensor(f"in_{name}_dram", a.shape, _mybir.dt.from_np(a.dtype), kind="ExternalInput").ap())
    shape = _np.shape(inputs["x"])
    args.append(nc.dram_tensor("out_dram", shape, _mybir.dt.float32, kind="ExternalOutput").ap())
    build_trunk(nc, *args)
    r = _run(nc, [arrays], core_ids=[0])
    return r.results[0]["out_dram"]
```

```python
from contextlib import ExitStack

import concourse.bass as bass
from concourse import mybir

F32 = mybir.dt.float32
F32R = mybir.dt.float32r
BF16 = mybir.dt.bfloat16
I32 = mybir.dt.int32
ALU = mybir.AluOpType
ACT = mybir.ActivationFunctionType
AX = mybir.AxisListType.X

P = 128
W = 512
RAW = 6
SPL = 3
LN_EPS = 1e-5


def build_trunk(nc, x, p, ln_g, ln_b, gm_w_in, gm_b_in, gm_ln_g, gm_ln_b, gm_w_s, gm_b_s, gm_w_out,
                fox_w_in, fox_b_f, fox_w_out, ffn_w_gate, ffn_w_up, ffn_w_down,
                moe_w_router, moe_w_gate, moe_w_up, moe_w_down, ple_w_gate, ple_b_gate, ple_w_proj, out):
    _, S, D = x.shape
    DEPTH = p.shape[0]
    PD = p.shape[3]
    T = S // P
    KD = D // P
    GW = gm_w_out.shape[1]
    GG = gm_w_s.shape[1]
    GC = GW // GG
    H = fox_b_f.shape[1]
    DH = D // H
    FA = DH + 2
    F = ffn_w_down.shape[1]
    NE = moe_w_router.shape[2]
    NJ = F // W
    ALPHA = float((2 * DEPTH) ** 0.25)
    assert T == 2 and D == 2 * W and F % W == 0 and GW == 4 * W and GC * 2 == W and PD == 2 * P
    assert gm_w_s.shape[2] == P and S == 2 * P

    G_GIN = 0
    N_GIN = 2 * GW // W
    G_GOUT = G_GIN + 2 * N_GIN
    G_FFN = G_GOUT + GW // (2 * P)
    G_BLK = 6
    G_PLE = G_FFN + G_BLK * NJ
    G_FIN = G_PLE + 5
    N_FIN = 3 * D // W
    G_FOUT = G_FIN + 2 * N_FIN
    G_MOE = G_FOUT + D // (2 * P)
    G_EXP = G_BLK * NJ
    assert G_EXP % RAW == 0 and G_BLK % SPL == 0 and G_BLK == RAW

    GIN_ORDER = [*range(N_GIN // 2, N_GIN), *range(N_GIN // 2)]

    base = (nc.sbuf_base + 31) // 32 * 32
    cursor = [base]

    def at(name, shape, dt, offset=None):
        size = 4
        for n in shape[1:]:
            size *= n
        if offset is None:
            offset = cursor[0]
            cursor[0] += (size + 31) // 32 * 32
        return nc.alloc_sbuf_tensor_at(name, shape, dt, offset=offset), offset + (size + 31) // 32 * 32

    def keep(name, shape, dt=F32):
        return at(name, shape, dt)[0]

    raw = keep("raw", [P, RAW, 4, W])
    wh = keep("wh", [P, SPL, 4, W], F32R)
    wl = keep("wl", [P, SPL, 4, W], F32R)
    h = keep("h", [P, T, D])
    hth_at = cursor[0]
    hth = keep("hth", [P, KD, S], F32R)
    htl = keep("htl", [P, KD, S], F32R)
    xh, nxt = at("xh", [P, T, D], F32R, hth_at)
    xl, _ = at("xl", [P, T, D], F32R, nxt)
    par_b = keep("par_b", [P, 4, D])
    par_a = cursor[0]
    b_in, end_a = at("b_in", [P, 2 * GW], F32)
    ln0, _ = at("ln0", [P, 4, D], F32, par_a)
    o_nat, nxt = at("o_nat", [P, T, D], F32, par_a)
    pn1, nxt = at("pn1", [P, T, PD], F32, par_a)
    pp1, nxt = at("pp1", [P, T, D], F32, nxt)
    ysh, nxt = at("ysh", [P, D], F32R, nxt)
    assert nxt <= end_a
    ple_b = keep("ple_b", [P, DEPTH, D])

    ident = keep("ident", [P, P])
    upper = keep("upper", [P, P])
    ones = keep("ones", [P, P])
    zeros = keep("zeros", [P, P], F32R)
    iota_i = keep("iota_i", [P, P], I32)
    iota = keep("iota", [P, P])
    ident_b = keep("ident_b", [P, P], BF16)
    mask_f = keep("mask_f", [P, P])
    mask = keep("mask", [P, P], BF16)
    bs_t = keep("bs_t", [P, GG])
    bf_bc = keep("bf_bc", [P, H])
    wf = keep("wf", [P, KD, H])
    wfh = keep("wfh", [P, KD, H], F32R)
    wfl = keep("wfl", [P, KD, H], F32R)
    wr = keep("wr", [P, KD, NE])
    wrh = keep("wrh", [P, KD, NE], F32R)
    wrl = keep("wrl", [P, KD, NE], F32R)
    stats = keep("stats", [P, T, 4, 6])
    mv = keep("mv", [P, T, 2])
    var = keep("var", [P, T])
    std = keep("std", [P, T])
    rstd = keep("rstd", [P, T])
    nwt = keep("nwt", [P, T])
    z_f = keep("z_f", [P, T, H])
    a_f = keep("a_f", [P, T, H])
    lg = keep("lg", [P, T, NE])
    top8 = keep("top8", [P, T, 8])
    eqk = keep("eqk", [P, T, NE])
    key = keep("key", [P, T])
    sel1 = keep("sel1", [P, T, NE])
    sel2 = keep("sel2", [P, T, NE])
    prio = keep("prio", [P, NE])
    prio_i = keep("prio_i", [P, NE], I32)
    gap = keep("gap", [P, T])
    den = keep("den", [P, T])
    w_top = keep("w_top", [P, 2, T])
    member = keep("member", [P, T, NE])
    slots = keep("slots", [P, 2, T, NE + 1])
    comb = keep("comb", [P, T, NE + 1])
    cnt = keep("cnt", [P, 1])
    cnt_i = keep("cnt_i", [P, 1], I32)
    wcur = keep("wcur", [P, T])
    wslot = keep("wslot", [P, 1])

    ph = cursor[0]
    u, nxt = at("u", [P, T, GW], F32, ph)
    v, nxt = at("v", [P, T, GW], F32, nxt)
    ws_raw, _ = at("ws_raw", [P, GG, P], F32, ph)
    ws_t, end = at("ws_t", [P, GG, P], F32, nxt)
    acc, nxt = at("acc", [P, T, D], F32, ph)
    bth, nxt = at("bth", [P, 4, S], F32R, nxt)
    btl, nxt = at("btl", [P, 4, S], F32R, nxt)
    sg, nxt = at("sg", [P, T, W], F32, nxt)
    hb, nxt = at("hb", [P, T, W], F32, nxt)
    per_layer = nxt
    xeh, nxt = at("xeh", [P, KD, P], F32R, nxt)
    xel, nxt = at("xel", [P, KD, P], F32R, nxt)
    sel, nxt = at("sel", [P, T, P], F32R, nxt)
    sel_t, nxt = at("sel_t", [P, S], F32R, nxt)
    end = max(end, nxt)
    ysl, nxt = at("ysl", [P, D], F32R, nxt)
    end = max(end, nxt)
    pn0, nxt = at("pn0", [P, T, PD], F32, per_layer)
    pth, nxt = at("pth", [P, PD // P, S], F32R, nxt)
    ptl, nxt = at("ptl", [P, PD // P, S], F32R, nxt)
    pp0, nxt = at("pp0", [P, T, D], F32, nxt)
    end = max(end, nxt)
    sig = acc
    q_nat, nxt = at("q_nat", [P, T, H, FA], F32, ph)
    k_nat, nxt = at("k_nat", [P, T, H, FA], F32, nxt)
    v_nat, nxt = at("v_nat", [P, T, D], F32, nxt)
    qk_t, nxt = at("qk_t", [P, 2, 2 * S], F32, nxt)
    prob, nxt = at("prob", [P, 2, 3 * P], F32, nxt)
    prob_t, nxt = at("prob_t", [P, 2, 3 * P], F32, nxt)
    nmax = at("nmax", [P, 2, T], F32, nxt)[0]
    rsum = at("rsum", [P, 2, T], F32, nxt + 32)[0]
    rinv = at("rinv", [P, 2, T], F32, nxt + 64)[0]
    end = max(end, nxt + 96)
    assert end <= nc.sbuf_usable_end, (end, nc.sbuf_usable_end)

    ps = [nc.alloc_psum_tensor(f"ps{i}", [P, W], F32) for i in range(8)]

    def sem(name):
        return nc.alloc_semaphore(name)

    raw_landed = [sem(f"raw_landed{i}") for i in range(RAW)]
    raw_landed2 = [sem(f"raw_landed2_{i}") for i in range(5)]
    streams = [dict(hi=sem(f"hi_split{i}"), lo=sem(f"lo_split{i}"), used=sem(f"used{i}"),
                    tp=sem(f"tp_filled{i}"), tp_hi=sem(f"tp_hi{i}"), tp_lo=sem(f"tp_lo{i}"),
                    var=sem(f"ln_var{i}"), std=sem(f"ln_std{i}"), h=sem(f"h_ready{i}"),
                    projc=sem(f"proj_copied{i}"), 
                    gb=sem(f"gate_biased{i}"), gs=sem(f"gate_sigmoid{i}"))
               for i in range(2)]
    x_landed = [sem(f"x_landed{i}") for i in range(2 * T)]
    ws_landed = sem("ws_landed")
    b_in_landed = sem("b_in_landed")
    first_tile = sem("first_tile")
    gln_landed = sem("gln_landed")
    bs_landed = sem("bs_landed")
    ln0_landed = sem("ln0_landed")
    ln1_landed = sem("ln1_landed")
    pleb_landed = sem("pleb_landed")
    pn_landed = [sem("pn0_landed"), sem("pn1_landed")]
    wf_landed = sem("wf_landed")
    bf_landed = sem("bf_landed")
    wr_landed = sem("wr_landed")
    out_landed = sem("out_landed")
    const_step = sem("const_step")
    const_ready = sem("const_ready")
    ws_tp = sem("ws_tp")
    ws_copied = sem("ws_copied")
    ws_masked = sem("ws_masked")
    gm_biased = sem("gm_biased")
    gm_gelu = sem("gm_gelu")
    v_normed = sem("v_normed")
    sv_full = sem("sv_full")
    mixed = sem("mixed")
    acc_init = sem("acc_init")
    silu_done = sem("silu_done")
    hid_ready = sem("hid_ready")
    part_full = sem("part_full")
    part_added = sem("part_added")
    small_split = sem("small_split")
    f_full = sem("f_full")
    f_exp = sem("f_exp")
    f_abs = sem("f_abs")
    f_log = sem("f_log")
    f_logf = sem("f_logf")
    c_full = sem("c_full")
    qk_ready = sem("qk_ready")
    fin_copied = sem("fin_copied")
    at_qk = sem("at_qk")
    at_qkc = sem("at_qkc")
    at_log = sem("at_log")
    at_max = sem("at_max")
    at_exp = sem("at_exp")
    at_pt = sem("at_pt")
    at_ptc = sem("at_ptc")
    at_o = sem("at_o")
    at_on = sem("at_on")
    lg_full = sem("lg_full")
    gap_ready = sem("gap_ready")
    gap_exp = sem("gap_exp")
    mem_ready = sem("mem_ready")
    rank_full = sem("rank_full")
    route_ready = sem("route_ready")
    xh_ready = sem("xh_ready")
    xl_ready = sem("xl_ready")
    sel_ready = sem("sel_ready")
    st_full = sem("st_full")
    st_copied = sem("st_copied")
    gx_full = sem("gx_full")
    gx_hi = sem("gx_hi")
    gx_lo = sem("gx_lo")
    e_silu = sem("e_silu")
    e_hid = sem("e_hid")
    e_tp = sem("e_tp")
    e_hi = sem("e_hi")
    e_lo = sem("e_lo")
    ys_hi = sem("ys_hi")
    ys_lo = sem("ys_lo")
    sc_full = sem("sc_full")
    sc_added = sem("sc_added")
    null_ready = sem("null_ready")
    null_full = sem("null_full")
    null_cleared = sem("null_cleared")
    moe_done = sem("moe_done")
    dve_step = sem("dve_step")
    dve_step2 = sem("dve_step2")

    def cols(w, n0, half):
        return w[half * 4 * P:(half + 1) * 4 * P, bass.ds(n0, W)].rearrange("(c p) n -> p c n", p=P)

    def rows(w, k0):
        return w[bass.ds(k0, 2 * P), :].rearrange("(c p) n -> p c n", p=P)

    def flat(t):
        return t.rearrange("p (c t) n -> p c (t n)", c=2)

    def split_phase(g):
        return g % RAW, g % SPL, g // RAW + 1

    whole = ExitStack()
    block = whole.enter_context(nc.Block())

    @block.sync
    def _(sp):
        g = [0]

        def load(src, by_rows=False):
            n = g[0]
            g[0] += 1
            slot = n % RAW
            if n >= RAW:
                sp.wait_ge(streams[0]["lo"], n - RAW + 1)
            dst = flat(raw[:, slot]) if by_rows else raw[:, slot]
            sp.dma_start(dst, src).then_inc(raw_landed[slot], 16)

        for i, nb in enumerate(GIN_ORDER):
            for half in range(2):
                if i == 0:
                    for m in range(T):
                        part = slice(half * W, (half + 1) * W)
                        sp.dma_start(h[:, m, part], x[0, m * P:(m + 1) * P, part])\
                            .then_inc(x_landed[half * T + m], 16)
                load(cols(gm_w_in[0], nb * W, half))
        for k in range(GW // (2 * P)):
            load(rows(gm_w_out[0], k * 2 * P), True)

        def block_loads(first, g0, gate, up, down, j, skip=0):
            for n in range(skip, 4):
                wait_load(g0 + n, first + n, cols((gate, up)[n // 2], j * W, n % 2))

        def wait_load(gv, gs, src, by_rows=False):
            slot = gs % RAW
            sp.wait_ge(streams[0]["lo"], gv - RAW + 1)
            dst = flat(raw[:, slot]) if by_rows else raw[:, slot]
            sp.dma_start(dst, src).then_inc(raw_landed[slot], 16)

        def swiglu_loads(first, g0, gate, up, down, headed=False):
            block_loads(first, g0, gate, up, down, 0, 2 if headed else 0)
            with sp.Fori(1, NJ) as j:
                gj = sp.snap(g0 + 4 + (j - 1) * G_BLK)
                block_loads(first + 4, gj, gate, up, down, j)
                for k in range(2):
                    wait_load(gj + 4 + k, first + 8 + k, rows(down, (j - 1) * W + k * 2 * P), True)
            for k in range(2):
                wait_load(g0 + G_EXP - 2 + k, first + G_EXP - 2 + k, rows(down, (NJ - 1) * W + k * 2 * P), True)

        swiglu_loads(G_FFN, G_FFN, ffn_w_gate[0], ffn_w_up[0], ffn_w_down[0])
        g[0] = G_PLE
        load(rows(ple_w_proj[0], 0), True)
        for nb in range(2):
            for half in range(2):
                load(cols(ple_w_gate[0], nb * W, half))
        for nb in range(N_FIN):
            for half in range(2):
                load(cols(fox_w_in[0], nb * W, half))
        for k in range(D // (2 * P)):
            load(rows(fox_w_out[0], k * 2 * P), True)

        def of(w, ex):
            return w[0, bass.ds(ex, 1)].rearrange("a k n -> (a k) n")

        def expert_head(gv, ex):
            for half in range(2):
                wait_load(gv + half, G_MOE + half, cols(of(moe_w_gate, ex), 0, half))

        def experts(rnd):
            with sp.Fori(rnd * NE, (rnd + 1) * NE) as e:
                g0 = sp.snap(G_MOE + e * G_EXP)
                ex = sp.snap(e - rnd * NE)
                swiglu_loads(G_MOE, g0, of(moe_w_gate, ex), of(moe_w_up, ex), of(moe_w_down, ex), True)
                expert_head(g0 + G_EXP, sp.snap((ex + 1) % NE))

        expert_head(G_MOE, 0)
        experts(0)
        sp.wait_ge(route_ready, 1)
        with sp.If(sp.value_load(cnt_i[0:1, 0:1], min_val=0, max_val=S) > P):
            experts(1)
        sp.wait_ge(moe_done, 1)
        sp.dma_start(flat(raw[:, 0]), rows(ple_w_proj[1], 0)).then_inc(raw_landed2[0], 16)
        for n in range(4):
            sp.dma_start(raw[:, 1 + n], cols(ple_w_gate[1], n // 2 * W, n % 2)).then_inc(raw_landed2[1 + n], 16)
        for nb in range(2):
            for m in range(T):
                sp.wait_ge(streams[1]["h"], 2 * T + 1 + nb * T + m)
                sp.dma_start(out[0, m * P:(m + 1) * P, nb * W:(nb + 1) * W],
                             h[:, m, nb * W:(nb + 1) * W]).then_inc(out_landed, 16)
        sp.wait_ge(out_landed, 16 * 2 * T)

    @block.gpsimd
    def _(pool):
        step = [0]

        def seq(ins):
            step[0] += 1
            ins.then_inc(const_step, 1)
            pool.wait_ge(const_step, step[0])

        def bcast(dst, src, s):
            pool.dma_start(dst, src.partition_broadcast(P)).then_inc(s, 16)

        seq(pool.memset(ident[:, :], 0.0))
        seq(pool.affine_select(out=ident[:, :], in_=ident[:, :], compare_op=ALU.not_equal, fill=1.0, base=0,
                               pattern=[[-1, P]], channel_multiplier=1))
        pool.dma_start(ws_raw[:, :, :], gm_w_s[0].rearrange("g t s -> t g s")).then_inc(ws_landed, 16)
        bcast(b_in[:, :], gm_b_in[0], b_in_landed)
        seq(pool.memset(ones[:, :], 1.0))
        seq(pool.affine_select(out=upper[:, :], in_=ones[:, :], compare_op=ALU.is_ge, fill=0.0, base=0,
                               pattern=[[1, P]], channel_multiplier=-1))
        seq(pool.memset(zeros[:, :].bitcast(F32), 0.0))
        seq(pool.memset(mask_f[:, :], 0.0))
        seq(pool.affine_select(out=mask_f[:, :], in_=mask_f[:, :], compare_op=ALU.is_ge, fill=-1e30, base=0,
                               pattern=[[-1, P]], channel_multiplier=1))
        seq(pool.tensor_copy(mask[:, :], mask_f[:, :]))
        seq(pool.tensor_copy(ident_b[:, :], ident[:, :]))
        seq(pool.iota(iota_i[:, :], pattern=[[1, P]], base=0, channel_multiplier=0))
        seq(pool.tensor_copy(iota[:, :], iota_i[:, :]))
        seq(pool.iota(prio_i[:, :], pattern=[[-1, NE]], base=NE, channel_multiplier=0))
        pool.tensor_copy(prio[:, :], prio_i[:, :]).then_inc(const_ready, 1)
        for i, src in enumerate((gm_ln_g, gm_ln_b)):
            bcast(par_b[:, 2 * i:2 * i + 2, :].rearrange("p a d -> p (a d)"), src[0], gln_landed)
        pool.dma_start(bs_t[:, :], gm_b_s[0].rearrange("g t -> t g"),
                       allow_slow_non_contiguous=True).then_inc(bs_landed, 16)
        bcast(ple_b[:, :, :].rearrange("p a d -> p (a d)"), ple_b_gate.rearrange("a d -> (a d)"), pleb_landed)
        pool.dma_start(wf[:, :, :], fox_w_in[0, :, 3 * D:3 * D + H].rearrange("(c p) n -> p c n", p=P))\
            .then_inc(wf_landed, 16)
        bcast(bf_bc[:, :], fox_b_f[0], bf_landed)
        pool.dma_start(wr[:, :, :], moe_w_router[0].rearrange("(c p) n -> p c n", p=P)).then_inc(wr_landed, 16)
        pool.wait_ge(ws_copied, 2)
        pool.affine_select(out=ws_t[:, :, :], in_=ws_t[:, :, :], compare_op=ALU.is_ge, fill=0.0, base=0,
                           pattern=[[0, GG], [1, P]], channel_multiplier=-1).then_inc(ws_masked, 1)

        def norms(dst, layer, s):
            for n in range(2):
                bcast(dst[:, 2 * n, :], ln_g[layer, n], s)
                bcast(dst[:, 2 * n + 1, :], ln_b[layer, n], s)

        pool.wait_ge(gm_biased, 2 * N_GIN)
        norms(ln0, 0, ln0_landed)
        pool.wait_ge(mixed, 2 * T * 2)
        norms(par_b, 1, ln1_landed)
        pool.wait_ge(streams[0]["used"], G_FFN)
        pool.dma_start(pn0[:, :, :], p[0, 0].rearrange("(m p) n -> p m n", p=P)).then_inc(pn_landed[0], 16)
        pool.wait_ge(streams[0]["used"], G_MOE)
        pool.dma_start(pn1[:, :, :], p[1, 0].rearrange("(m p) n -> p m n", p=P)).then_inc(pn_landed[1], 16)

    @block.scalar
    def _(act):
        s0, s1 = streams

        def round_hi(g, st=s0, landed=None):
            slot, ss, n = split_phase(g)
            if landed is None:
                act.wait_ge(raw_landed[slot], 16 * n)
            else:
                act.wait_ge(landed[g], 16)
            if g >= SPL:
                act.wait_ge(st["used"], g - SPL + 1)
            nc.scalar.copy(wh[:, ss], raw[:, slot]).then_inc(st["hi"], 1)

        def round_at(gv, gs, rv):
            act.wait_ge(raw_landed[gs % RAW], rv * 16)
            act.wait_ge(s0["used"], gv - SPL + 1)
            nc.scalar.copy(wh[:, gs % SPL], raw[:, gs % RAW]).then_inc(s0["hi"], 1)

        nt = [0, 0]

        def tp_hi(dst, n=W, which=0):
            st = streams[which]
            act.wait_ge(st["tp"], nt[which] + 1)
            bank = ps[6 + nt[which] % 2]
            nc.scalar.copy(dst, bank[:, 0:n].rearrange("p (c t) -> p c t", t=P)).then_inc(st["tp_hi"], 1)
            nt[which] += 1

        def stream_t(dst, q, m):
            return dst[:, 4 * q:4 * q + 4, m * P:(m + 1) * P]

        def ln_sqrt(k, which=0):
            act.wait_ge(streams[which]["var"], k)
            nc.scalar.activation(std[:, :], var[:, :], ACT.Sqrt).then_inc(streams[which]["std"], 1)

        def stream_hi(which=0):
            for q in range(2):
                for m in range(T):
                    tp_hi(stream_t(hth, q, m), W, which)

        for q in range(2):
            for m in range(T):
                tp_hi(stream_t(hth, q, m))
            round_hi(q)
        for i in range(N_GIN):
            round_hi(2 * i + 2)
            round_hi(2 * i + 3)
            act.wait_ge(gm_biased, T * (i + 1))
            nb = GIN_ORDER[i] * W
            dst = u[:, :, nb:nb + W] if nb < GW else v[:, :, nb - GW:nb - GW + W]
            nc.scalar.activation(dst, dst, ACT.Gelu_apprx_tanh).then_inc(gm_gelu, 1)
            if i == 4:
                ln_sqrt(1)
        for q in range(5):
            if q < 4:
                for m in range(T):
                    tp_hi(stream_t(hth, q % 2, m))
            if q >= 1:
                round_hi(G_GOUT + 2 * q)
                round_hi(G_GOUT + 2 * q + 1)

        ln_sqrt(2)
        stream_hi()
        act.wait_ge(s0["h"], 2 * T)
        for m in range(T):
            nc.scalar.mul(acc[:, m, :], h[:, m, :], ALPHA).then_inc(acc_init, 1)
        g = G_FFN

        def silu(j):
            for m in range(T):
                nc.scalar.activation(sg[:, m, :], ps[m][:, :], ACT.Silu).then_inc(silu_done, 1)

        round_hi(g + 2)
        round_hi(g + 3)
        act.wait_ge(s0["used"], g + 2)
        silu(0)
        round_hi(g + 4)
        round_hi(g + 5)
        n_tp = nt[0]
        with act.Fori(1, NJ) as j:
            gj = act.snap(g + 4 + (j - 1) * G_BLK)
            rj = act.snap((g + 4) // RAW + j)

            def rnd(k):
                round_at(gj + k, g + 4 + k, rj + ((g + 4 + k) // RAW - (g + 4) // RAW))

            rnd(2)
            rnd(3)
            act.wait_ge(hid_ready, T * j)
            act.wait_ge(s0["used"], gj + 2)
            silu(j)
            for m in range(T):
                act.wait_ge(s0["tp"], j * T + (n_tp - T + m + 1))
                nc.scalar.copy(bth[:, :, m * P:(m + 1) * P],
                               ps[6 + m][:, :].rearrange("p (c t) -> p c t", t=P)).then_inc(s0["tp_hi"], 1)
            for k in range(4, 8):
                rnd(k)
        nt[0] += (NJ - 1) * T
        for m in range(T):
            tp_hi(bth[:, :, m * P:(m + 1) * P])

        def ple(which, g0, pp, landed=None):
            st = streams[which]
            for m in range(T):
                tp_hi(pth[:, :, m * P:(m + 1) * P], 2 * P, which)
            round_hi(g0, st, landed)
            round_hi(g0 + 1, st, landed)
            round_hi(g0 + 2, st, landed)
            for i in range(2 * T):
                act.wait_ge(st["used"], g0 + 1)
                nc.scalar.copy(pp[:, i // 2, i % 2 * W:(i % 2 + 1) * W], ps[i][:, :]).then_inc(st["projc"], 1)

        def ple_gate(which, g0, last, landed=None):
            st = streams[which]
            ln_sqrt(3 if which == 0 else 1, which)
            stream_hi(which)
            for nb in range(2):
                for k in range(2):
                    n = g0 + 3 + 2 * nb + k
                    if n < last:
                        round_hi(n, st, landed)
                for m in range(T):
                    act.wait_ge(st["gb"], nb * T + m + 1)
                    part = sig[:, m, nb * W:(nb + 1) * W]
                    nc.scalar.activation(part, part, ACT.Sigmoid).then_inc(st["gs"], 1)

        ple(0, G_PLE, pp0)
        ple_gate(0, G_PLE, G_PLE + 7)
        act.wait_ge(wf_landed, 16)
        nc.scalar.copy(wfh[:, :, :], wf[:, :, :]).then_inc(small_split, 1)
        act.wait_ge(wr_landed, 16)
        nc.scalar.copy(wrh[:, :, :], wr[:, :, :]).then_inc(small_split, 1)
        stream_hi()
        for i in range(N_FIN):
            round_hi(G_FIN + 2 * i + 2)
            round_hi(G_FIN + 2 * i + 3)
            act.wait_ge(s0["used"], G_FIN + 2 * i + 2)
            what, half = i // 2, i % 2
            for m in range(T):
                bank = ps[i % 2 * 2 + m]
                if what < 2:
                    dst = (q_nat, k_nat)[what][:, m, half * (H // 2):(half + 1) * (H // 2), 0:DH]
                    src = bank[:, :].rearrange("p (h d) -> p h d", d=DH)
                    ins = nc.scalar.mul(dst, src, DH ** -0.5) if what == 0 else nc.scalar.copy(dst, src)
                else:
                    ins = nc.scalar.copy(v_nat[:, m, half * W:(half + 1) * W], bank[:, :])
                ins.then_inc(fin_copied, 1)
            if i == 1:
                act.wait_ge(f_abs, 1)
                nc.scalar.activation(a_f[:, :, :], a_f[:, :, :], ACT.Exp, scale=-1.0).then_inc(f_exp, 1)
            if i == 2:
                act.wait_ge(f_abs, 2)
                nc.scalar.activation(a_f[:, :, :], a_f[:, :, :], ACT.Ln).then_inc(f_log, 1)
        for s in range(H + 1):
            if s < H:
                act.wait_ge(at_qk, s + 1)
                nc.scalar.copy(qk_t[0:FA, s % 2, :], ps[6 + s % 2][0:FA, :]).then_inc(at_qkc, 1)
            if s >= 1:
                hd = s - 1
                act.wait_ge(at_max, T * (hd + 1))
                if hd >= 2:
                    act.wait_ge(at_pt, hd - 1)
                for m, (a, b) in enumerate(((0, P), (P, 3 * P))):
                    nc.scalar.activation(prob[:, hd % 2, a:b], ps[hd % 2][:, a:b], ACT.Exp, bias=nmax[:, hd % 2, m:m + 1],
                                         accum_out=rsum[:, hd % 2, m:m + 1]).then_inc(at_exp, 1)
        stream_hi()
        round_hi(G_FOUT + 2)
        round_hi(G_FOUT + 3)
        round_hi(G_MOE)
        round_hi(G_MOE + 1)
        ln_sqrt(4)
        stream_hi()
        act.wait_ge(s0["h"], 2 * T * 4)
        for m in range(T):
            nc.scalar.mul(acc[:, m, :], h[:, m, :], ALPHA).then_inc(acc_init, 1)
        act.wait_ge(lg_full, 1)
        for m in range(T):
            nc.scalar.copy(xh[:, m, :], h[:, m, :]).then_inc(xh_ready, 1)
        act.wait_ge(gap_ready, 1)
        nc.scalar.activation(gap[:, :], gap[:, :], ACT.Exp).then_inc(gap_exp, 1)

        def scale_out():
            for half in range(2):
                nc.scalar.activation(ysh[:, half * W:(half + 1) * W], ps[2 + half][:, :], ACT.Copy,
                                     scale=wslot[:, 0:1]).then_inc(ys_hi, 1)

        def gathered(n):
            for q in range(2):
                act.wait_ge(gx_full, n * 2 - (1 - q))
                nc.scalar.copy(xeh[:, 4 * q:4 * q + 4, :],
                               ps[4 + q][:, :].rearrange("p (c t) -> p c t", t=P)).then_inc(gx_hi, 1)

        def experts(rnd_no):
            gathered(1 + rnd_no * (NE + 1))
            act.wait_ge(null_ready, rnd_no + 1)
            act.wait_ge(null_full, rnd_no + 1)
            with act.Fori(rnd_no * NE, (rnd_no + 1) * NE) as e:
                g0 = act.snap(G_MOE + e * G_EXP)
                r0 = act.snap(G_MOE // RAW + e * NJ)
                e1 = act.snap(e + 1)

                def rnd(k):
                    round_at(g0 + k, G_MOE + k, r0 + ((G_MOE + k) // RAW - G_MOE // RAW + 1))

                act.wait_ge(s0["used"], g0)
                scale_out()
                rnd(2)
                rnd(3)
                act.wait_ge(s0["used"], g0 + 2)
                nc.scalar.activation(sg[:, 0, :], ps[0][:, :], ACT.Silu).then_inc(e_silu, 1)
                rnd(4)
                rnd(5)
                act.wait_ge(st_full, e1)
                nc.scalar.copy(sel_t[:, :], ps[7][:, 0:S]).then_inc(st_copied, 1)
                nc.scalar.copy(wslot[:, :], ps[7][:, S:S + 1]).then_inc(st_copied, 1)
                with act.Fori(1, NJ) as j:
                    gj = act.snap(g0 + j * G_BLK)
                    rj = act.snap(r0 + j)
                    ej = act.snap(e * NJ + j)

                    def rnd_j(k):
                        k -= 2
                        round_at(gj + k, G_MOE + k, rj + ((G_MOE + k) // RAW - G_MOE // RAW + 1))

                    rnd_j(2)
                    rnd_j(3)
                    act.wait_ge(e_hid, ej)
                    act.wait_ge(s0["used"], gj)
                    nc.scalar.activation(sg[:, 0, :], ps[0][:, :], ACT.Silu).then_inc(e_silu, 1)
                    act.wait_ge(e_tp, ej)
                    nc.scalar.copy(bth[:, :, 0:P],
                                   ps[6][:, :].rearrange("p (c t) -> p c t", t=P)).then_inc(e_hi, 1)
                    for k in range(4, 8):
                        rnd_j(k)
                gathered(e + (rnd_no + 2))
                act.wait_ge(e_tp, e1 * NJ)
                nc.scalar.copy(bth[:, :, 0:P],
                               ps[6][:, :].rearrange("p (c t) -> p c t", t=P)).then_inc(e_hi, 1)
                rnd(G_EXP)
                rnd(G_EXP + 1)
            act.wait_ge(s0["used"], G_MOE + (rnd_no + 1) * NE * G_EXP)
            scale_out()

        experts(0)
        act.wait_ge(route_ready, 1)
        with act.If(act.value_load(cnt_i[0:1, 0:1], min_val=0, max_val=S) > P):
            experts(1)
        ple(1, 0, pp1, raw_landed2)
        ple_gate(1, 0, 5, raw_landed2)

    @block.vector
    def _(dve):
        s0, s1 = streams
        step = [0, 0]

        def seq(ins, which=0):
            s = (dve_step, dve_step2)[which]
            step[which] += 1
            ins.then_inc(s, 1)
            dve.wait_ge(s, step[which])

        def rest_lo(g, st=s0):
            slot, ss, _ = split_phase(g)
            dve.wait_ge(st["hi"], g + 1)
            nc.vector.tensor_tensor(wl[:, ss], raw[:, slot], wh[:, ss].bitcast(F32), ALU.subtract)\
                .then_inc(st["lo"], 1)

        def rest_at(gv, gs):
            dve.wait_ge(s0["hi"], gv + 1)
            nc.vector.tensor_tensor(wl[:, gs % SPL], raw[:, gs % RAW], wh[:, gs % SPL].bitcast(F32),
                                    ALU.subtract).then_inc(s0["lo"], 1)

        nt = [0, 0]

        def tp_lo(dst, hi, n=W, which=0):
            st = streams[which]
            dve.wait_ge(st["tp_hi"], nt[which] + 1)
            bank = ps[6 + nt[which] % 2]
            nc.vector.tensor_tensor(dst, bank[:, 0:n].rearrange("p (c t) -> p c t", t=P), hi.bitcast(F32),
                                    ALU.subtract).then_inc(st["tp_lo"], 1)
            nt[which] += 1

        def stream_t(dst, q, m):
            return dst[:, 4 * q:4 * q + 4, m * P:(m + 1) * P]

        def stream_lo(q, m, which=0):
            tp_lo(stream_t(htl, q, m), stream_t(hth, q, m), W, which)

        def ln_var(n_stats, which=0):
            for m in range(T):
                seq(nc.vector.bn_aggr(mv[:, m, :], stats[:, m, 0:n_stats, :].rearrange("p a b -> p (a b)")), which)
            nc.vector.tensor_scalar(var[:, :], mv[:, :, 1], LN_EPS, None, ALU.add)\
                .then_inc(streams[which]["var"], 1)

        def ln_rstd(k, which=0):
            dve.wait_ge(streams[which]["std"], k)
            seq(nc.vector.reciprocal(rstd[:, :], std[:, :]), which)
            seq(nc.vector.tensor_tensor(nwt[:, :], rstd[:, :], rstd[:, :], ALU.mult), which)
            seq(nc.vector.tensor_tensor(nwt[:, :], nwt[:, :], var[:, :], ALU.mult), which)
            seq(nc.vector.tensor_scalar(nwt[:, :], nwt[:, :], -0.5, 1.5, ALU.mult, ALU.add), which)
            seq(nc.vector.tensor_tensor(rstd[:, :], rstd[:, :], nwt[:, :], ALU.mult), which)

        def centre(t, m, part, gain, which=0):
            return nc.vector.scalar_tensor_tensor(out=t[:, m, part], in0=t[:, m, part], scalar=mv[:, m, 0:1],
                                                  in1=gain, op0=ALU.subtract, op1=ALU.mult)

        def scale_bias(dst, t, m, part, bias):
            return nc.vector.scalar_tensor_tensor(out=dst[:, m, part], in0=t[:, m, part],
                                                  scalar=rstd[:, m:m + 1], in1=bias, op0=ALU.mult, op1=ALU.add)

        def acc_stats(m, half, which=0):
            seq(nc.vector.bn_stats(stats[:, m, half, :], acc[:, m, half * W:(half + 1) * W]), which)

        def norm(k, par, n, which=0):
            ln_var(2, which)
            for half in range(2):
                for m in range(T):
                    part = slice(half * W, (half + 1) * W)
                    seq(centre(acc, m, part, par[:, 2 * n, part]), which)
            ln_rstd(k, which)

            def quarter_out(half, m):
                part = slice(half * W, (half + 1) * W)
                scale_bias(h, acc, m, part, par[:, 2 * n + 1, part]).then_inc(streams[which]["h"], 1)

            quarter_out(0, 0)
            quarter_out(0, 1)
            quarter_out(1, 0)
            stream_lo(0, 0, which)
            stream_lo(0, 1, which)
            quarter_out(1, 1)
            stream_lo(1, 0, which)
            stream_lo(1, 1, which)

        def residual(k, g_end):
            for m in range(T):
                if m == 0:
                    dve.wait_ge(first_tile, k)
                else:
                    dve.wait_ge(s0["used"], g_end)
                for half in range(2):
                    part = slice(half * W, (half + 1) * W)
                    seq(nc.vector.scalar_tensor_tensor(out=acc[:, m, part], in0=h[:, m, part], scalar=ALPHA,
                                                       in1=ps[2 * m + half][:, :], op0=ALU.mult, op1=ALU.add))
                for half in range(2):
                    acc_stats(m, half)

        for q in range(2):
            for m in range(T):
                stream_lo(q, m)
            rest_lo(q)
        for i in range(2):
            dve.wait_ge(ws_tp, i + 1)
            nc.vector.tensor_copy(ws_t[:, 4 * i:4 * i + 4, :],
                                  ps[4 + i][:, :].rearrange("p (g t) -> p g t", t=P)).then_inc(ws_copied, 1)
        dve.wait_ge(b_in_landed, 16)

        def v_stats(i):
            dve.wait_ge(gm_gelu, i + 1)
            for m in range(T):
                seq(nc.vector.bn_stats(stats[:, m, i, :], v[:, m, i * W:(i + 1) * W]))

        for i in range(N_GIN):
            rest_lo(2 * i + 2)
            rest_lo(2 * i + 3)
            dve.wait_ge(s0["used"], 2 * i + 2)
            nb = GIN_ORDER[i] * W
            for m in range(T):
                dst = u[:, m, nb:nb + W] if nb < GW else v[:, m, nb - GW:nb - GW + W]
                nc.vector.tensor_tensor(dst, ps[i % 2 * 2 + m][:, :], b_in[:, nb:nb + W], ALU.add)\
                    .then_inc(gm_biased, 1)
            if 1 <= i <= 4:
                v_stats(i - 1)
            if i == 4:
                ln_var(4)
                dve.wait_ge(gln_landed, 32)
            if i in (4, 5):
                m = i - 4
                for q in range(2):
                    part = slice(q * D, (q + 1) * D)
                    seq(centre(v, m, part, par_b[:, q, :]))
            if i == 5:
                ln_rstd(1)
            if i in (6, 7):
                m = i - 6
                for q in range(2):
                    part = slice(q * D, (q + 1) * D)
                    scale_bias(v, v, m, part, par_b[:, 2 + q, :]).then_inc(v_normed, 1)
        dve.wait_ge(gm_gelu, N_GIN)
        dve.wait_ge(bs_landed, 16)

        def mix(q):
            for m in range(T):
                dve.wait_ge(sv_full, q * T + m + 1)
                for k in range(2):
                    grp = 2 * q + k
                    part = u[:, m, grp * GC:(grp + 1) * GC]
                    nc.vector.scalar_tensor_tensor(out=part, in0=ps[4 + m][:, k * GC:(k + 1) * GC],
                                                   scalar=bs_t[:, grp:grp + 1], in1=part, op0=ALU.add,
                                                   op1=ALU.mult).then_inc(mixed, 1)

        def u_lo(q):
            for m in range(T):
                stream_lo(q % 2, m)

        mix(0)
        mix(1)
        u_lo(0)
        for q in range(1, 4):
            if q >= 2:
                rest_lo(G_GOUT + 2 * q - 2)
                rest_lo(G_GOUT + 2 * q - 1)
            if q < 3:
                mix(q + 1)
            u_lo(q)
        rest_lo(G_GOUT + 6)
        rest_lo(G_GOUT + 7)
        rest_lo(G_FFN)
        residual(1, G_FFN)
        dve.wait_ge(ln0_landed, 64)
        norm(2, ln0, 0)
        rest_lo(G_FFN + 1)
        g = G_FFN

        def hid(j):
            for m in range(T):
                nc.vector.tensor_tensor(hb[:, m, :], ps[2 + m][:, :], sg[:, m, :], ALU.mult)\
                    .then_inc(hid_ready, 1)

        def parts(n0, gv, last=False):
            for i in range(2 * T):
                m, half = i // 2, i % 2
                part = acc[:, m, half * W:(half + 1) * W]
                if i < 2 * T - 1:
                    dve.wait_ge(part_full, n0 + (i + 1))
                else:
                    dve.wait_ge(s0["used"], gv + 2)
                nc.vector.tensor_tensor(part, part, ps[4 + i % 2][:, :], ALU.add).then_inc(part_added, 1)
                if last:
                    dve.wait_ge(part_added, (NJ - 1) * 2 * T + i + 1)
                    acc_stats(m, half)

        rest_lo(g + 2)
        rest_lo(g + 3)
        rest_lo(g + 4)
        rest_lo(g + 5)
        dve.wait_ge(acc_init, T)
        dve.wait_ge(silu_done, T)
        dve.wait_ge(s0["used"], g + 4)
        hid(0)
        n_tp = nt[0]
        with dve.Fori(1, NJ) as j:
            gj = dve.snap(g + 4 + (j - 1) * G_BLK)
            rest_at(gj + 2, g + 6)
            rest_at(gj + 3, g + 7)
            for m in range(T):
                dve.wait_ge(s0["tp_hi"], j * T + (n_tp - T + m + 1))
                nc.vector.tensor_tensor(btl[:, :, m * P:(m + 1) * P],
                                        ps[6 + m][:, :].rearrange("p (c t) -> p c t", t=P),
                                        bth[:, :, m * P:(m + 1) * P].bitcast(F32), ALU.subtract)\
                    .then_inc(s0["tp_lo"], 1)
            rest_at(gj + 4, g + 8)
            rest_at(gj + 5, g + 9)
            dve.wait_ge(silu_done, j * T + T)
            dve.wait_ge(s0["used"], gj + 4)
            hid(j)
            rest_at(gj + 6, g + 10)
            parts((j - 1) * (2 * T - 1), gj + 4)
            rest_at(gj + 7, g + 11)
        nt[0] += (NJ - 1) * T
        for m in range(T):
            tp_lo(btl[:, :, m * P:(m + 1) * P], bth[:, :, m * P:(m + 1) * P])
        parts((NJ - 1) * (2 * T - 1), g + G_EXP - 2, True)

        def ple(which, g0, k, par, pp, last):
            st = streams[which]
            for m in range(T):
                tp_lo(ptl[:, :, m * P:(m + 1) * P], pth[:, :, m * P:(m + 1) * P], 2 * P, which)
            for i in range(3):
                rest_lo(g0 + i, st)
            if which == 1:
                for m in range(T):
                    for half in range(2):
                        acc_stats(m, half, 1)
            norm(k, par, 1, which)
            for nb in range(2):
                for i in range(2):
                    n = g0 + 3 + 2 * nb + i
                    if n < last:
                        rest_lo(n, st)
                part = slice(nb * W, (nb + 1) * W)
                dve.wait_ge(st["used"], g0 + 3 + 2 * nb)
                for m in range(T):
                    nc.vector.tensor_tensor(sig[:, m, part], ps[2 * nb + m][:, :], ple_b[:, which, part],
                                            ALU.add).then_inc(st["gb"], 1)
                for m in range(T):
                    dve.wait_ge(st["gs"], nb * T + m + 1)
                    seq(nc.vector.tensor_tensor(sig[:, m, part], sig[:, m, part], pp[:, m, part], ALU.mult), which)
                    nc.vector.tensor_tensor(h[:, m, part], h[:, m, part], sig[:, m, part], ALU.add)\
                        .then_inc(st["h"], 1)

        dve.wait_ge(pleb_landed, 16)
        ple(0, G_PLE, 3, ln0, pp0, G_PLE + 7)
        dve.wait_ge(small_split, 1)
        nc.vector.tensor_tensor(wfl[:, :, :], wf[:, :, :], wfh[:, :, :].bitcast(F32), ALU.subtract)\
            .then_inc(small_split, 1)
        dve.wait_ge(small_split, 3)
        nc.vector.tensor_tensor(wrl[:, :, :], wr[:, :, :], wrh[:, :, :].bitcast(F32), ALU.subtract)\
            .then_inc(small_split, 1)
        for nb in range(2):
            for m in range(T):
                stream_lo(nb, m)
        for i in range(N_FIN):
            rest_lo(G_FIN + 2 * i + 2)
            rest_lo(G_FIN + 2 * i + 3)
            if i == 1:
                dve.wait_ge(f_full, 1)
                dve.wait_ge(bf_landed, 16)
                for m in range(T):
                    seq(nc.vector.tensor_tensor(z_f[:, m, :], ps[4][:, m * H:(m + 1) * H], bf_bc[:, :], ALU.add))
                nc.vector.scalar_tensor_tensor(out=a_f[:, :, :], in0=z_f[:, :, :], scalar=-1.0, in1=z_f[:, :, :],
                                               op0=ALU.mult, op1=ALU.max).then_inc(f_abs, 1)
                dve.wait_ge(f_abs, 1)
                seq(nc.vector.tensor_scalar(z_f[:, :, :], z_f[:, :, :], 0.0, None, ALU.min))
                dve.wait_ge(f_exp, 1)
                nc.vector.tensor_scalar(a_f[:, :, :], a_f[:, :, :], 1.0, None, ALU.add).then_inc(f_abs, 1)
            if i == 3:
                dve.wait_ge(f_log, 1)
                nc.vector.tensor_tensor(z_f[:, :, :], z_f[:, :, :], a_f[:, :, :], ALU.subtract)\
                    .then_inc(f_logf, 1)
        dve.wait_ge(c_full, 1)
        for m in range(T):
            c = ps[5][:, m * H:(m + 1) * H]
            nc.vector.memset(q_nat[:, m, :, DH], 1.0).then_inc(qk_ready, 1)
            nc.vector.tensor_copy(q_nat[:, m, :, DH + 1], c).then_inc(qk_ready, 1)
            nc.vector.tensor_scalar(k_nat[:, m, :, DH], c, -1.0, None, ALU.mult).then_inc(qk_ready, 1)
            nc.vector.memset(k_nat[:, m, :, DH + 1], 1.0).then_inc(qk_ready, 1)
        for s in range(1, H + 3):
            if s <= H:
                hd = s - 1
                dve.wait_ge(at_log, hd + 1)
                for m, (a, b) in enumerate(((0, P), (P, 3 * P))):
                    nc.vector.tensor_reduce(nmax[:, hd % 2, m:m + 1], ps[hd % 2][:, a:b], AX, ALU.max,
                                            negate=True).then_inc(at_max, 1)
            if 0 <= s - 2 < H:
                hd = s - 2
                dve.wait_ge(at_pt, hd + 1)
                if hd >= 2:
                    dve.wait_ge(at_o, hd - 1)
                nc.vector.tensor_copy(prob_t[:, hd % 2, :], ps[2 + hd % 2][:, 0:3 * P]).then_inc(at_ptc, 1)
                if hd >= 2:
                    dve.wait_ge(at_on, hd - 1)
                seq(nc.vector.reciprocal(rinv[:, hd % 2, :], rsum[:, hd % 2, :]))
            if s >= 3:
                hd = s - 3
                dve.wait_ge(at_o, hd + 1)
                nc.vector.tensor_tensor(o_nat[:, :, hd * DH:(hd + 1) * DH],
                                        ps[4 + hd % 2][:, 0:T * DH].rearrange("p (m d) -> p m d", d=DH),
                                        rinv[:, hd % 2, :].rearrange("p (m a) -> p m a", a=1)
                                        .broadcast_to([P, T, DH]), ALU.mult).then_inc(at_on, 1)
        for q in range(2):
            for m in range(T):
                stream_lo(q, m)
        rest_lo(G_FOUT + 2)
        rest_lo(G_FOUT + 3)
        rest_lo(G_MOE)
        residual(2, G_MOE)
        dve.wait_ge(ln1_landed, 64)
        norm(4, par_b, 0)
        rest_lo(G_MOE + 1)
        dve.wait_ge(lg_full, 1)
        dve.wait_ge(const_ready, 1)
        seq(nc.vector.tensor_copy(lg[:, :, :], ps[4][:, 0:T * NE].rearrange("p (m e) -> p m e", e=NE)))
        for m in range(T):
            seq(nc.vector.max(top8[:, m, :], lg[:, m, :]))
        nc.vector.tensor_tensor(gap[:, :], top8[:, :, 1], top8[:, :, 0], ALU.subtract).then_inc(gap_ready, 1)

        def wide(t):
            return t.rearrange("p (m a) -> p m a", a=1).broadcast_to([P, T, NE])

        prios = prio[:, :].rearrange("p (a e) -> p a e", a=1).broadcast_to([P, T, NE])

        def first(dst, rank, but=None):
            seq(nc.vector.tensor_tensor(eqk[:, :, :], lg[:, :, :], wide(top8[:, :, rank]), ALU.is_equal))
            if but is not None:
                seq(nc.vector.tensor_tensor(eqk[:, :, :], eqk[:, :, :], but, ALU.is_gt))
            seq(nc.vector.tensor_tensor(eqk[:, :, :], eqk[:, :, :], prios, ALU.mult))
            seq(nc.vector.tensor_reduce(key[:, :], eqk[:, :, :], AX, ALU.max))
            seq(nc.vector.tensor_tensor(dst, prios, wide(key[:, :]), ALU.is_equal))

        first(sel1[:, :, :], 0)
        first(sel2[:, :, :], 1, sel1[:, :, :])
        nc.vector.tensor_tensor(member[:, :, :], sel1[:, :, :], sel2[:, :, :], ALU.add).then_inc(mem_ready, 1)
        dve.wait_ge(gap_exp, 1)
        seq(nc.vector.tensor_scalar(den[:, :], gap[:, :], 1.0, None, ALU.add))
        seq(nc.vector.reciprocal(w_top[:, 0, :], den[:, :]))
        seq(nc.vector.tensor_tensor(w_top[:, 1, :], w_top[:, 0, :], gap[:, :], ALU.mult))
        for m in range(T):
            seq(nc.vector.tensor_scalar(comb[:, m, 0:NE], sel1[:, m, :], w_top[:, 0, m:m + 1], None, ALU.mult))
            seq(nc.vector.scalar_tensor_tensor(out=comb[:, m, 0:NE], in0=sel2[:, m, :], scalar=w_top[:, 1, m:m + 1],
                                               in1=comb[:, m, 0:NE], op0=ALU.mult, op1=ALU.add))
        dve.wait_ge(rank_full, 1)
        ranks = ps[5][:, 0:T * NE].rearrange("p (m e) -> p m e", e=NE)
        seq(nc.vector.memset(comb[:, :, NE:NE + 1], 0.0))
        seq(nc.vector.memset(slots[:, 0, :, NE:NE + 1], -1.0))
        seq(nc.vector.tensor_tensor(slots[:, 0, :, 0:NE], member[:, :, :], ranks, ALU.mult))
        seq(nc.vector.tensor_scalar(slots[:, 0, :, 0:NE], slots[:, 0, :, 0:NE], -1.0, None, ALU.add))
        seq(nc.vector.tensor_scalar(slots[:, 1, :, :], slots[:, 0, :, :], float(-P), None, ALU.add))
        seq(nc.vector.tensor_reduce(cnt[:, :], ps[5][:, T * NE:(T + 1) * NE], AX, ALU.max))
        nc.vector.tensor_copy(cnt_i[:, :], cnt[:, :]).then_inc(route_ready, 1)
        for m in range(T):
            dve.wait_ge(xh_ready, m + 1)
            nc.vector.tensor_tensor(xl[:, m, :], h[:, m, :], xh[:, m, :].bitcast(F32), ALU.subtract)\
                .then_inc(xl_ready, 1)
        dve.wait_ge(acc_init, 2 * T)

        def select(rnd_no, ex):
            for m in range(T):
                nc.vector.tensor_scalar(sel[:, m, :], iota[:, :], slots[:, rnd_no, m, ex], None,
                                        ALU.is_equal).then_inc(sel_ready, 1)

        def weights(ex):
            nc.vector.tensor_copy(wcur[:, :], comb[:, :, ex].rearrange("p m a -> p (m a)")).then_inc(sel_ready, 1)

        def gathered(n):
            for q in range(2):
                dve.wait_ge(gx_hi, n * 2 - (1 - q))
                part = slice(4 * q, 4 * q + 4)
                nc.vector.tensor_tensor(xel[:, part, :], ps[4 + q][:, :].rearrange("p (c t) -> p c t", t=P),
                                        xeh[:, part, :].bitcast(F32), ALU.subtract).then_inc(gx_lo, 1)

        def scale_out(n):
            for half in range(2):
                dve.wait_ge(ys_hi, n * 2 - (1 - half))
                part = slice(half * W, (half + 1) * W)
                nc.vector.scalar_tensor_tensor(out=ysl[:, part], in0=ps[2 + half][:, :], scalar=wslot[:, 0:1],
                                               in1=ysh[:, part].bitcast(F32), op0=ALU.mult,
                                               op1=ALU.subtract).then_inc(ys_lo, 1)

        def add_scattered(n):
            for i in range(2 * T):
                half, m = i // 2, i % 2
                dve.wait_ge(sc_full, n * (2 * T) - (2 * T - 1 - i))
                part = acc[:, m, half * W:(half + 1) * W]
                nc.vector.tensor_tensor(part, part, ps[4 + i % 2][:, :], ALU.add).then_inc(sc_added, 1)

        def experts(rnd_no):
            select(rnd_no, slice(0, 1))
            weights(slice(0, 1))
            nc.vector.memset(sel_t[:, :].bitcast(F32), 0.0).then_inc(null_cleared, 1)
            dve.wait_ge(null_cleared, 2 * rnd_no + 1)
            nc.vector.memset(wslot[:, :], 0.0).then_inc(null_cleared, 1)
            dve.wait_ge(null_cleared, 2 * rnd_no + 2)
            nc.vector.memset(nwt[:, :], 0.0).then_inc(null_ready, 1)
            gathered(1 + rnd_no * (NE + 1))
            with dve.Fori(rnd_no * NE, (rnd_no + 1) * NE) as e:
                g0 = dve.snap(G_MOE + e * G_EXP)
                e1 = dve.snap(e + 1)
                en = dve.snap(e + (rnd_no + 1))
                nxt_ex = dve.snap(e + (1 - rnd_no * NE))
                scale_out(en)
                rest_at(g0 + 2, G_MOE + 2)
                rest_at(g0 + 3, G_MOE + 3)
                add_scattered(en)
                rest_at(g0 + 4, G_MOE + 4)
                rest_at(g0 + 5, G_MOE + 5)

                def hidden(n, gv):
                    dve.wait_ge(e_silu, n)
                    dve.wait_ge(s0["used"], gv)
                    nc.vector.tensor_tensor(hb[:, 0, :], ps[1][:, :], sg[:, 0, :], ALU.mult).then_inc(e_hid, 1)

                def hidden_lo(n):
                    dve.wait_ge(e_hi, n)
                    nc.vector.tensor_tensor(btl[:, :, 0:P], ps[6][:, :].rearrange("p (c t) -> p c t", t=P),
                                            bth[:, :, 0:P].bitcast(F32), ALU.subtract).then_inc(e_lo, 1)

                hidden(e * NJ + 1, g0 + 4)
                dve.wait_ge(st_full, e1)
                select(rnd_no, bass.ds(nxt_ex, 1))
                weights(bass.ds(nxt_ex, 1))
                with dve.Fori(1, NJ) as j:
                    gj = dve.snap(g0 + j * G_BLK)
                    ej = dve.snap(e * NJ + j)
                    rest_at(gj, G_MOE)
                    rest_at(gj + 1, G_MOE + 1)
                    hidden_lo(ej)
                    rest_at(gj + 2, G_MOE + 2)
                    rest_at(gj + 3, G_MOE + 3)
                    hidden(ej + 1, gj + 2)
                    rest_at(gj + 4, G_MOE + 4)
                    rest_at(gj + 5, G_MOE + 5)
                gathered(e + (rnd_no + 2))
                hidden_lo(e1 * NJ)
                rest_at(g0 + G_EXP, G_MOE)
                rest_at(g0 + (G_EXP + 1), G_MOE + 1)
            n = (rnd_no + 1) * (NE + 1)
            scale_out(n)
            add_scattered(n)
            dve.wait_ge(sc_added, n * (2 * T))

        experts(0)
        dve.wait_ge(route_ready, 1)
        with dve.If(dve.value_load(cnt_i[0:1, 0:1], min_val=0, max_val=S) > P):
            experts(1)
        nc.vector.memset(nwt[:, :], 0.0).then_inc(moe_done, 1)
        ple(1, 0, 1, par_b, pp1, 5)

    @block.tensor
    def _(pe):
        s0, s1 = streams

        def mm(o, a, b, start, stop):
            return nc.tensor.matmul(o, a, b, start=start, stop=stop)

        def mm3(o, ah, al, slot, c, start, stop):
            mm(o, ah, wh[:, slot, c], start, False)
            mm(o, ah, wl[:, slot, c], False, False)
            return mm(o, al, wh[:, slot, c], False, stop)

        nt = [0, 0]

        def turn(srcs, which=0):
            st = streams[which]
            n = nt[which]
            if n >= 2:
                pe.wait_ge(st["tp_lo"], n - 1)
            for c, src in enumerate(srcs):
                last = nc.tensor.transpose(ps[6 + n % 2][:, c * P:(c + 1) * P], src, ident[:, :])
            last.then_inc(st["tp"], 1)
            nt[which] += 1

        def turned(which=0):
            pe.wait_ge(streams[which]["tp_lo"], nt[which])

        def quarter(t, m, q):
            return [t[:, m, (4 * q + c) * P:(4 * q + c + 1) * P] for c in range(4)]

        def cols_granules(g, banks, st=s0, g_of=None, fresh=None):
            for half in range(2):
                if fresh is not None:
                    pe.wait_ge(st["tp_lo"], fresh + T * (half + 1))
                pe.wait_ge(st["lo"], g + half + 1)
                for c in range(4):
                    k = 4 * half + c
                    for m in range(T):
                        tok = slice(m * P, (m + 1) * P)
                        last = mm3(ps[banks[m]][:, :], hth[:, k, tok], htl[:, k, tok],
                                   (g_of if g_of is not None else g) % SPL if half == 0 else
                                   ((g_of if g_of is not None else g) + 1) % SPL, c, k == 0, k == KD - 1)
                last.then_inc(st["used"], 1)

        def rows_granule(g, ah, al, k0, first, final, st=s0):
            pe.wait_ge(st["lo"], g + 1)
            for kk in range(2):
                for m in range(T):
                    tok = slice(m * P, (m + 1) * P)
                    for half in range(2):
                        last = mm3(ps[2 * m + half][:, :], ah[:, k0 + kk, tok], al[:, k0 + kk, tok], g % SPL,
                                   2 * kk + half, first and kk == 0, final and kk == 1)
            last.then_inc(st["used"], 1)

        def rows_last(g, ah, al, k0):
            pe.wait_ge(s0["lo"], g + 2)
            for m in range(T):
                tok = slice(m * P, (m + 1) * P)
                for half in range(2):
                    for kk in range(4):
                        last = mm3(ps[2 * m + half][:, :], ah[:, k0 + kk, tok], al[:, k0 + kk, tok],
                                   (g + kk // 2) % SPL, 2 * (kk % 2) + half, False, kk == 3)
                if m == 0:
                    last.then_inc(first_tile, 1)
            last.then_inc(s0["used"], 2)

        pe.wait_ge(const_step, 2)
        for q in range(2):
            for m in range(T):
                pe.wait_ge(x_landed[q * T + m], 16)
                turn(quarter(h, m, q))
        pe.wait_ge(ws_landed, 16)
        for i in range(2):
            for c in range(4):
                last = nc.tensor.transpose(ps[4 + i][:, c * P:(c + 1) * P], ws_raw[:, 4 * i + c, :], ident[:, :])
            last.then_inc(ws_tp, 1)
        for i in range(N_GIN):
            if i >= 2:
                pe.wait_ge(gm_biased, T * (i - 1))
            cols_granules(2 * i, [i % 2 * 2, i % 2 * 2 + 1], fresh=0 if i == 0 else None)
        pe.wait_ge(v_normed, 2 * T)
        pe.wait_ge(ws_masked, 1)

        def u_turn(q):
            for m in range(T):
                pe.wait_ge(mixed, (q * T + m + 1) * 2)
                turn(quarter(u, m, q))

        def u_product(q):
            pe.wait_ge(s0["tp_lo"], n_u + T * (q + 1))
            if q == 3:
                rows_last(G_GOUT + 6, hth, htl, 4)
                return
            for k in range(2):
                rows_granule(G_GOUT + 2 * q + k, hth, htl, 4 * (q % 2) + 2 * k, q == 0 and k == 0, False)

        def spatial(q):
            for m in range(T):
                if q >= 1:
                    pe.wait_ge(mixed, ((q - 1) * T + m + 1) * 2)
                for k in range(2):
                    grp = 2 * q + k
                    last = mm(ps[4 + m][:, k * GC:(k + 1) * GC], ws_t[:, grp, :], v[:, m, grp * GC:(grp + 1) * GC],
                              True, True)
                last.then_inc(sv_full, 1)

        n_u = nt[0]
        spatial(0)
        pe.wait_ge(gm_biased, T * N_GIN)
        for q in range(4):
            if q < 3:
                spatial(q + 1)
            u_turn(q)
            if q >= 1:
                u_product(q - 1)
        u_product(3)

        n_h = [0]

        def stream_turn(which=0):
            for q in range(2):
                for m in range(T):
                    n_h[0] += 1
                    pe.wait_ge(streams[which]["h"], n_h[0])
                    turn(quarter(h, m, q), which)

        stream_turn()

        g = G_FFN

        def down(gv, gs, n0):
            pe.wait_ge(s0["lo"], gv + 2)
            for i in range(2 * T):
                m, half = i // 2, i % 2
                if i >= 2:
                    pe.wait_ge(part_added, n0 + (i - 1))
                for kk in range(4):
                    tok = slice(m * P, (m + 1) * P)
                    last = mm3(ps[4 + i % 2][:, :], bth[:, kk, tok], btl[:, kk, tok], (gs + kk // 2) % SPL,
                               2 * (kk % 2) + half, kk == 0, kk == 3)
                if i < 2 * T - 1:
                    last.then_inc(part_full, 1)
                else:
                    last.then_inc(s0["used"], 2)

        cols_granules(g, [0, 1], fresh=nt[0] - 2 * T)
        cols_granules(g + 2, [2, 3])
        n_tp = nt[0]
        with pe.Fori(1, NJ) as j:
            gj = pe.snap(g + 4 + (j - 1) * G_BLK)
            pe.wait_ge(silu_done, j * T)
            cols_granules(gj, [0, 1], g_of=g + 4)
            for m in range(T):
                pe.wait_ge(hid_ready, (j - 1) * T + (m + 1))
                for c in range(4):
                    last = nc.tensor.transpose(ps[6 + m][:, c * P:(c + 1) * P], hb[:, m, c * P:(c + 1) * P],
                                               ident[:, :])
                last.then_inc(s0["tp"], 1)
            cols_granules(gj + 2, [2, 3], g_of=g + 6)
            pe.wait_ge(s0["tp_lo"], j * T + n_tp)
            down(gj + 4, g + 8, (j - 1) * (2 * T))
        nt[0] += (NJ - 1) * T
        assert nt[0] % 2 == 0
        pe.wait_ge(hid_ready, NJ * T)
        for m in range(T):
            turn([hb[:, m, c * P:(c + 1) * P] for c in range(4)])
        turned()
        down(g + G_EXP - 2, g + G_EXP - 2, (NJ - 1) * 2 * T)

        def ple(which, g0, pn):
            st = streams[which]
            pe.wait_ge(pn_landed[which], 16)
            for m in range(T):
                turn([pn[:, m, c * P:(c + 1) * P] for c in range(2)], which)
            turned(which)
            rows_granule(g0, pth, ptl, 0, True, True, st)
            stream_turn(which)
            pe.wait_ge(st["projc"], 2 * T)
            for nb in range(2):
                cols_granules(g0 + 1 + 2 * nb, [2 * nb, 2 * nb + 1], st, None, nt[which] - 2 * T)

        ple(0, G_PLE, pn0)
        stream_turn()

        def small(bank, n, wsh, wsl):
            for m in range(T):
                tok = slice(m * P, (m + 1) * P)
                o = ps[bank][:, m * n:(m + 1) * n]
                for k in range(KD):
                    mm(o, hth[:, k, tok], wsh[:, k, :], k == 0, False)
                    mm(o, hth[:, k, tok], wsl[:, k, :], False, False)
                    last = mm(o, htl[:, k, tok], wsh[:, k, :], False, k == KD - 1)
            return last

        def prefix(bank, n, src):
            mm(ps[bank][:, 0:n], upper[:, :], src[:, 0, :], True, True)
            mm(ps[bank][:, n:2 * n], upper[:, :], src[:, 1, :], True, False)
            return mm(ps[bank][:, n:2 * n], ones[:, :], src[:, 0, :], False, True)

        for i in range(N_FIN):
            if i >= 2:
                pe.wait_ge(fin_copied, T * (i - 1))
            cols_granules(G_FIN + 2 * i, [i % 2 * 2, i % 2 * 2 + 1], fresh=nt[0] - 2 * T if i == 0 else None)
            if i == 0:
                pe.wait_ge(small_split, 4)
                small(4, H, wfh, wfl).then_inc(f_full, 1)
            if i == 4:
                pe.wait_ge(f_logf, 1)
                pe.wait_ge(const_ready, 1)
                prefix(5, H, z_f).then_inc(c_full, 1)
        pe.wait_ge(fin_copied, T * N_FIN)
        pe.wait_ge(qk_ready, 4 * T)
        for s in range(H + 3):
            if s < H:
                b = s % 2
                if s >= 2:
                    pe.wait_ge(at_qkc, s - 1)
                for i, t in enumerate((q_nat, k_nat)):
                    for m in range(T):
                        last = nc.tensor.transpose(ps[6 + b][0:FA, i * S + m * P:i * S + (m + 1) * P],
                                                   t[:, m, s, :], ident[:, :])
                last.then_inc(at_qk, 1)
            if 0 <= s - 1 < H:
                hd = s - 1
                b = hd % 2
                pe.wait_ge(at_qkc, hd + 1)
                if hd >= 2:
                    pe.wait_ge(at_exp, T * (hd - 1))
                mm(ps[b][:, 0:P], qk_t[0:FA, b, 0:P], qk_t[0:FA, b, S:S + P], True, False)
                mm(ps[b][:, 0:P], ident_b[:, :], mask[:, :], False, True)
                mm(ps[b][:, P:3 * P], qk_t[0:FA, b, P:2 * P], qk_t[0:FA, b, S:2 * S], True, False)
                mm(ps[b][:, 2 * P:3 * P], ident_b[:, :], mask[:, :], False, True).then_inc(at_log, 1)
            if 0 <= s - 2 < H:
                hd = s - 2
                b = hd % 2
                pe.wait_ge(at_exp, T * (hd + 1))
                if hd >= 2:
                    pe.wait_ge(at_ptc, hd - 1)
                for c in range(3):
                    last = nc.tensor.transpose(ps[2 + b][:, c * P:(c + 1) * P], prob[:, b, c * P:(c + 1) * P],
                                               ident[:, :])
                last.then_inc(at_pt, 1)
            if s >= 3:
                hd = s - 3
                b = hd % 2
                pe.wait_ge(at_ptc, hd + 1)
                if hd >= 2:
                    pe.wait_ge(at_on, hd - 1)
                val = slice(hd * DH, (hd + 1) * DH)
                mm(ps[4 + b][:, 0:DH], prob_t[:, b, 0:P], v_nat[:, 0, val], True, True)
                mm(ps[4 + b][:, DH:2 * DH], prob_t[:, b, P:2 * P], v_nat[:, 0, val], True, False)
                mm(ps[4 + b][:, DH:2 * DH], prob_t[:, b, 2 * P:3 * P], v_nat[:, 1, val], False, True)\
                    .then_inc(at_o, 1)
        pe.wait_ge(at_on, H)
        for q in range(2):
            for m in range(T):
                turn(quarter(o_nat, m, q))
        pe.wait_ge(s0["tp_lo"], nt[0] - T)
        for k in range(2):
            rows_granule(G_FOUT + k, hth, htl, 2 * k, k == 0, False)
        turned()
        rows_last(G_FOUT + 2, hth, htl, 4)
        stream_turn()
        turned()
        small(4, NE, wrh, wrl).then_inc(lg_full, 1)
        pe.wait_ge(mem_ready, 1)
        prefix(5, NE, member)
        mm(ps[5][:, T * NE:(T + 1) * NE], ones[:, :], member[:, 0, :], True, False)
        mm(ps[5][:, T * NE:(T + 1) * NE], ones[:, :], member[:, 1, :], False, True).then_inc(rank_full, 1)
        pe.wait_ge(route_ready, 1)
        pe.wait_ge(xl_ready, T)

        def clear_out(stop):
            for half in range(2):
                for c in range(4):
                    last = mm(ps[2 + half][:, c * P:(c + 1) * P], zeros[:, :], zeros[:, :], c == 0, stop and c == 3)
            return last

        def gather(n):
            pe.wait_ge(sel_ready, n * (T + 1))
            for q in range(2):
                for c in range(4):
                    k = slice((4 * q + c) * P, (4 * q + c + 1) * P)
                    o = ps[4 + q][:, c * P:(c + 1) * P]
                    for m in range(T):
                        mm(o, xh[:, m, k], sel[:, m, :], m == 0, False)
                        last = mm(o, xl[:, m, k], sel[:, m, :], False, m == T - 1)
                last.then_inc(gx_full, 1)

        def scatter(n):
            for i in range(2 * T):
                half, m = i // 2, i % 2
                if m == 0:
                    pe.wait_ge(ys_lo, n * 2 - (1 - half))
                if i >= 2:
                    pe.wait_ge(sc_added, n * (2 * T) - (2 * T - (i - 1)))
                part = slice(half * W, (half + 1) * W)
                tok = slice(m * P, (m + 1) * P)
                mm(ps[4 + i % 2][:, :], sel_t[:, tok], ysh[:, part], True, False)
                mm(ps[4 + i % 2][:, :], sel_t[:, tok], ysl[:, part], False, True).then_inc(sc_full, 1)

        def experts(rnd_no):
            gather(1 + rnd_no * (NE + 1))
            clear_out(True).then_inc(null_full, 1)
            pe.wait_ge(null_ready, rnd_no + 1)
            with pe.Fori(rnd_no * NE, (rnd_no + 1) * NE) as e:
                g0 = pe.snap(G_MOE + e * G_EXP)
                e1 = pe.snap(e + 1)
                en = pe.snap(e + (rnd_no + 1))
                pe.wait_ge(gx_lo, en * 2)

                def gate_or_up(gv, gs, bank):
                    for half in range(2):
                        pe.wait_ge(s0["lo"], gv + (half + 1))
                        for c in range(4):
                            k = 4 * half + c
                            last = mm3(ps[bank][:, :], xeh[:, k, :], xel[:, k, :], (gs + half) % SPL, c, k == 0,
                                       k == KD - 1)
                        last.then_inc(s0["used"], 1)

                def hidden_turn(n):
                    pe.wait_ge(e_hid, n)
                    for c in range(4):
                        last = nc.tensor.transpose(ps[6][:, c * P:(c + 1) * P], hb[:, 0, c * P:(c + 1) * P],
                                                   ident[:, :])
                    last.then_inc(e_tp, 1)

                def expert_down(n, gv, gs, final):
                    pe.wait_ge(e_lo, n)
                    for i in range(2):
                        pe.wait_ge(s0["lo"], gv + (i + 1))
                        for kk in range(2):
                            for half in range(2):
                                last = mm3(ps[2 + half][:, :], bth[:, 2 * i + kk, 0:P], btl[:, 2 * i + kk, 0:P],
                                           (gs + i) % SPL, 2 * kk + half, False, final and i == 1 and kk == 1)
                        last.then_inc(s0["used"], 1)

                gate_or_up(g0, G_MOE, 0)
                scatter(en)
                gate_or_up(g0 + 2, G_MOE + 2, 1)
                for m in range(T):
                    nc.tensor.transpose(ps[7][:, m * P:(m + 1) * P], sel[:, m, :].bitcast(F32), ident[:, :])
                for m in range(T):
                    last = mm(ps[7][:, S:S + 1], sel[:, m, :].bitcast(F32), wcur[:, m:m + 1], m == 0, m == T - 1)
                last.then_inc(st_full, 1)
                clear_out(False)
                with pe.Fori(1, NJ) as j:
                    gj = pe.snap(g0 + j * G_BLK)
                    ej = pe.snap(e * NJ + j)
                    pe.wait_ge(e_silu, ej)
                    gate_or_up(gj - 2, G_MOE - 2, 0)
                    hidden_turn(ej)
                    gate_or_up(gj, G_MOE, 1)
                    expert_down(ej, gj + 2, G_MOE + 2, False)
                gather(e + (rnd_no + 2))
                hidden_turn(e1 * NJ)
                expert_down(e1 * NJ, g0 + (G_EXP - 2), G_MOE - 2, True)
            scatter((rnd_no + 1) * (NE + 1))

        experts(0)
        with pe.If(pe.value_load(cnt_i[0:1, 0:1], min_val=0, max_val=S) > P):
            experts(1)
        pe.wait_ge(moe_done, 1)
        n_h[0] = 0
        ple(1, 0, pn1)

    whole.close()


_INS = ["x", "p", "ln_g", "ln_b", "gm_w_in", "gm_b_in", "gm_ln_g", "gm_ln_b", "gm_w_s", "gm_b_s", "gm_w_out",
        "fox_w_in", "fox_b_f", "fox_w_out", "ffn_w_gate", "ffn_w_up", "ffn_w_down",
        "moe_w_router", "moe_w_gate", "moe_w_up", "moe_w_down", "ple_w_gate", "ple_b_gate", "ple_w_proj"]


def kernel(**inputs):
    import numpy as _np
    import concourse.bacc as _bacc
    from concourse import mybir as _mybir
    from concourse.bass_utils import run_bass_kernel_spmd as _run

    nc = _bacc.Bacc("TRN2", target_bir_lowering=False, num_devices=1)
    arrays, args = {}, []
    for name in _INS:
        a = _np.ascontiguousarray(inputs[name])
        arrays[f"in_{name}_dram"] = a
        args.append(nc.dram_tensor(f"in_{name}_dram", a.shape, _mybir.dt.from_np(a.dtype), kind="ExternalInput").ap())
    shape = _np.shape(inputs["x"])
    args.append(nc.dram_tensor("out_dram", shape, _mybir.dt.float32, kind="ExternalOutput").ap())
    build_trunk(nc, *args)
    r = _run(nc, [arrays], core_ids=[0])
    return r.results[0]["out_dram"]
```

```python
from contextlib import ExitStack

import concourse.bass as bass
from concourse import mybir

F32 = mybir.dt.float32
F32R = mybir.dt.float32r
BF16 = mybir.dt.bfloat16
I32 = mybir.dt.int32
ALU = mybir.AluOpType
ACT = mybir.ActivationFunctionType
AX = mybir.AxisListType.X

P = 128
W = 512
RAW = 6
SPL = 3
LN_EPS = 1e-5


def build_trunk(nc, x, p, ln_g, ln_b, gm_w_in, gm_b_in, gm_ln_g, gm_ln_b, gm_w_s, gm_b_s, gm_w_out,
                fox_w_in, fox_b_f, fox_w_out, ffn_w_gate, ffn_w_up, ffn_w_down,
                moe_w_router, moe_w_gate, moe_w_up, moe_w_down, ple_w_gate, ple_b_gate, ple_w_proj, out):
    _, S, D = x.shape
    DEPTH = p.shape[0]
    PD = p.shape[3]
    T = S // P
    KD = D // P
    GW = gm_w_out.shape[1]
    GG = gm_w_s.shape[1]
    GC = GW // GG
    H = fox_b_f.shape[1]
    DH = D // H
    FA = DH + 2
    F = ffn_w_down.shape[1]
    NE = moe_w_router.shape[2]
    NJ = F // W
    ALPHA = float((2 * DEPTH) ** 0.25)
    assert T == 2 and D == 2 * W and F % W == 0 and GW == 4 * W and GC * 2 == W and PD == 2 * P
    assert gm_w_s.shape[2] == P and S == 2 * P

    G_GIN = 0
    N_GIN = 2 * GW // W
    G_GOUT = G_GIN + 2 * N_GIN
    G_FFN = G_GOUT + GW // (2 * P)
    G_BLK = 6
    G_PLE = G_FFN + G_BLK * NJ
    G_FIN = G_PLE + 5
    N_FIN = 3 * D // W
    G_FOUT = G_FIN + 2 * N_FIN
    G_PROJ = G_FOUT + D // (2 * P)
    G_MOE = G_PROJ + 1
    G_EXP = G_BLK * NJ
    G_TAIL = G_MOE + NE * G_EXP + 2
    assert G_EXP % RAW == 0 and G_BLK % SPL == 0 and G_BLK == RAW

    LAST_BANKS = (4, 5, 0, 1)

    GIN_ORDER = [*range(N_GIN // 2, N_GIN), *range(N_GIN // 2)]

    base = (nc.sbuf_base + 31) // 32 * 32
    cursor = [base]

    def at(name, shape, dt, offset=None):
        size = 4
        for n in shape[1:]:
            size *= n
        if offset is None:
            offset = cursor[0]
            cursor[0] += (size + 31) // 32 * 32
        return nc.alloc_sbuf_tensor_at(name, shape, dt, offset=offset), offset + (size + 31) // 32 * 32

    def keep(name, shape, dt=F32):
        return at(name, shape, dt)[0]

    raw = keep("raw", [P, RAW, 4, W])
    wh = keep("wh", [P, SPL, 4, W], F32R)
    wl = keep("wl", [P, SPL, 4, W], F32R)
    h = keep("h", [P, T, D])
    hth_at = cursor[0]
    hth = keep("hth", [P, KD, S], F32R)
    htl = keep("htl", [P, KD, S], F32R)
    xh, nxt = at("xh", [P, T, D], F32R, hth_at)
    xl, _ = at("xl", [P, T, D], F32R, nxt)
    par_b = keep("par_b", [P, 4, D])
    par_a = cursor[0]
    b_in, end_a = at("b_in", [P, 2 * GW], F32)
    ln0, _ = at("ln0", [P, 4, D], F32, par_a)
    o_nat, nxt = at("o_nat", [P, T, D], F32, par_a)
    pn1, nxt = at("pn1", [P, T, PD], F32, nxt)
    ysh, nxt = at("ysh", [P, D], F32R, nxt)
    pth1, nxt = at("pth1", [P, PD // P, S], F32R, nxt)
    pp1, _ = at("pp1", [P, T, D], F32, par_a)
    assert nxt <= end_a
    ple_b = keep("ple_b", [P, DEPTH, D])

    ident = keep("ident", [P, P])
    upper = keep("upper", [P, P])
    ones = keep("ones", [P, P])
    zeros = keep("zeros", [P, P], F32R)
    iota_i = keep("iota_i", [P, P], I32)
    iota = keep("iota", [P, P])
    ident_b = keep("ident_b", [P, P], BF16)
    mask_at = cursor[0]
    mask_f = keep("mask_f", [P, P])
    upper_b, nxt = at("upper_b", [P, P], BF16, mask_at)
    ones_b, _ = at("ones_b", [P, P], BF16, mask_at + 2 * P)
    mask = keep("mask", [P, P], BF16)
    bs_t = keep("bs_t", [P, GG])
    bf_bc = keep("bf_bc", [P, H])
    wf = keep("wf", [P, KD, H])
    wfh = keep("wfh", [P, KD, H], F32R)
    wfl = keep("wfl", [P, KD, H], F32R)
    wr = keep("wr", [P, KD, NE])
    wrh = keep("wrh", [P, KD, NE], F32R)
    wrl = keep("wrl", [P, KD, NE], F32R)
    stats = keep("stats", [P, T, 4, 6])
    mv = keep("mv", [P, T, 2])
    var = keep("var", [P, T])
    std = keep("std", [P, T])
    rstd = keep("rstd", [P, T])
    nwt = keep("nwt", [P, T])
    z_f = keep("z_f", [P, T, H])
    a_f = keep("a_f", [P, T, H])
    small_t = keep("small_t", [P, S])
    lg = keep("lg", [P, T, NE])
    top8 = keep("top8", [P, T, 8])
    eqk = keep("eqk", [P, T, NE])
    key = keep("key", [P, T])
    sel1 = keep("sel1", [P, T, NE])
    sel2 = keep("sel2", [P, T, NE])
    prio = keep("prio", [P, NE])
    prio_i = keep("prio_i", [P, NE], I32)
    gap = keep("gap", [P, T])
    den = keep("den", [P, T])
    w_top = keep("w_top", [P, 2, T])
    member = keep("member", [P, T, NE])
    member_b = keep("member_b", [P, T, NE], BF16)
    slots = keep("slots", [P, 2, T, NE + 1])
    comb = keep("comb", [P, T, NE + 1])
    cnt = keep("cnt", [P, 1])
    cnt_i = keep("cnt_i", [P, 1], I32)
    wcur = keep("wcur", [P, T])
    wslot = keep("wslot", [P, 1])

    ph = cursor[0]
    u, nxt = at("u", [P, T, GW], F32, ph)
    v, nxt = at("v", [P, T, GW], F32, nxt)
    ws_raw, _ = at("ws_raw", [P, GG, P], F32, ph)
    ws_t, end = at("ws_t", [P, GG, P], F32, nxt)
    acc, nxt = at("acc", [P, T, D], F32, ph)
    bth, nxt = at("bth", [P, 4, S], F32R, nxt)
    btl, nxt = at("btl", [P, 4, S], F32R, nxt)
    ptl1, _ = at("ptl1", [P, PD // P, S], F32R, nxt + 4 * W)
    sg, nxt = at("sg", [P, T, W], F32, nxt)
    hb, nxt = at("hb", [P, T, W], F32, nxt)
    per_layer = nxt
    xeh, nxt = at("xeh", [P, KD, P], F32R, nxt)
    xel, nxt = at("xel", [P, KD, P], F32R, nxt)
    sel, nxt = at("sel", [P, T, P], F32R, nxt)
    sel_t, nxt = at("sel_t", [P, S], F32R, nxt)
    end = max(end, nxt)
    ysl, nxt = at("ysl", [P, D], F32R, nxt)
    end = max(end, nxt)
    pn0, nxt = at("pn0", [P, T, PD], F32, per_layer)
    pth, nxt = at("pth", [P, PD // P, S], F32R, nxt)
    ptl, nxt = at("ptl", [P, PD // P, S], F32R, nxt)
    pp0, nxt = at("pp0", [P, T, D], F32, nxt)
    end = max(end, nxt)
    sig = acc
    q_nat, nxt = at("q_nat", [P, T, H, FA], F32, ph)
    k_nat, nxt = at("k_nat", [P, T, H, FA], F32, nxt)
    v_nat, nxt = at("v_nat", [P, T, D], F32, nxt)
    qk_t, nxt = at("qk_t", [P, 2, 2 * S], F32, nxt)
    prob, nxt = at("prob", [P, 2, 3 * P], F32, nxt)
    prob_t, nxt = at("prob_t", [P, 2, 3 * P], F32, nxt)
    nmax = at("nmax", [P, 2, T], F32, nxt)[0]
    rsum = at("rsum", [P, 2, T], F32, nxt + 32)[0]
    rinv = at("rinv", [P, 2, T], F32, nxt + 64)[0]
    end = max(end, nxt + 96)
    assert end <= nc.sbuf_usable_end, (end, nc.sbuf_usable_end)

    ps = [nc.alloc_psum_tensor(f"ps{i}", [P, W], F32) for i in range(8)]

    def sem(name):
        return nc.alloc_semaphore(name)

    raw_landed = [sem(f"raw_landed{i}") for i in range(RAW)]
    raw_landed2 = [sem(f"raw_landed2_{i}") for i in range(4)]
    streams = [dict(hi=sem(f"hi_split{i}"), lo=sem(f"lo_split{i}"), used=sem(f"used{i}"),
                    tp=sem(f"tp_filled{i}"), tp_hi=sem(f"tp_hi{i}"), tp_lo=sem(f"tp_lo{i}"),
                    var=sem(f"ln_var{i}"), std=sem(f"ln_std{i}"), h=sem(f"h_ready{i}"),
                    gb=sem(f"gate_biased{i}"), gs=sem(f"gate_sigmoid{i}"))
               for i in range(2)]
    x_landed = [sem(f"x_landed{i}") for i in range(2 * T)]
    ws_landed = sem("ws_landed")
    b_in_landed = [sem(f"b_in_landed{i}") for i in range(3)]
    bank_full = sem("bank_full")
    sum_read = sem("sum_read")
    gln_landed = sem("gln_landed")
    bs_landed = sem("bs_landed")
    ln0_landed = sem("ln0_landed")
    ln1_landed = sem("ln1_landed")
    pleb_landed = sem("pleb_landed")
    pn_landed = [sem("pn0_landed"), sem("pn1_landed")]
    wf_landed = sem("wf_landed")
    bf_landed = sem("bf_landed")
    wr_landed = sem("wr_landed")
    out_landed = sem("out_landed")
    const_step = sem("const_step")
    const_ready = sem("const_ready")
    ws_tp = sem("ws_tp")
    ws_copied = sem("ws_copied")
    ws_masked = sem("ws_masked")
    gm_biased = sem("gm_biased")
    gm_gelu = sem("gm_gelu")
    v_normed = sem("v_normed")
    sv_full = sem("sv_full")
    mixed = sem("mixed")
    acc_init = sem("acc_init")
    silu_done = sem("silu_done")
    hid_ready = sem("hid_ready")
    part_full = sem("part_full")
    part_added = sem("part_added")
    small_split = sem("small_split")
    small_full = sem("small_full")
    small_copied = sem("small_copied")
    f_full = sem("f_full")
    f_exp = sem("f_exp")
    f_abs = sem("f_abs")
    f_log = sem("f_log")
    f_logf = sem("f_logf")
    c_full = sem("c_full")
    qk_ready = sem("qk_ready")
    fin_copied = sem("fin_copied")
    at_qk = sem("at_qk")
    at_qkc = sem("at_qkc")
    at_log = sem("at_log")
    at_max = sem("at_max")
    at_exp = sem("at_exp")
    at_pt = sem("at_pt")
    at_ptc = sem("at_ptc")
    at_o = sem("at_o")
    at_on = sem("at_on")
    lg_full = sem("lg_full")
    gap_ready = sem("gap_ready")
    gap_exp = sem("gap_exp")
    mem_ready = sem("mem_ready")
    rank_full = sem("rank_full")
    route_ready = sem("route_ready")
    xh_ready = sem("xh_ready")
    xl_ready = sem("xl_ready")
    sel_ready = sem("sel_ready")
    st_full = sem("st_full")
    st_copied = sem("st_copied")
    gx_full = sem("gx_full")
    gx_hi = sem("gx_hi")
    gx_lo = sem("gx_lo")
    e_silu = sem("e_silu")
    e_hid = sem("e_hid")
    e_tp = sem("e_tp")
    e_hi = sem("e_hi")
    e_lo = sem("e_lo")
    ys_hi = sem("ys_hi")
    ys_lo = sem("ys_lo")
    last_hi = sem("last_hi")
    last_lo = sem("last_lo")
    last_full = sem("last_full")
    last_gate = sem("last_gate")
    proj_copied = sem("proj_copied")
    sc_full = sem("sc_full")
    sc_added = sem("sc_added")
    null_ready = sem("null_ready")
    null_full = sem("null_full")
    dve_step = sem("dve_step")
    dve_step2 = sem("dve_step2")

    def cols(w, n0, half):
        return w[half * 4 * P:(half + 1) * 4 * P, bass.ds(n0, W)].rearrange("(c p) n -> p c n", p=P)

    def rows(w, k0):
        return w[bass.ds(k0, 2 * P), :].rearrange("(c p) n -> p c n", p=P)

    def flat(t):
        return t.rearrange("p (c t) n -> p c (t n)", c=2)

    def place(g, which):
        g += (0, G_TAIL)[which]
        return g % RAW, g % SPL

    whole = ExitStack()
    block = whole.enter_context(nc.Block())

    @block.sync
    def _(sp):
        g = [0]

        def load(src, by_rows=False):
            n = g[0]
            g[0] += 1
            slot = n % RAW
            if n >= RAW:
                sp.wait_ge(streams[0]["lo"], n - RAW + 1)
            dst = flat(raw[:, slot]) if by_rows else raw[:, slot]
            sp.dma_start(dst, src).then_inc(raw_landed[slot], 16)

        for i, nb in enumerate(GIN_ORDER):
            for half in range(2):
                if i == 0:
                    for m in range(T):
                        part = slice(half * W, (half + 1) * W)
                        sp.dma_start(h[:, m, part], x[0, m * P:(m + 1) * P, part])\
                            .then_inc(x_landed[half * T + m], 16)
                load(cols(gm_w_in[0], nb * W, half))
        for k in range(GW // (2 * P)):
            load(rows(gm_w_out[0], k * 2 * P), True)

        def block_loads(first, g0, gate, up, j, skip=0):
            for n in range(skip, 4):
                wait_load(g0 + n, first + n, cols((gate, up)[n // 2], j * W, n % 2))

        def wait_load(gv, gs, src, by_rows=False):
            slot = gs % RAW
            sp.wait_ge(streams[0]["lo"], gv - RAW + 1)
            dst = flat(raw[:, slot]) if by_rows else raw[:, slot]
            sp.dma_start(dst, src).then_inc(raw_landed[slot], 16)

        def swiglu_loads(first, g0, gate, up, down, headed=False):
            block_loads(first, g0, gate, up, 0, 2 if headed else 0)
            with sp.Fori(1, NJ) as j:
                gj = sp.snap(g0 + 4 + (j - 1) * G_BLK)
                block_loads(first + 4, gj, gate, up, j)
                for k in range(2):
                    wait_load(gj + 4 + k, first + 8 + k, rows(down, (j - 1) * W + k * 2 * P), True)
            for k in range(2):
                wait_load(g0 + G_EXP - 2 + k, first + G_EXP - 2 + k, rows(down, (NJ - 1) * W + k * 2 * P), True)

        swiglu_loads(G_FFN, G_FFN, ffn_w_gate[0], ffn_w_up[0], ffn_w_down[0])
        g[0] = G_PLE
        load(rows(ple_w_proj[0], 0), True)
        for nb in range(2):
            for half in range(2):
                load(cols(ple_w_gate[0], nb * W, half))
        for nb in range(N_FIN):
            for half in range(2):
                load(cols(fox_w_in[0], nb * W, half))
        for k in range(D // (2 * P)):
            load(rows(fox_w_out[0], k * 2 * P), True)
        load(rows(ple_w_proj[1], 0), True)

        def of(w, ex):
            return w[0, bass.ds(ex, 1)].rearrange("a k n -> (a k) n")

        def expert_head(gv, ex):
            for half in range(2):
                wait_load(gv + half, G_MOE + half, cols(of(moe_w_gate, ex), 0, half))

        def experts(rnd):
            with sp.Fori(rnd * NE, (rnd + 1) * NE) as e:
                g0 = sp.snap(G_MOE + e * G_EXP)
                ex = sp.snap(e - rnd * NE)
                swiglu_loads(G_MOE, g0, of(moe_w_gate, ex), of(moe_w_up, ex), of(moe_w_down, ex), True)
                expert_head(g0 + G_EXP, sp.snap((ex + 1) % NE))

        expert_head(G_MOE, 0)
        experts(0)
        sp.wait_ge(route_ready, 1)
        with sp.If(sp.value_load(cnt_i[0:1, 0:1], min_val=0, max_val=S) > P):
            experts(1)
            sp.wait_ge(streams[0]["lo"], G_TAIL + NE * G_EXP)
        for n in range(4):
            sp.wait_ge(streams[0]["lo"], G_TAIL + n - RAW + 1)
            sp.dma_start(raw[:, place(n, 1)[0]], cols(ple_w_gate[1], n // 2 * W, n % 2))\
                .then_inc(raw_landed2[n], 16)
        for nb in range(2):
            for m in range(T):
                sp.wait_ge(streams[1]["h"], 2 * T + 1 + nb * T + m)
                sp.dma_start(out[0, m * P:(m + 1) * P, nb * W:(nb + 1) * W],
                             h[:, m, nb * W:(nb + 1) * W]).then_inc(out_landed, 16)
        sp.wait_ge(out_landed, 16 * 2 * T)

    @block.gpsimd
    def _(pool):
        step = [0]

        def seq(ins):
            step[0] += 1
            ins.then_inc(const_step, 1)
            pool.wait_ge(const_step, step[0])

        def bcast(dst, src, s):
            pool.dma_start(dst, src.partition_broadcast(P)).then_inc(s, 16)

        seq(pool.memset(ident[:, :], 0.0))
        seq(pool.affine_select(out=ident[:, :], in_=ident[:, :], compare_op=ALU.not_equal, fill=1.0, base=0,
                               pattern=[[-1, P]], channel_multiplier=1))
        bcast(b_in[:, GW:GW + W], gm_b_in[0, GW:GW + W], b_in_landed[0])
        seq(pool.memset(ones[:, :], 1.0))
        seq(pool.affine_select(out=upper[:, :], in_=ones[:, :], compare_op=ALU.is_ge, fill=0.0, base=0,
                               pattern=[[1, P]], channel_multiplier=-1))
        seq(pool.memset(zeros[:, :].bitcast(F32), 0.0))
        seq(pool.memset(mask_f[:, :], 0.0))
        seq(pool.affine_select(out=mask_f[:, :], in_=mask_f[:, :], compare_op=ALU.is_ge, fill=-1e30, base=0,
                               pattern=[[-1, P]], channel_multiplier=1))
        seq(pool.tensor_copy(mask[:, :], mask_f[:, :]))
        seq(pool.tensor_copy(upper_b[:, :], upper[:, :]))
        seq(pool.tensor_copy(ones_b[:, :], ones[:, :]))
        seq(pool.tensor_copy(ident_b[:, :], ident[:, :]))
        seq(pool.iota(iota_i[:, :], pattern=[[1, P]], base=0, channel_multiplier=0))
        seq(pool.tensor_copy(iota[:, :], iota_i[:, :]))
        seq(pool.iota(prio_i[:, :], pattern=[[-1, NE]], base=NE, channel_multiplier=0))
        pool.tensor_copy(prio[:, :], prio_i[:, :]).then_inc(const_ready, 1)
        pool.wait_ge(streams[0]["hi"], 1)
        pool.dma_start(ws_raw[:, :, :], gm_w_s[0].rearrange("g t s -> t g s")).then_inc(ws_landed, 16)
        pool.wait_ge(streams[0]["hi"], 3)
        bcast(b_in[:, GW + W:2 * GW], gm_b_in[0, GW + W:2 * GW], b_in_landed[1])
        pool.wait_ge(streams[0]["hi"], 5)
        bcast(b_in[:, 0:GW], gm_b_in[0, 0:GW], b_in_landed[2])
        for i, src in enumerate((gm_ln_g, gm_ln_b)):
            bcast(par_b[:, 2 * i:2 * i + 2, :].rearrange("p a d -> p (a d)"), src[0], gln_landed)
        pool.dma_start(bs_t[:, :], gm_b_s[0].rearrange("g t -> t g"),
                       allow_slow_non_contiguous=True).then_inc(bs_landed, 16)
        bcast(ple_b[:, :, :].rearrange("p a d -> p (a d)"), ple_b_gate.rearrange("a d -> (a d)"), pleb_landed)
        pool.dma_start(wf[:, :, :], fox_w_in[0, :, 3 * D:3 * D + H].rearrange("(c p) n -> p c n", p=P))\
            .then_inc(wf_landed, 16)
        bcast(bf_bc[:, :], fox_b_f[0], bf_landed)
        pool.dma_start(wr[:, :, :], moe_w_router[0].rearrange("(c p) n -> p c n", p=P)).then_inc(wr_landed, 16)
        pool.wait_ge(ws_copied, 2)
        pool.affine_select(out=ws_t[:, :, :], in_=ws_t[:, :, :], compare_op=ALU.is_ge, fill=0.0, base=0,
                           pattern=[[0, GG], [1, P]], channel_multiplier=-1).then_inc(ws_masked, 1)

        def norms(dst, layer, s):
            for n in range(2):
                bcast(dst[:, 2 * n, :], ln_g[layer, n], s)
                bcast(dst[:, 2 * n + 1, :], ln_b[layer, n], s)

        pool.wait_ge(gm_biased, 2 * N_GIN)
        norms(ln0, 0, ln0_landed)
        pool.wait_ge(mixed, 2 * T * 2)
        norms(par_b, 1, ln1_landed)

        def rest_lo(g, which=0):
            slot, ss = place(g, which)
            st = streams[which]
            if g:
                pool.wait_ge(st["lo"], g)
            pool.wait_ge(st["hi"], g + 1)
            pool.tensor_tensor(wl[:, ss], raw[:, slot], wh[:, ss].bitcast(F32), ALU.subtract).then_inc(st["lo"], 1)

        rest_lo(G_FFN + 1)
        pool.wait_ge(streams[0]["used"], G_FFN)
        pool.dma_start(pn0[:, :, :], p[0, 0].rearrange("(m p) n -> p m n", p=P)).then_inc(pn_landed[0], 16)
        rest_lo(G_PLE + 1)
        pool.wait_ge(streams[0]["h"], 4 * T)
        pool.dma_start(pn1[:, :, :], p[1, 0].rearrange("(m p) n -> p m n", p=P)).then_inc(pn_landed[1], 16)
        for m in range(T):
            pool.wait_ge(xh_ready, m + 1)
            pool.tensor_tensor(xl[:, m, :], h[:, m, :], xh[:, m, :].bitcast(F32), ALU.subtract)\
                .then_inc(xl_ready, 1)
        rest_lo(0, 1)
        rest_lo(1, 1)

    @block.scalar
    def _(act):
        s0 = streams[0]

        def round_hi(g, which=0):
            slot, ss = place(g, which)
            st = streams[which]
            if which == 0:
                act.wait_ge(raw_landed[slot], 16 * (g // RAW + 1))
            else:
                act.wait_ge(raw_landed2[g], 16)
            if g >= SPL:
                act.wait_ge(st["used"], g - SPL + 1)
            nc.scalar.copy(wh[:, ss], raw[:, slot]).then_inc(st["hi"], 1)

        def round_at(gv, gs, rv):
            act.wait_ge(raw_landed[gs % RAW], rv * 16)
            act.wait_ge(s0["used"], gv - SPL + 1)
            nc.scalar.copy(wh[:, gs % SPL], raw[:, gs % RAW]).then_inc(s0["hi"], 1)

        nt = [0, 0]

        def tp_hi(dst, n=W, which=0):
            st = streams[which]
            act.wait_ge(st["tp"], nt[which] + 1)
            bank = ps[6 + nt[which] % 2]
            nc.scalar.copy(dst, bank[:, 0:n].rearrange("p (c t) -> p c t", t=P)).then_inc(st["tp_hi"], 1)
            nt[which] += 1

        def stream_t(dst, q, m):
            return dst[:, 4 * q:4 * q + 4, m * P:(m + 1) * P]

        def ln_sqrt(k, which=0, m=slice(None)):
            act.wait_ge(streams[which]["var"], k)
            nc.scalar.activation(std[:, m], var[:, m], ACT.Sqrt).then_inc(streams[which]["std"], 1)

        def stream_hi(which=0):
            for q in range(2):
                for m in range(T):
                    tp_hi(stream_t(hth, q, m), W, which)

        def norm_sqrt(k, m, which=0):
            ln_sqrt((0 if which else 1 + (k - 1) * T) + m + 1, which, slice(m, m + 1))

        def tile_hi(m, which=0):
            for q in range(2):
                tp_hi(stream_t(hth, q, m), W, which)

        for q in range(2):
            for m in range(T):
                tp_hi(stream_t(hth, q, m))
            round_hi(q)
        for i in range(N_GIN):
            round_hi(2 * i + 2)
            round_hi(2 * i + 3)
            act.wait_ge(gm_biased, T * (i + 1))
            nb = GIN_ORDER[i] * W
            dst = u[:, :, nb:nb + W] if nb < GW else v[:, :, nb - GW:nb - GW + W]
            nc.scalar.activation(dst, dst, ACT.Gelu_apprx_tanh).then_inc(gm_gelu, 1)
            if i == 4:
                ln_sqrt(1)
        for q in range(5):
            if q < 4:
                for m in range(T):
                    tp_hi(stream_t(hth, q % 2, m))
            if q >= 1:
                round_hi(G_GOUT + 2 * q)
                if q < 4:
                    round_hi(G_GOUT + 2 * q + 1)
        norm_sqrt(1, 0)
        round_hi(G_FFN + 1)
        tile_hi(0)
        norm_sqrt(1, 1)
        tile_hi(1)
        act.wait_ge(s0["h"], 2 * T)
        for m in range(T):
            nc.scalar.mul(acc[:, m, :], h[:, m, :], ALPHA).then_inc(acc_init, 1)
        g = G_FFN

        def silu(j):
            for m in range(T):
                nc.scalar.activation(sg[:, m, :], ps[m][:, :], ACT.Silu).then_inc(silu_done, 1)

        round_hi(g + 2)
        round_hi(g + 3)
        act.wait_ge(s0["used"], g + 2)
        silu(0)
        round_hi(g + 4)
        for m in range(T):
            tp_hi(pth[:, :, m * P:(m + 1) * P], 2 * P)
        n_tp = nt[0]
        with act.Fori(1, NJ) as j:
            gj = act.snap(g + 4 + (j - 1) * G_BLK)
            rj = act.snap((g + 4) // RAW + j)

            def rnd(k):
                round_at(gj + k, g + 4 + k, rj + ((g + 4 + k) // RAW - (g + 4) // RAW))

            rnd(1)
            rnd(2)
            rnd(3)
            act.wait_ge(hid_ready, T * j)
            act.wait_ge(s0["used"], gj + 2)
            silu(j)
            for m in range(T):
                act.wait_ge(s0["tp"], j * T + (n_tp - T + m + 1))
                nc.scalar.copy(bth[:, :, m * P:(m + 1) * P],
                               ps[6 + m][:, :].rearrange("p (c t) -> p c t", t=P)).then_inc(s0["tp_hi"], 1)
            for k in range(4, 7):
                rnd(k)
        nt[0] += (NJ - 1) * T
        for m in range(T):
            tp_hi(bth[:, :, m * P:(m + 1) * P])
        round_hi(g + G_EXP - 1)

        def projected(g, pp, banks):
            for i in range(2 * T):
                act.wait_ge(s0["used"], g + 1)
                nc.scalar.copy(pp[:, i // 2, i % 2 * W:(i % 2 + 1) * W], ps[banks[i]][:, :])\
                    .then_inc(proj_copied, 1)

        def ple(which, g0, ready, last):
            st = streams[which]
            for nb in range(2):
                for k in range(2):
                    n = g0 + 2 + 2 * nb + k
                    if ready <= n < last:
                        round_hi(n, which)
                for m in range(T):
                    act.wait_ge(st["gb"], nb * T + m + 1)
                    part = sig[:, m, nb * W:(nb + 1) * W]
                    nc.scalar.activation(part, part, ACT.Sigmoid).then_inc(st["gs"], 1)
                if which == 0:
                    for m in range(T):
                        tp_hi(stream_t(hth, nb, m))

        round_hi(G_PLE)
        norm_sqrt(2, 0)
        tile_hi(0)
        round_hi(G_PLE + 1)
        norm_sqrt(2, 1)
        round_hi(G_PLE + 2)
        projected(G_PLE, pp0, (4, 5, 0, 1))
        tile_hi(1)
        ple(0, G_PLE + 1, G_PLE + 3, G_PLE + 7)

        def small_out(times, bank, n):
            act.wait_ge(small_full, times)
            nc.scalar.copy(small_t[0:n, :], ps[bank][0:n, 0:S]).then_inc(small_copied, 1)

        act.wait_ge(wf_landed, 16)
        nc.scalar.copy(wfh[:, :, :], wf[:, :, :]).then_inc(small_split, 1)
        act.wait_ge(wr_landed, 16)
        nc.scalar.copy(wrh[:, :, :], wr[:, :, :]).then_inc(small_split, 1)
        for i in range(N_FIN):
            round_hi(G_FIN + 2 * i + 2)
            round_hi(G_FIN + 2 * i + 3)
            act.wait_ge(s0["used"], G_FIN + 2 * i + 2)
            what, half = i // 2, i % 2
            for m in range(T):
                bank = ps[(i + 1) % 2 * 2 + m]
                if what < 2:
                    dst = (q_nat, k_nat)[what][:, m, half * (H // 2):(half + 1) * (H // 2), 0:DH]
                    src = bank[:, :].rearrange("p (h d) -> p h d", d=DH)
                    ins = nc.scalar.mul(dst, src, DH ** -0.5) if what == 0 else nc.scalar.copy(dst, src)
                else:
                    ins = nc.scalar.copy(v_nat[:, m, half * W:(half + 1) * W], bank[:, :])
                ins.then_inc(fin_copied, 1)
            if i == 0:
                small_out(1, 5, H)
            if i == 1:
                act.wait_ge(f_abs, 1)
                nc.scalar.activation(a_f[:, :, :], a_f[:, :, :], ACT.Exp, scale=-1.0).then_inc(f_exp, 1)
            if i == 2:
                act.wait_ge(f_abs, 2)
                nc.scalar.activation(a_f[:, :, :], a_f[:, :, :], ACT.Ln).then_inc(f_log, 1)
        for s in range(H + 1):
            if s < H:
                act.wait_ge(at_qk, s + 1)
                nc.scalar.copy(qk_t[0:FA, s % 2, :], ps[6 + s % 2][0:FA, :]).then_inc(at_qkc, 1)
            if s >= 1:
                hd = s - 1
                act.wait_ge(at_max, T * (hd + 1))
                if hd >= 2:
                    act.wait_ge(at_pt, hd - 1)
                for m, (a, b) in enumerate(((0, P), (P, 3 * P))):
                    nc.scalar.activation(prob[:, hd % 2, a:b], ps[hd % 2][:, a:b], ACT.Exp,
                                         bias=nmax[:, hd % 2, m:m + 1], accum_out=rsum[:, hd % 2, m:m + 1]).then_inc(at_exp, 1)
        stream_hi()
        round_hi(G_FOUT + 2)
        for m in range(T):
            tp_hi(pth1[:, :, m * P:(m + 1) * P], 2 * P)
        round_hi(G_FOUT + 3)
        round_hi(G_PROJ)
        norm_sqrt(3, 0)
        tile_hi(0)
        round_hi(G_MOE)
        norm_sqrt(3, 1)
        round_hi(G_MOE + 1)
        tile_hi(1)
        projected(G_PROJ, pp1, (4, 5, 0, 1))
        small_out(2, 2, NE)
        for m in range(T):
            nc.scalar.copy(xh[:, m, :], h[:, m, :]).then_inc(xh_ready, 1)
        act.wait_ge(gap_ready, 1)
        nc.scalar.activation(gap[:, :], gap[:, :], ACT.Exp).then_inc(gap_exp, 1)
        act.wait_ge(s0["h"], 2 * T * 4)
        for m in range(T):
            nc.scalar.mul(acc[:, m, :], h[:, m, :], ALPHA).then_inc(acc_init, 1)

        def scale_out(done):
            for half in range(2):
                nc.scalar.mul(ysh[:, half * W:(half + 1) * W], ps[2 + half][:, :], wslot[:, 0:1])\
                    .then_inc(done, 1)

        def gathered(n):
            for q in range(2):
                act.wait_ge(gx_full, n * 2 - (1 - q))
                nc.scalar.copy(xeh[:, 4 * q:4 * q + 4, :],
                               ps[4 + q][:, :].rearrange("p (c t) -> p c t", t=P)).then_inc(gx_hi, 1)

        def experts(rnd_no):
            if rnd_no:
                gathered(1 + rnd_no * (NE + 1))
            with act.Fori(rnd_no * NE, (rnd_no + 1) * NE) as e:
                g0 = act.snap(G_MOE + e * G_EXP)
                r0 = act.snap(G_MOE // RAW + e * NJ)
                e1 = act.snap(e + 1)

                def rnd(k):
                    round_at(g0 + k, G_MOE + k, r0 + ((G_MOE + k) // RAW - G_MOE // RAW + 1))

                rnd(2)
                act.wait_ge(s0["used"], g0)
                scale_out(ys_hi)
                rnd(3)
                act.wait_ge(s0["used"], g0 + 2)
                nc.scalar.activation(sg[:, 0, :], ps[0][:, :], ACT.Silu).then_inc(e_silu, 1)
                rnd(4)
                rnd(5)
                act.wait_ge(st_full, e1)
                nc.scalar.copy(sel_t[:, :], ps[7][:, 0:S]).then_inc(st_copied, 1)
                nc.scalar.copy(wslot[:, :], ps[7][:, S:S + 1]).then_inc(st_copied, 1)
                with act.Fori(1, NJ) as j:
                    gj = act.snap(g0 + j * G_BLK)
                    rj = act.snap(r0 + j)
                    ej = act.snap(e * NJ + j)

                    def rnd_j(k):
                        k -= 2
                        round_at(gj + k, G_MOE + k, rj + ((G_MOE + k) // RAW - G_MOE // RAW + 1))

                    rnd_j(2)
                    rnd_j(3)
                    act.wait_ge(e_hid, ej)
                    act.wait_ge(s0["used"], gj)
                    nc.scalar.activation(sg[:, 0, :], ps[0][:, :], ACT.Silu).then_inc(e_silu, 1)
                    act.wait_ge(e_tp, ej)
                    nc.scalar.copy(bth[:, :, 0:P],
                                   ps[6][:, :].rearrange("p (c t) -> p c t", t=P)).then_inc(e_hi, 1)
                    for k in range(4, 8):
                        rnd_j(k)
                act.wait_ge(e_tp, e1 * NJ)
                nc.scalar.copy(bth[:, :, 0:P],
                               ps[6][:, :].rearrange("p (c t) -> p c t", t=P)).then_inc(e_hi, 1)
                gathered(e + (rnd_no + 2))
                rnd(G_EXP)
                rnd(G_EXP + 1)
            act.wait_ge(s0["used"], G_MOE + (rnd_no + 1) * NE * G_EXP)

        gathered(1)
        act.wait_ge(null_ready, 2)
        act.wait_ge(null_full, 1)
        experts(0)
        act.wait_ge(route_ready, 1)
        with act.If(act.value_load(cnt_i[0:1, 0:1], min_val=0, max_val=S) > P):
            experts(1)
            act.wait_ge(s0["lo"], G_TAIL + NE * G_EXP)
        scale_out(last_hi)
        act.wait_ge(s0["lo"], G_TAIL)
        round_hi(0, 1)
        norm_sqrt(1, 0, 1)
        round_hi(1, 1)
        tile_hi(0, 1)
        round_hi(2, 1)
        norm_sqrt(1, 1, 1)
        tile_hi(1, 1)
        ple(1, 0, 3, 4)

    @block.vector
    def _(dve):
        s0 = streams[0]
        step = [0, 0]

        def seq(ins, which=0):
            s = (dve_step, dve_step2)[which]
            step[which] += 1
            ins.then_inc(s, 1)
            dve.wait_ge(s, step[which])

        def rest_lo(g, which=0):
            slot, ss = place(g, which)
            st = streams[which]
            dve.wait_ge(st["hi"], g + 1)
            nc.vector.tensor_tensor(wl[:, ss], raw[:, slot], wh[:, ss].bitcast(F32), ALU.subtract)\
                .then_inc(st["lo"], 1)

        def rest_at(gv, gs):
            dve.wait_ge(s0["hi"], gv + 1)
            nc.vector.tensor_tensor(wl[:, gs % SPL], raw[:, gs % RAW], wh[:, gs % SPL].bitcast(F32),
                                    ALU.subtract).then_inc(s0["lo"], 1)

        nt = [0, 0]

        def tp_lo(dst, hi, n=W, which=0):
            st = streams[which]
            dve.wait_ge(st["tp_hi"], nt[which] + 1)
            bank = ps[6 + nt[which] % 2]
            nc.vector.tensor_tensor(dst, bank[:, 0:n].rearrange("p (c t) -> p c t", t=P), hi.bitcast(F32),
                                    ALU.subtract).then_inc(st["tp_lo"], 1)
            nt[which] += 1

        def stream_t(dst, q, m):
            return dst[:, 4 * q:4 * q + 4, m * P:(m + 1) * P]

        def stream_lo(q, m, which=0):
            tp_lo(stream_t(htl, q, m), stream_t(hth, q, m), W, which)

        def ln_var(n_stats, which=0):
            for m in range(T):
                seq(nc.vector.bn_aggr(mv[:, m, :], stats[:, m, 0:n_stats, :].rearrange("p a b -> p (a b)")), which)
            nc.vector.tensor_scalar(var[:, :], mv[:, :, 1], LN_EPS, None, ALU.add)\
                .then_inc(streams[which]["var"], 1)

        def ln_rstd(k, which=0, m=slice(None)):
            dve.wait_ge(streams[which]["std"], k)
            seq(nc.vector.reciprocal(rstd[:, m], std[:, m]), which)
            seq(nc.vector.tensor_tensor(nwt[:, m], rstd[:, m], rstd[:, m], ALU.mult), which)
            seq(nc.vector.tensor_tensor(nwt[:, m], nwt[:, m], var[:, m], ALU.mult), which)
            seq(nc.vector.tensor_scalar(nwt[:, m], nwt[:, m], -0.5, 1.5, ALU.mult, ALU.add), which)
            seq(nc.vector.tensor_tensor(rstd[:, m], rstd[:, m], nwt[:, m], ALU.mult), which)

        def centre(t, m, part, gain, which=0):
            return nc.vector.scalar_tensor_tensor(out=t[:, m, part], in0=t[:, m, part], scalar=mv[:, m, 0:1],
                                                  in1=gain, op0=ALU.subtract, op1=ALU.mult)

        def scale_bias(dst, t, m, part, bias):
            return nc.vector.scalar_tensor_tensor(out=dst[:, m, part], in0=t[:, m, part],
                                                  scalar=rstd[:, m:m + 1], in1=bias, op0=ALU.mult, op1=ALU.add)

        def acc_stats(m, half, which=0):
            seq(nc.vector.bn_stats(stats[:, m, half, :], acc[:, m, half * W:(half + 1) * W]), which)

        def norm(k, total, par, n, which=0, meanwhile=None):
            for m in range(T):
                total(m, 0)
                acc_stats(m, 0, which)
                if m > 0:
                    for q in range(2):
                        stream_lo(q, m - 1, which)
                total(m, 1)
                acc_stats(m, 1, which)
                seq(nc.vector.bn_aggr(mv[:, m, :], stats[:, m, 0:2, :].rearrange("p a b -> p (a b)")), which)
                nc.vector.tensor_scalar(var[:, m:m + 1], mv[:, m, 1:2], LN_EPS, None, ALU.add)\
                    .then_inc(streams[which]["var"], 1)
                for half in range(2):
                    part = slice(half * W, (half + 1) * W)
                    seq(centre(acc, m, part, par[:, 2 * n, part]), which)
                ln_rstd((0 if which else 1 + (k - 1) * T) + m + 1, which, slice(m, m + 1))
                for half in range(2):
                    part = slice(half * W, (half + 1) * W)
                    scale_bias(h, acc, m, part, par[:, 2 * n + 1, part]).then_inc(streams[which]["h"], 1)
            if meanwhile is not None:
                meanwhile()
            for q in range(2):
                stream_lo(q, T - 1, which)

        def residual(k, g_end):
            def total(m, half):
                if m == T - 1 and half == 1:
                    dve.wait_ge(s0["used"], g_end)
                else:
                    dve.wait_ge(bank_full, (k - 1) * 3 + 2 * m + half + 1)
                part = slice(half * W, (half + 1) * W)
                nc.vector.scalar_tensor_tensor(out=acc[:, m, part], in0=h[:, m, part], scalar=ALPHA,
                                               in1=ps[2 * m + half][:, :], op0=ALU.mult, op1=ALU.add)\
                    .then_inc(sum_read, 1)
                dve.wait_ge(sum_read, (k - 1) * 2 * T + 2 * m + half + 1)
            return total

        for q in range(2):
            for m in range(T):
                stream_lo(q, m)
            rest_lo(q)
        def v_stats(i):
            dve.wait_ge(gm_gelu, i + 1)
            for m in range(T):
                seq(nc.vector.bn_stats(stats[:, m, i, :], v[:, m, i * W:(i + 1) * W]))

        def mix(q):
            dve.wait_ge(gm_gelu, N_GIN // 2 + q + 1)
            for m in range(T):
                dve.wait_ge(sv_full, q * T + m + 1)
                for k in range(2):
                    grp = 2 * q + k
                    part = u[:, m, grp * GC:(grp + 1) * GC]
                    nc.vector.scalar_tensor_tensor(out=part, in0=ps[4 + m][:, k * GC:(k + 1) * GC],
                                                   scalar=bs_t[:, grp:grp + 1], in1=part, op0=ALU.add,
                                                   op1=ALU.mult).then_inc(mixed, 1)

        for i in range(N_GIN):
            rest_lo(2 * i + 2)
            rest_lo(2 * i + 3)
            if i == N_GIN - 1:
                dve.wait_ge(bs_landed, 16)
                mix(0)
            if i in (0, 1, N_GIN // 2):
                dve.wait_ge(b_in_landed[min(i, 2)], 16)
            dve.wait_ge(s0["used"], 2 * i + 2)
            nb = GIN_ORDER[i] * W
            for m in range(T):
                dst = u[:, m, nb:nb + W] if nb < GW else v[:, m, nb - GW:nb - GW + W]
                nc.vector.tensor_tensor(dst, ps[i % 2 * 2 + m][:, :], b_in[:, nb:nb + W], ALU.add)\
                    .then_inc(gm_biased, 1)
            if i == 1:
                for k in range(2):
                    dve.wait_ge(ws_tp, k + 1)
                    nc.vector.tensor_copy(ws_t[:, 4 * k:4 * k + 4, :],
                                          ps[4 + k][:, :].rearrange("p (g t) -> p g t", t=P)).then_inc(ws_copied, 1)
            if 1 <= i <= 4:
                v_stats(i - 1)
            if i == 4:
                ln_var(4)
                dve.wait_ge(gln_landed, 32)
            if i in (4, 5):
                m = i - 4
                for q in range(2):
                    part = slice(q * D, (q + 1) * D)
                    seq(centre(v, m, part, par_b[:, q, :]))
            if i == 5:
                ln_rstd(1)
            for m, q in {5: [(0, 0)], 6: [(0, 1), (1, 0), (1, 1)]}.get(i, []):
                part = slice(q * D, (q + 1) * D)
                scale_bias(v, v, m, part, par_b[:, 2 + q, :]).then_inc(v_normed, 1)
        def u_lo(q):
            for m in range(T):
                stream_lo(q % 2, m)

        mix(1)
        u_lo(0)
        for q in range(1, 4):
            if q >= 2:
                rest_lo(G_GOUT + 2 * q - 2)
                rest_lo(G_GOUT + 2 * q - 1)
            if q < 3:
                mix(q + 1)
            u_lo(q)
        rest_lo(G_GOUT + 6)
        rest_lo(G_GOUT + 7)
        rest_lo(G_FFN)
        dve.wait_ge(ln0_landed, 64)
        norm(1, residual(1, G_FFN), ln0, 0)
        g = G_FFN

        def hid(j):
            for m in range(T):
                nc.vector.tensor_tensor(hb[:, m, :], ps[2 + m][:, :], sg[:, m, :], ALU.mult)\
                    .then_inc(hid_ready, 1)

        def part_in(i, n0, gv, bank):
            m, half = i // 2, i % 2
            part = acc[:, m, half * W:(half + 1) * W]
            if i < 2 * T - 1:
                dve.wait_ge(part_full, n0 + (i + 1))
            else:
                dve.wait_ge(s0["used"], gv + 2)
            nc.vector.tensor_tensor(part, part, ps[bank][:, :], ALU.add).then_inc(part_added, 1)

        def parts(n0, gv):
            for i in range(2 * T):
                part_in(i, n0, gv, 4 + i % 2)

        def last_part(m, half):
            i = 2 * m + half
            part_in(i, (NJ - 1) * (2 * T - 1), G_PLE - 2, i)
            dve.wait_ge(part_added, (NJ - 1) * 2 * T + i + 1)

        dve.wait_ge(s0["lo"], g + 2)
        rest_lo(g + 2)
        rest_lo(g + 3)
        rest_lo(g + 4)
        dve.wait_ge(acc_init, T)
        dve.wait_ge(silu_done, T)
        dve.wait_ge(s0["used"], g + 4)
        hid(0)
        for m in range(T):
            tp_lo(ptl[:, :, m * P:(m + 1) * P], pth[:, :, m * P:(m + 1) * P], 2 * P)
        n_tp = nt[0]
        with dve.Fori(1, NJ) as j:
            gj = dve.snap(g + 4 + (j - 1) * G_BLK)
            rest_at(gj + 1, g + 5)
            rest_at(gj + 2, g + 6)
            rest_at(gj + 3, g + 7)
            for m in range(T):
                dve.wait_ge(s0["tp_hi"], j * T + (n_tp - T + m + 1))
                nc.vector.tensor_tensor(btl[:, :, m * P:(m + 1) * P],
                                        ps[6 + m][:, :].rearrange("p (c t) -> p c t", t=P),
                                        bth[:, :, m * P:(m + 1) * P].bitcast(F32), ALU.subtract)\
                    .then_inc(s0["tp_lo"], 1)
            rest_at(gj + 4, g + 8)
            rest_at(gj + 5, g + 9)
            dve.wait_ge(silu_done, j * T + T)
            dve.wait_ge(s0["used"], gj + 4)
            hid(j)
            rest_at(gj + 6, g + 10)
            parts((j - 1) * (2 * T - 1), gj + 4)
        nt[0] += (NJ - 1) * T
        for m in range(T):
            tp_lo(btl[:, :, m * P:(m + 1) * P], bth[:, :, m * P:(m + 1) * P])
        rest_lo(g + G_EXP - 1)
        rest_lo(G_PLE)

        def ple(which, g0, pp, last):
            st = streams[which]
            if which == 1:
                dve.wait_ge(st["lo"], 2)
            for nb in range(2):
                for i in range(2):
                    n = g0 + 2 + 2 * nb + i
                    if n < last:
                        rest_lo(n, which)
                part = slice(nb * W, (nb + 1) * W)

                def bias(m):
                    nc.vector.tensor_tensor(sig[:, m, part], ps[2 * (1 - nb) + m][:, :], ple_b[:, which, part],
                                            ALU.add).then_inc(st["gb"], 1)

                def gated(m):
                    dve.wait_ge(st["gs"], nb * T + m + 1)
                    seq(nc.vector.tensor_tensor(sig[:, m, part], sig[:, m, part], pp[:, m, part], ALU.mult), which)
                    nc.vector.tensor_tensor(h[:, m, part], h[:, m, part], sig[:, m, part], ALU.add)\
                        .then_inc(st["h"], 1)

                if nb == 1 and which == 1:
                    dve.wait_ge(last_gate, 1)
                    bias(0)
                    gated(0)
                    dve.wait_ge(st["used"], g0 + 4)
                    bias(1)
                    gated(1)
                else:
                    dve.wait_ge(st["used"], g0 + 2 + 2 * nb)
                    for m in range(T):
                        bias(m)
                    for m in range(T):
                        gated(m)
                if which == 0:
                    for m in range(T):
                        stream_lo(nb, m)

        def gate_rest():
            dve.wait_ge(s0["lo"], G_PLE + 2)
            rest_lo(G_PLE + 2)

        norm(2, last_part, ln0, 1, meanwhile=gate_rest)
        dve.wait_ge(pleb_landed, 16)
        ple(0, G_PLE + 1, pp0, G_PLE + 7)
        dve.wait_ge(small_split, 1)
        nc.vector.tensor_tensor(wfl[:, :, :], wf[:, :, :], wfh[:, :, :].bitcast(F32), ALU.subtract)\
            .then_inc(small_split, 1)
        dve.wait_ge(small_split, 3)
        nc.vector.tensor_tensor(wrl[:, :, :], wr[:, :, :], wrh[:, :, :].bitcast(F32), ALU.subtract)\
            .then_inc(small_split, 1)
        for i in range(N_FIN):
            rest_lo(G_FIN + 2 * i + 2)
            rest_lo(G_FIN + 2 * i + 3)
            if i == 1:
                dve.wait_ge(f_full, 1)
                dve.wait_ge(bf_landed, 16)
                for m in range(T):
                    seq(nc.vector.tensor_tensor(z_f[:, m, :], ps[4][:, m * H:(m + 1) * H], bf_bc[:, :], ALU.add))
                nc.vector.scalar_tensor_tensor(out=a_f[:, :, :], in0=z_f[:, :, :], scalar=-1.0, in1=z_f[:, :, :],
                                               op0=ALU.mult, op1=ALU.max).then_inc(f_abs, 1)
                dve.wait_ge(f_abs, 1)
                seq(nc.vector.tensor_scalar(z_f[:, :, :], z_f[:, :, :], 0.0, None, ALU.min))
                dve.wait_ge(f_exp, 1)
                nc.vector.tensor_scalar(a_f[:, :, :], a_f[:, :, :], 1.0, None, ALU.add).then_inc(f_abs, 1)
            if i == 3:
                dve.wait_ge(f_log, 1)
                nc.vector.tensor_tensor(z_f[:, :, :], z_f[:, :, :], a_f[:, :, :], ALU.subtract)\
                    .then_inc(f_logf, 1)
        dve.wait_ge(c_full, 1)
        for m in range(T):
            c = ps[5][:, m * H:(m + 1) * H]
            nc.vector.memset(q_nat[:, m, :, DH], 1.0).then_inc(qk_ready, 1)
            nc.vector.tensor_copy(q_nat[:, m, :, DH + 1], c).then_inc(qk_ready, 1)
            nc.vector.tensor_scalar(k_nat[:, m, :, DH], c, -1.0, None, ALU.mult).then_inc(qk_ready, 1)
            nc.vector.memset(k_nat[:, m, :, DH + 1], 1.0).then_inc(qk_ready, 1)
        for s in range(1, H + 3):
            if s <= H:
                hd = s - 1
                dve.wait_ge(at_log, hd + 1)
                for m, (a, b) in enumerate(((0, P), (P, 3 * P))):
                    nc.vector.tensor_reduce(nmax[:, hd % 2, m:m + 1], ps[hd % 2][:, a:b], AX, ALU.max,
                                            negate=True).then_inc(at_max, 1)
            if 0 <= s - 2 < H:
                hd = s - 2
                dve.wait_ge(at_pt, hd + 1)
                if hd >= 2:
                    dve.wait_ge(at_o, hd - 1)
                nc.vector.tensor_copy(prob_t[:, hd % 2, :], ps[2 + hd % 2][:, 0:3 * P]).then_inc(at_ptc, 1)
                if hd >= 2:
                    dve.wait_ge(at_on, hd - 1)
                seq(nc.vector.reciprocal(rinv[:, hd % 2, :], rsum[:, hd % 2, :]))
            if s >= 3:
                hd = s - 3
                dve.wait_ge(at_o, hd + 1)
                nc.vector.tensor_tensor(o_nat[:, :, hd * DH:(hd + 1) * DH],
                                        ps[4 + hd % 2][:, 0:T * DH].rearrange("p (m d) -> p m d", d=DH),
                                        rinv[:, hd % 2, :].rearrange("p (m a) -> p m a", a=1)
                                        .broadcast_to([P, T, DH]), ALU.mult).then_inc(at_on, 1)
        for q in range(2):
            for m in range(T):
                stream_lo(q, m)
        rest_lo(G_FOUT + 2)
        for m in range(T):
            tp_lo(ptl1[:, :, m * P:(m + 1) * P], pth1[:, :, m * P:(m + 1) * P], 2 * P)
        rest_lo(G_FOUT + 3)
        rest_lo(G_PROJ)
        dve.wait_ge(ln1_landed, 64)
        norm(3, residual(2, G_PROJ), par_b, 0)
        rest_lo(G_MOE)


        def select(rnd_no, ex):
            for m in range(T):
                nc.vector.tensor_scalar(sel[:, m, :], iota[:, :], slots[:, rnd_no, m, ex], None,
                                        ALU.is_equal).then_inc(sel_ready, 1)

        def weights(ex):
            nc.vector.tensor_copy(wcur[:, :], comb[:, :, ex].rearrange("p m a -> p (m a)")).then_inc(sel_ready, 1)

        dve.wait_ge(lg_full, 1)
        dve.wait_ge(const_ready, 1)
        seq(nc.vector.tensor_copy(lg[:, :, :], ps[3][:, 0:T * NE].rearrange("p (m e) -> p m e", e=NE)))
        for m in range(T):
            seq(nc.vector.max(top8[:, m, :], lg[:, m, :]))
        nc.vector.tensor_tensor(gap[:, :], top8[:, :, 1], top8[:, :, 0], ALU.subtract).then_inc(gap_ready, 1)

        def wide(t):
            return t.rearrange("p (m a) -> p m a", a=1).broadcast_to([P, T, NE])

        prios = prio[:, :].rearrange("p (a e) -> p a e", a=1).broadcast_to([P, T, NE])

        def first(dst, rank, but=None):
            seq(nc.vector.tensor_tensor(eqk[:, :, :], lg[:, :, :], wide(top8[:, :, rank]), ALU.is_equal))
            if but is not None:
                seq(nc.vector.tensor_tensor(eqk[:, :, :], eqk[:, :, :], but, ALU.is_gt))
            seq(nc.vector.tensor_tensor(eqk[:, :, :], eqk[:, :, :], prios, ALU.mult))
            seq(nc.vector.tensor_reduce(key[:, :], eqk[:, :, :], AX, ALU.max))
            seq(nc.vector.tensor_tensor(dst, prios, wide(key[:, :]), ALU.is_equal))

        first(sel1[:, :, :], 0)
        first(sel2[:, :, :], 1, sel1[:, :, :])
        nc.vector.tensor_tensor(member_b[:, :, :], sel1[:, :, :], sel2[:, :, :], ALU.add).then_inc(mem_ready, 1)
        seq(nc.vector.tensor_tensor(member[:, :, :], sel1[:, :, :], sel2[:, :, :], ALU.add))
        dve.wait_ge(rank_full, 1)
        ranks = ps[2][:, 0:T * NE].rearrange("p (m e) -> p m e", e=NE)
        seq(nc.vector.memset(slots[:, 0, :, NE:NE + 1], -1.0))
        seq(nc.vector.tensor_tensor(slots[:, 0, :, 0:NE], member[:, :, :], ranks, ALU.mult))
        seq(nc.vector.tensor_scalar(slots[:, 0, :, 0:NE], slots[:, 0, :, 0:NE], -1.0, None, ALU.add))
        seq(nc.vector.tensor_reduce(cnt[:, :], ps[2][:, T * NE:(T + 1) * NE], AX, ALU.max))
        select(0, slice(0, 1))
        rest_lo(G_MOE + 1)
        dve.wait_ge(gap_exp, 1)
        seq(nc.vector.tensor_scalar(den[:, :], gap[:, :], 1.0, None, ALU.add))
        seq(nc.vector.reciprocal(w_top[:, 0, :], den[:, :]))
        seq(nc.vector.tensor_tensor(w_top[:, 1, :], w_top[:, 0, :], gap[:, :], ALU.mult))
        for m in range(T):
            seq(nc.vector.tensor_scalar(comb[:, m, 0:NE], sel1[:, m, :], w_top[:, 0, m:m + 1], None, ALU.mult))
            seq(nc.vector.scalar_tensor_tensor(out=comb[:, m, 0:NE], in0=sel2[:, m, :], scalar=w_top[:, 1, m:m + 1],
                                               in1=comb[:, m, 0:NE], op0=ALU.mult, op1=ALU.add))
        seq(nc.vector.memset(comb[:, :, NE:NE + 1], 0.0))
        weights(slice(0, 1))
        seq(nc.vector.tensor_scalar(slots[:, 1, :, :], slots[:, 0, :, :], float(-P), None, ALU.add))
        nc.vector.tensor_copy(cnt_i[:, :], cnt[:, :]).then_inc(route_ready, 1)
        dve.wait_ge(acc_init, 2 * T)

        def gathered(n):
            for q in range(2):
                dve.wait_ge(gx_hi, n * 2 - (1 - q))
                part = slice(4 * q, 4 * q + 4)
                nc.vector.tensor_tensor(xel[:, part, :], ps[4 + q][:, :].rearrange("p (c t) -> p c t", t=P),
                                        xeh[:, part, :].bitcast(F32), ALU.subtract).then_inc(gx_lo, 1)

        def scale_out(n, hi, done):
            for half in range(2):
                dve.wait_ge(hi, n * 2 - (1 - half))
                part = slice(half * W, (half + 1) * W)
                nc.vector.scalar_tensor_tensor(out=ysl[:, part], in0=ps[2 + half][:, :], scalar=wslot[:, 0:1],
                                               in1=ysh[:, part].bitcast(F32), op0=ALU.mult,
                                               op1=ALU.subtract).then_inc(done, 1)

        def add_scattered(n):
            for i in range(2 * T):
                half, m = i // 2, i % 2
                dve.wait_ge(sc_full, n * (2 * T) - (2 * T - 1 - i))
                part = acc[:, m, half * W:(half + 1) * W]
                nc.vector.tensor_tensor(part, part, ps[4 + i][:, :], ALU.add).then_inc(sc_added, 1)

        def experts(rnd_no):
            if rnd_no:
                select(rnd_no, slice(0, 1))
                weights(slice(0, 1))
            gathered(1 + rnd_no * (NE + 1))
            with dve.Fori(rnd_no * NE, (rnd_no + 1) * NE) as e:
                g0 = dve.snap(G_MOE + e * G_EXP)
                e1 = dve.snap(e + 1)
                nxt_ex = dve.snap(e + (1 - rnd_no * NE))
                scale_out(e1, ys_hi, ys_lo)
                rest_at(g0 + 2, G_MOE + 2)
                rest_at(g0 + 3, G_MOE + 3)
                add_scattered(e1)
                rest_at(g0 + 4, G_MOE + 4)
                rest_at(g0 + 5, G_MOE + 5)

                def hidden(n, gv):
                    dve.wait_ge(e_silu, n)
                    dve.wait_ge(s0["used"], gv)
                    nc.vector.tensor_tensor(hb[:, 0, :], ps[1][:, :], sg[:, 0, :], ALU.mult).then_inc(e_hid, 1)

                def hidden_lo(n):
                    dve.wait_ge(e_hi, n)
                    nc.vector.tensor_tensor(btl[:, :, 0:P], ps[6][:, :].rearrange("p (c t) -> p c t", t=P),
                                            bth[:, :, 0:P].bitcast(F32), ALU.subtract).then_inc(e_lo, 1)

                hidden(e * NJ + 1, g0 + 4)
                dve.wait_ge(st_full, e1)
                select(rnd_no, bass.ds(nxt_ex, 1))
                weights(bass.ds(nxt_ex, 1))
                with dve.Fori(1, NJ) as j:
                    gj = dve.snap(g0 + j * G_BLK)
                    ej = dve.snap(e * NJ + j)
                    rest_at(gj, G_MOE)
                    rest_at(gj + 1, G_MOE + 1)
                    hidden_lo(ej)
                    rest_at(gj + 2, G_MOE + 2)
                    rest_at(gj + 3, G_MOE + 3)
                    hidden(ej + 1, gj + 2)
                    rest_at(gj + 4, G_MOE + 4)
                    rest_at(gj + 5, G_MOE + 5)
                hidden_lo(e1 * NJ)
                gathered(e + (rnd_no + 2))
                rest_at(g0 + G_EXP, G_MOE)
                rest_at(g0 + (G_EXP + 1), G_MOE + 1)

        nc.vector.memset(sel_t[:, :].bitcast(F32), 0.0).then_inc(null_ready, 1)
        nc.vector.memset(wslot[:, :], 0.0).then_inc(null_ready, 1)
        experts(0)
        dve.wait_ge(route_ready, 1)
        with dve.If(dve.value_load(cnt_i[0:1, 0:1], min_val=0, max_val=S) > P):
            experts(1)
        scale_out(1, last_hi, last_lo)
        def last_total(m, half):
            dve.wait_ge(last_full, 2 * m + half + 1)
            part = acc[:, m, half * W:(half + 1) * W]
            seq(nc.vector.tensor_tensor(part, part, ps[LAST_BANKS[2 * m + half]][:, :], ALU.add), 1)

        norm(1, last_total, par_b, 1, 1)
        ple(1, 0, pp1, 4)

    @block.tensor
    def _(pe):
        s0 = streams[0]

        def mm(o, a, b, start, stop):
            return nc.tensor.matmul(o, a, b, start=start, stop=stop)

        def mm3(o, ah, al, slot, c, start, stop):
            mm(o, ah, wh[:, slot, c], start, False)
            mm(o, ah, wl[:, slot, c], False, False)
            return mm(o, al, wh[:, slot, c], False, stop)

        nt = [0, 0]

        def turn(srcs, which=0):
            st = streams[which]
            n = nt[which]
            if n >= 2:
                pe.wait_ge(st["tp_lo"], n - 1)
            for c, src in enumerate(srcs):
                last = nc.tensor.transpose(ps[6 + n % 2][:, c * P:(c + 1) * P], src, ident[:, :])
            last.then_inc(st["tp"], 1)
            nt[which] += 1

        def turned(which=0):
            pe.wait_ge(streams[which]["tp_lo"], nt[which])

        def quarter(t, m, q):
            return [t[:, m, (4 * q + c) * P:(4 * q + c + 1) * P] for c in range(4)]

        def cols_granules(g, banks, st=s0, g_of=None, fresh=None, between=None):
            for half in range(2):
                if fresh is not None:
                    pe.wait_ge(st["tp_lo"], fresh + T * (half + 1))
                pe.wait_ge(st["lo"], g + half + 1)
                for c in range(4):
                    k = 4 * half + c
                    for m in range(T):
                        tok = slice(m * P, (m + 1) * P)
                        last = mm3(ps[banks[m]][:, :], hth[:, k, tok], htl[:, k, tok],
                                   ((g if g_of is None else g_of) + half) % SPL, c, k == 0, k == KD - 1)
                last.then_inc(st["used"], 1)
                if half == 0 and between is not None:
                    between()

        def cols_by_tile(g, banks, fresh, st=s0, offset=0, between=None):
            for m in range(T):
                tok = slice(m * P, (m + 1) * P)
                for half in range(2):
                    pe.wait_ge(st["tp_lo"], fresh + 2 * m + half + 1)
                    if m == 0:
                        pe.wait_ge(st["lo"], g + half + 1)
                    for c in range(4):
                        k = 4 * half + c
                        last = mm3(ps[banks[m]][:, :], hth[:, k, tok], htl[:, k, tok],
                                   (g + offset + half) % SPL, c, k == 0, k == KD - 1)
                    if m == T - 1:
                        last.then_inc(st["used"], 1)
                    if m == 0 and half == 0 and between is not None:
                        between()

        def rows_granule(g, ah, al, k0, first, final, banks=(0, 1, 2, 3)):
            pe.wait_ge(s0["lo"], g + 1)
            for kk in range(2):
                for m in range(T):
                    tok = slice(m * P, (m + 1) * P)
                    for half in range(2):
                        last = mm3(ps[banks[2 * m + half]][:, :], ah[:, k0 + kk, tok], al[:, k0 + kk, tok], g % SPL,
                                   2 * kk + half, first and kk == 0, final and kk == 1)
            last.then_inc(s0["used"], 1)

        def rows_last(g, ah, al, k0):
            pe.wait_ge(s0["lo"], g + 2)
            for m in range(T):
                tok = slice(m * P, (m + 1) * P)
                for half in range(2):
                    for kk in range(4):
                        last = mm3(ps[2 * m + half][:, :], ah[:, k0 + kk, tok], al[:, k0 + kk, tok],
                                   (g + kk // 2) % SPL, 2 * (kk % 2) + half, False, kk == 3)
                    if m < T - 1 or half == 0:
                        last.then_inc(bank_full, 1)
            last.then_inc(s0["used"], 2)

        pe.wait_ge(const_step, 2)
        for q in range(2):
            for m in range(T):
                pe.wait_ge(x_landed[q * T + m], 16)
                turn(quarter(h, m, q))

        def spatial(q):
            for m in range(T):
                if q >= 1:
                    pe.wait_ge(mixed, ((q - 1) * T + m + 1) * 2)
                for k in range(2):
                    grp = 2 * q + k
                    last = mm(ps[4 + m][:, k * GC:(k + 1) * GC], ws_t[:, grp, :], v[:, m, grp * GC:(grp + 1) * GC],
                              True, True)
                last.then_inc(sv_full, 1)

        def first_spatial():
            pe.wait_ge(v_normed, 2 * T)
            pe.wait_ge(ws_masked, 1)
            spatial(0)

        for i in range(N_GIN):
            if i >= 2:
                pe.wait_ge(gm_biased, T * (i - 1))
            cols_granules(2 * i, [i % 2 * 2, i % 2 * 2 + 1], fresh=0 if i == 0 else None,
                          between=first_spatial if i == N_GIN - 1 else None)
            if i == 0:
                pe.wait_ge(ws_landed, 16)
                for k in range(2):
                    for c in range(4):
                        last = nc.tensor.transpose(ps[4 + k][:, c * P:(c + 1) * P], ws_raw[:, 4 * k + c, :],
                                                   ident[:, :])
                    last.then_inc(ws_tp, 1)
        def u_turn(q):
            for m in range(T):
                pe.wait_ge(mixed, (q * T + m + 1) * 2)
                turn(quarter(u, m, q))

        def u_product(q):
            pe.wait_ge(s0["tp_lo"], n_u + T * (q + 1))
            if q == 3:
                rows_last(G_GOUT + 6, hth, htl, 4)
                return
            for k in range(2):
                rows_granule(G_GOUT + 2 * q + k, hth, htl, 4 * (q % 2) + 2 * k, q == 0 and k == 0, False)

        n_u = nt[0]
        pe.wait_ge(gm_biased, T * N_GIN)
        for q in range(4):
            if q < 3:
                spatial(q + 1)
            u_turn(q)
            if q >= 1:
                u_product(q - 1)
        u_product(3)

        n_h = [0]

        def turn_embedding(pn):
            for m in range(T):
                turn([pn[:, m, c * P:(c + 1) * P] for c in range(2)])

        def turn_half(q, which=0):
            for m in range(T):
                n_h[0] += 1
                pe.wait_ge(streams[which]["h"], n_h[0])
                turn(quarter(h, m, q), which)

        def turn_tile(m, which=0):
            for q in range(2):
                n_h[0] += 1
                pe.wait_ge(streams[which]["h"], n_h[0])
                turn(quarter(h, m, q), which)

        fresh = nt[0]
        turn_tile(0)

        g = G_FFN

        def down(gv, gs, n0):
            pe.wait_ge(s0["lo"], gv + 2)
            for i in range(2 * T):
                m, half = i // 2, i % 2
                if i >= 2:
                    pe.wait_ge(part_added, n0 + (i - 1))
                for kk in range(4):
                    tok = slice(m * P, (m + 1) * P)
                    last = mm3(ps[4 + i % 2][:, :], bth[:, kk, tok], btl[:, kk, tok], (gs + kk // 2) % SPL,
                               2 * (kk % 2) + half, kk == 0, kk == 3)
                if i < 2 * T - 1:
                    last.then_inc(part_full, 1)
                else:
                    last.then_inc(s0["used"], 2)

        cols_by_tile(g, [0, 1], fresh, between=lambda: turn_tile(1))
        cols_granules(g + 2, [2, 3])
        pe.wait_ge(pn_landed[0], 16)
        turn_embedding(pn0)
        n_tp = nt[0]
        with pe.Fori(1, NJ) as j:
            gj = pe.snap(g + 4 + (j - 1) * G_BLK)
            pe.wait_ge(silu_done, j * T)
            cols_granules(gj, [0, 1], g_of=g + 4)
            pe.wait_ge(s0["tp_lo"], j * T + (n_tp - T))
            for m in range(T):
                pe.wait_ge(hid_ready, (j - 1) * T + (m + 1))
                for c in range(4):
                    last = nc.tensor.transpose(ps[6 + m][:, c * P:(c + 1) * P], hb[:, m, c * P:(c + 1) * P],
                                               ident[:, :])
                last.then_inc(s0["tp"], 1)
            cols_granules(gj + 2, [2, 3], g_of=g + 6)
            pe.wait_ge(s0["tp_lo"], j * T + n_tp)
            down(gj + 4, g + 8, (j - 1) * (2 * T))
        nt[0] += (NJ - 1) * T
        assert nt[0] % 2 == 0
        pe.wait_ge(hid_ready, NJ * T)
        for m in range(T):
            turn([hb[:, m, c * P:(c + 1) * P] for c in range(4)])
        turned()
        for m in range(T):
            tok = slice(m * P, (m + 1) * P)
            for i in range(2):
                gd = g + G_EXP - 2 + i
                pe.wait_ge(s0["lo"], gd + 1)
                for half in range(2):
                    for kk in range(2):
                        last = mm3(ps[2 * m + half][:, :], bth[:, 2 * i + kk, tok], btl[:, 2 * i + kk, tok],
                                   gd % SPL, 2 * kk + half, i == 0 and kk == 0, i == 1 and kk == 1)
                    if i == 1 and (m < T - 1 or half == 0):
                        last.then_inc(part_full, 1)
        last.then_inc(s0["used"], 2)

        def ple(which, g0, fresh, between=None):
            st = streams[which]
            offset = (0, G_TAIL)[which]
            cols_by_tile(g0, [2, 3], fresh, st, offset, between)
            if which == 0:
                pe.wait_ge(proj_copied, 2 * T)
                cols_granules(g0 + 2, [0, 1], between=lambda: turn_half(0))
                return
            for m in range(T):
                tok = slice(m * P, (m + 1) * P)
                for k in range(KD):
                    if m == 0 and k % 4 == 0:
                        pe.wait_ge(st["lo"], g0 + 3 + k // 4)
                    last = mm3(ps[m][:, :], hth[:, k, tok], htl[:, k, tok], (offset + g0 + 2 + k // 4) % SPL,
                               k % 4, k == 0, k == KD - 1)
                if m == 0:
                    last.then_inc(last_gate, 1)
            last.then_inc(st["used"], 2)

        fresh = nt[0]
        turn_tile(0)
        pe.wait_ge(part_added, (NJ - 1) * 2 * T + 2)
        rows_granule(G_PLE, pth, ptl, 0, True, True, banks=(4, 5, 0, 1))
        turn_tile(1)
        ple(0, G_PLE + 1, fresh)
        n_fin = nt[0] - T

        def small(bank, n, wsh, wsl, fresh):
            for m in range(T):
                tok = slice(m * P, (m + 1) * P)
                o = ps[bank][0:n, tok]
                for k in range(KD):
                    if fresh is not None and k % 4 == 0:
                        pe.wait_ge(s0["tp_lo"], fresh + 2 * m + k // 4 + 1)
                    mm(o, wsh[:, k, :], hth[:, k, tok], k == 0, False)
                    mm(o, wsl[:, k, :], hth[:, k, tok], False, False)
                    last = mm(o, wsh[:, k, :], htl[:, k, tok], False, k == KD - 1)
            last.then_inc(small_full, 1)

        def small_turn(bank, n, times):
            pe.wait_ge(small_copied, times)
            for m in range(T):
                last = nc.tensor.transpose(ps[bank][:, m * n:(m + 1) * n], small_t[0:n, m * P:(m + 1) * P],
                                           ident[0:n, 0:n])
            return last

        def prefix(bank, n, src, upto, every):
            mm(ps[bank][:, 0:n], upto[:, :], src[:, 0, :], True, True)
            mm(ps[bank][:, n:2 * n], upto[:, :], src[:, 1, :], True, False)
            return mm(ps[bank][:, n:2 * n], every[:, :], src[:, 0, :], False, True)

        for i in range(N_FIN):
            if i >= 2:
                pe.wait_ge(fin_copied, T * (i - 1))
            cols_granules(G_FIN + 2 * i, [(i + 1) % 2 * 2, (i + 1) % 2 * 2 + 1], fresh=n_fin if i == 0 else None,
                          between={0: lambda: turn_half(1),
                                   1: lambda: small_turn(4, H, 1).then_inc(f_full, 1)}.get(i))
            if i == 0:
                pe.wait_ge(small_split, 4)
                small(5, H, wfh, wfl, None)
            if i == 4:
                pe.wait_ge(f_logf, 1)
                pe.wait_ge(const_ready, 1)
                prefix(5, H, z_f, upper, ones).then_inc(c_full, 1)
        pe.wait_ge(fin_copied, T * N_FIN)
        pe.wait_ge(qk_ready, 4 * T)
        for s in range(H + 3):
            if s < H:
                b = s % 2
                if s >= 2:
                    pe.wait_ge(at_qkc, s - 1)
                for i, t in enumerate((q_nat, k_nat)):
                    for m in range(T):
                        last = nc.tensor.transpose(ps[6 + b][0:FA, i * S + m * P:i * S + (m + 1) * P],
                                                   t[:, m, s, :], ident[:, :])
                last.then_inc(at_qk, 1)
            if 0 <= s - 1 < H:
                hd = s - 1
                b = hd % 2
                pe.wait_ge(at_qkc, hd + 1)
                if hd >= 2:
                    pe.wait_ge(at_exp, T * (hd - 1))
                mm(ps[b][:, 0:P], qk_t[0:FA, b, 0:P], qk_t[0:FA, b, S:S + P], True, False)
                mm(ps[b][:, 0:P], ident_b[:, :], mask[:, :], False, True)
                mm(ps[b][:, P:3 * P], qk_t[0:FA, b, P:2 * P], qk_t[0:FA, b, S:2 * S], True, False)
                mm(ps[b][:, 2 * P:3 * P], ident_b[:, :], mask[:, :], False, True).then_inc(at_log, 1)
            if 0 <= s - 2 < H:
                hd = s - 2
                b = hd % 2
                pe.wait_ge(at_exp, T * (hd + 1))
                if hd >= 2:
                    pe.wait_ge(at_ptc, hd - 1)
                for c in range(3):
                    last = nc.tensor.transpose(ps[2 + b][:, c * P:(c + 1) * P], prob[:, b, c * P:(c + 1) * P],
                                               ident[:, :])
                last.then_inc(at_pt, 1)
            if s >= 3:
                hd = s - 3
                b = hd % 2
                pe.wait_ge(at_ptc, hd + 1)
                if hd >= 2:
                    pe.wait_ge(at_on, hd - 1)
                val = slice(hd * DH, (hd + 1) * DH)
                mm(ps[4 + b][:, 0:DH], prob_t[:, b, 0:P], v_nat[:, 0, val], True, True)
                mm(ps[4 + b][:, DH:2 * DH], prob_t[:, b, P:2 * P], v_nat[:, 0, val], True, False)
                mm(ps[4 + b][:, DH:2 * DH], prob_t[:, b, 2 * P:3 * P], v_nat[:, 1, val], False, True)\
                    .then_inc(at_o, 1)
        pe.wait_ge(at_on, H)
        for q in range(2):
            for m in range(T):
                turn(quarter(o_nat, m, q))
        pe.wait_ge(s0["tp_lo"], nt[0] - T)
        rows_granule(G_FOUT, hth, htl, 0, True, False)
        pe.wait_ge(pn_landed[1], 16)
        turn_embedding(pn1)
        rows_granule(G_FOUT + 1, hth, htl, 2, False, False)
        turned()
        rows_last(G_FOUT + 2, hth, htl, 4)
        fresh = nt[0]
        turn_tile(0)
        pe.wait_ge(sum_read, 2 * T + 2)
        rows_granule(G_PROJ, pth1, ptl1, 0, True, True, banks=(4, 5, 0, 1))
        turn_tile(1)
        small(2, NE, wrh, wrl, fresh)
        small_turn(3, NE, 2).then_inc(lg_full, 1)
        pe.wait_ge(mem_ready, 1)
        prefix(2, NE, member_b, upper_b, ones_b)
        mm(ps[2][:, T * NE:(T + 1) * NE], ones_b[:, :], member_b[:, 0, :], True, False)
        mm(ps[2][:, T * NE:(T + 1) * NE], ones_b[:, :], member_b[:, 1, :], False, True).then_inc(rank_full, 1)
        pe.wait_ge(xl_ready, T)

        def clear_out(stop):
            for half in range(2):
                for c in range(4):
                    last = mm(ps[2 + half][:, c * P:(c + 1) * P], zeros[:, :], zeros[:, :], c == 0, stop and c == 3)
            return last

        def gather(n):
            pe.wait_ge(sel_ready, n * (T + 1) - 1)
            for q in range(2):
                for c in range(4):
                    k = slice((4 * q + c) * P, (4 * q + c + 1) * P)
                    o = ps[4 + q][:, c * P:(c + 1) * P]
                    for m in range(T):
                        mm(o, xh[:, m, k], sel[:, m, :], m == 0, False)
                        last = mm(o, xl[:, m, k], sel[:, m, :], False, m == T - 1)
                last.then_inc(gx_full, 1)

        def scatter_part(bank, m, half):
            part = slice(half * W, (half + 1) * W)
            tok = slice(m * P, (m + 1) * P)
            mm(ps[bank][:, :], sel_t[:, tok], ysh[:, part], True, False)
            return mm(ps[bank][:, :], sel_t[:, tok], ysl[:, part], False, True)

        def scatter(n):
            for i in range(2 * T):
                half, m = i // 2, i % 2
                if m == 0:
                    pe.wait_ge(ys_lo, n * 2 - (1 - half))
                scatter_part(4 + i, m, half).then_inc(sc_full, 1)

        def experts(rnd_no):
            if rnd_no:
                gather(1 + rnd_no * (NE + 1))
            with pe.Fori(rnd_no * NE, (rnd_no + 1) * NE) as e:
                g0 = pe.snap(G_MOE + e * G_EXP)
                e1 = pe.snap(e + 1)
                en = pe.snap(e + (rnd_no + 1))

                def gate_or_up(gv, gs, bank, gathered=None):
                    for half in range(2):
                        if gathered is not None:
                            pe.wait_ge(gx_lo, gathered - (1 - half))
                        pe.wait_ge(s0["lo"], gv + (half + 1))
                        for c in range(4):
                            k = 4 * half + c
                            last = mm3(ps[bank][:, :], xeh[:, k, :], xel[:, k, :], (gs + half) % SPL, c, k == 0,
                                       k == KD - 1)
                        last.then_inc(s0["used"], 1)

                def hidden_turn(n):
                    pe.wait_ge(e_hid, n)
                    for c in range(4):
                        last = nc.tensor.transpose(ps[6][:, c * P:(c + 1) * P], hb[:, 0, c * P:(c + 1) * P],
                                                   ident[:, :])
                    last.then_inc(e_tp, 1)

                def expert_down(n, gv, gs, final):
                    pe.wait_ge(e_lo, n)
                    for i in range(2):
                        pe.wait_ge(s0["lo"], gv + (i + 1))
                        for kk in range(2):
                            for half in range(2):
                                last = mm3(ps[2 + half][:, :], bth[:, 2 * i + kk, 0:P], btl[:, 2 * i + kk, 0:P],
                                           (gs + i) % SPL, 2 * kk + half, False, final and i == 1 and kk == 1)
                        last.then_inc(s0["used"], 1)

                gate_or_up(g0, G_MOE, 0, en * 2)
                scatter(e1)
                gate_or_up(g0 + 2, G_MOE + 2, 1)
                pe.wait_ge(sc_added, e1 * (2 * T))
                pe.wait_ge(sel_ready, en * (T + 1))
                for m in range(T):
                    nc.tensor.transpose(ps[7][:, m * P:(m + 1) * P], sel[:, m, :].bitcast(F32), ident[:, :])
                for m in range(T):
                    last = mm(ps[7][:, S:S + 1], sel[:, m, :].bitcast(F32), wcur[:, m:m + 1], m == 0, m == T - 1)
                last.then_inc(st_full, 1)
                clear_out(False)
                with pe.Fori(1, NJ) as j:
                    gj = pe.snap(g0 + j * G_BLK)
                    ej = pe.snap(e * NJ + j)
                    pe.wait_ge(e_silu, ej)
                    gate_or_up(gj - 2, G_MOE - 2, 0)
                    hidden_turn(ej)
                    gate_or_up(gj, G_MOE, 1)
                    expert_down(ej, gj + 2, G_MOE + 2, False)
                hidden_turn(e1 * NJ)
                gather(e + (rnd_no + 2))
                expert_down(e1 * NJ, g0 + (G_EXP - 2), G_MOE - 2, True)

        pe.wait_ge(proj_copied, 4 * T)
        gather(1)
        clear_out(True).then_inc(null_full, 1)
        pe.wait_ge(null_ready, 2)
        experts(0)
        pe.wait_ge(route_ready, 1)
        with pe.If(pe.value_load(cnt_i[0:1, 0:1], min_val=0, max_val=S) > P):
            experts(1)
        for m in range(T):
            for half in range(2):
                if m == 0:
                    pe.wait_ge(last_lo, half + 1)
                scatter_part(LAST_BANKS[2 * m + half], m, half).then_inc(last_full, 1)
        n_h[0] = 0
        turn_tile(0, 1)
        ple(1, 0, 0, lambda: turn_tile(1, 1))

    whole.close()


_INS = ["x", "p", "ln_g", "ln_b", "gm_w_in", "gm_b_in", "gm_ln_g", "gm_ln_b", "gm_w_s", "gm_b_s", "gm_w_out",
        "fox_w_in", "fox_b_f", "fox_w_out", "ffn_w_gate", "ffn_w_up", "ffn_w_down",
        "moe_w_router", "moe_w_gate", "moe_w_up", "moe_w_down", "ple_w_gate", "ple_b_gate", "ple_w_proj"]


def kernel(**inputs):
    import numpy as _np
    import concourse.bacc as _bacc
    from concourse import mybir as _mybir
    from concourse.bass_utils import run_bass_kernel_spmd as _run

    nc = _bacc.Bacc("TRN2", target_bir_lowering=False, num_devices=1)
    arrays, args = {}, []
    for name in _INS:
        a = _np.ascontiguousarray(inputs[name])
        arrays[f"in_{name}_dram"] = a
        args.append(nc.dram_tensor(f"in_{name}_dram", a.shape, _mybir.dt.from_np(a.dtype), kind="ExternalInput").ap())
    shape = _np.shape(inputs["x"])
    args.append(nc.dram_tensor("out_dram", shape, _mybir.dt.float32, kind="ExternalOutput").ap())
    build_trunk(nc, *args)
    r = _run(nc, [arrays], core_ids=[0])
    return r.results[0]["out_dram"]
```
